# Optimizing a Trainium2 kernel written in Bass

```python
import math
import jax
import jax.numpy as jnp
from jax import lax
import numpy as np
import jax, jax.numpy as jnp

D_MODEL = 1024
BATCH = 1
SEQ = 256
DEPTH = 2

MIX_W = D_MODEL // 4
N_BRANCH = 4
CHUNK = 64
EPS = 1e-6
ROPE_BASE = 10000.0
CONV_K = 4

RET_HEADS = 4
RET_DK = MIX_W // RET_HEADS
RET_DV = MIX_W // RET_HEADS

SSD_HEADS = 4
SSD_P = MIX_W // SSD_HEADS
SSD_N = 128
SSD_GROUPS = 2
SSD_CONV_CH = MIX_W + 2 * SSD_GROUPS * SSD_N

GLA_HEADS = 4
GLA_DK = MIX_W // (2 * GLA_HEADS)
GLA_DV = MIX_W // GLA_HEADS
GLA_RANK = 16
GLA_TAU = 16.0

ML_HEADS = 4
ML_DK = MIX_W // ML_HEADS
ML_DV = MIX_W // ML_HEADS

D_FF = 2816
N_EXPERTS = 8
TOP_K = 2
EXPERT_FF = 2816

IN_SIZES = (
    MIX_W, MIX_W, MIX_W, MIX_W,
    MIX_W, SSD_CONV_CH, SSD_HEADS,
    GLA_HEADS * GLA_DK, GLA_HEADS * GLA_DK, MIX_W, MIX_W, GLA_RANK,
    2 * MIX_W, MIX_W, MIX_W, ML_HEADS, ML_HEADS,
    N_BRANCH * D_MODEL,
)
IN_COLS = sum(IN_SIZES)


def rmsnorm(x, g):
    xf = x.astype(jnp.float32)
    y = xf * lax.rsqrt(jnp.mean(xf * xf, axis=-1, keepdims=True) + EPS)
    return (y * g.astype(jnp.float32)).astype(x.dtype)

def head_rmsnorm(t, g):
    nh, d = t.shape[-2], t.shape[-1]
    return rmsnorm(t, g.reshape(nh, d))

def rotary(t, pos):
    half = t.shape[-1] // 2
    inv = ROPE_BASE ** (-jnp.arange(half, dtype=jnp.float32) / half)
    ang = pos.astype(jnp.float32)[:, None] * inv[None, :]
    cos = jnp.cos(ang)[None, :, None, :]
    sin = jnp.sin(ang)[None, :, None, :]
    t1 = t[..., :half].astype(jnp.float32)
    t2 = t[..., half:].astype(jnp.float32)
    return jnp.concatenate([t1 * cos - t2 * sin, t1 * sin + t2 * cos], axis=-1)

def causal_dwconv(u, w, b):
    ch = u.shape[-1]
    y = lax.conv_general_dilated(u, w[:, None, :].astype(u.dtype), window_strides=(1,),
                                 padding=[(CONV_K - 1, 0)],
                                 dimension_numbers=('NWC', 'WIO', 'NWC'),
                                 feature_group_count=ch)
    return y + b

def _chunk(t):
    t = t.astype(jnp.float32)
    bsz, seq, nh = t.shape[:3]
    t = t.reshape((bsz, seq // CHUNK, CHUNK, nh) + t.shape[3:])
    return jnp.moveaxis(t, (1, 3), (0, 2))

def _unchunk(t):
    t = jnp.moveaxis(t, (0, 2), (1, 3))
    return t.reshape((t.shape[0], t.shape[1] * t.shape[2]) + t.shape[3:])

def _tri():
    return jnp.tril(jnp.ones((CHUNK, CHUNK), dtype=bool))

def retention_scan(q, k, v, log_gamma):
    bsz, _, nh, dk = q.shape
    dv = v.shape[-1]
    idx = jnp.arange(CHUNK, dtype=jnp.float32)
    rel = idx[:, None] - idx[None, :]
    tri = rel >= 0
    decay = jnp.where(tri[None], jnp.exp(jnp.where(tri, rel, 0.0)[None] * log_gamma[:, None, None]), 0.0)
    q_decay = jnp.exp((idx + 1.0)[None, :] * log_gamma[:, None])
    k_decay = jnp.exp((CHUNK - 1.0 - idx)[None, :] * log_gamma[:, None])
    chunk_decay = jnp.exp(CHUNK * log_gamma)

    def step(state, inp):
        qc, kc, vc = inp
        s = jnp.einsum('bhid,bhjd->bhij', qc, kc) * decay
        o = (jnp.einsum('bhij,bhjv->bhiv', s, vc)
             + jnp.einsum('bhid,bhdv->bhiv', qc, state) * q_decay[:, :, None])
        state = (state * chunk_decay[:, None, None]
                 + jnp.einsum('bhjd,bhjv->bhdv', kc * k_decay[:, :, None], vc))
        return state, o

    s0 = jnp.zeros((bsz, nh, dk, dv), jnp.float32)
    _, o = lax.scan(step, s0, (_chunk(q), _chunk(k), _chunk(v)))
    return _unchunk(o)

def ssd_scan(x, dt, bmat, cmat, a):
    bsz, _, nh, p = x.shape
    n = bmat.shape[-1]
    tri = _tri()

    def step(state, inp):
        xc, dtc, bc, cc = inp
        acs = jnp.cumsum(dtc * a[None, :, None], axis=-1)
        seg = jnp.exp(jnp.where(tri, acs[..., :, None] - acs[..., None, :], -jnp.inf))
        scores = jnp.einsum('bhin,bhjn->bhij', cc, bc) * seg
        xdt = xc * dtc[..., None]
        y = (jnp.einsum('bhij,bhjp->bhip', scores, xdt)
             + jnp.einsum('bhin,bhpn->bhip', cc, state) * jnp.exp(acs)[..., None])
        w_end = jnp.exp(acs[..., -1:] - acs)
        state = (state * jnp.exp(acs[..., -1])[..., None, None]
                 + jnp.einsum('bhjp,bhjn->bhpn', xdt * w_end[..., None], bc))
        return state, y

    s0 = jnp.zeros((bsz, nh, p, n), jnp.float32)
    _, y = lax.scan(step, s0, (_chunk(x), _chunk(dt), _chunk(bmat), _chunk(cmat)))
    return _unchunk(y)

def gla_scan(q, k, v, log_alpha):
    bsz, _, nh, dk = q.shape
    dv = v.shape[-1]
    tri = _tri()

    def step(state, inp):
        qc, kc, vc, gc = inp
        g = jnp.cumsum(gc, axis=2)
        seg = jnp.exp(jnp.where(tri[:, :, None], g[:, :, :, None, :] - g[:, :, None, :, :], -jnp.inf))
        att = jnp.sum(qc[:, :, :, None, :] * kc[:, :, None, :, :] * seg, axis=-1)
        o = (jnp.einsum('bhij,bhjv->bhiv', att, vc)
             + jnp.einsum('bhid,bhdv->bhiv', qc * jnp.exp(g), state))
        g_end = g[:, :, -1:, :]
        state = (state * jnp.exp(g_end[:, :, 0, :])[..., None]
                 + jnp.einsum('bhjd,bhjv->bhdv', kc * jnp.exp(g_end - g), vc))
        return state, o

    s0 = jnp.zeros((bsz, nh, dk, dv), jnp.float32)
    _, o = lax.scan(step, s0, (_chunk(q), _chunk(k), _chunk(v), _chunk(log_alpha)))
    return _unchunk(o)

def mlstm_scan(q, k, v, i_pre, log_f):
    bsz, _, nh, dk = q.shape
    dv = v.shape[-1]
    tri = _tri()

    def step(carry, inp):
        c_st, n_st, m = carry
        qc, kc, vc, ic, fc = inp
        b = jnp.cumsum(fc, axis=-1)
        dlog = jnp.where(tri, b[..., :, None] - b[..., None, :] + ic[..., None, :], -jnp.inf)
        inter = b + m[..., None]
        m_t = jnp.maximum(inter, jnp.max(dlog, axis=-1))
        s = jnp.einsum('bhid,bhjd->bhij', qc, kc) * jnp.exp(dlog - m_t[..., None])
        inter_w = jnp.exp(inter - m_t)
        num = (jnp.einsum('bhij,bhjv->bhiv', s, vc)
               + jnp.einsum('bhid,bhdv->bhiv', qc, c_st) * inter_w[..., None])
        den = jnp.sum(s, axis=-1) + jnp.einsum('bhid,bhd->bhi', qc, n_st) * inter_w
        h = num / jnp.maximum(jnp.abs(den), jnp.exp(-m_t))[..., None]
        b_end = b[..., -1]
        w_log = b_end[..., None] - b + ic
        m_new = jnp.maximum(b_end + m, jnp.max(w_log, axis=-1))
        w = jnp.exp(w_log - m_new[..., None])
        carry_decay = jnp.exp(b_end + m - m_new)
        kw = kc * w[..., None]
        c_st = c_st * carry_decay[..., None, None] + jnp.einsum('bhjd,bhjv->bhdv', kw, vc)
        n_st = n_st * carry_decay[..., None] + jnp.sum(kw, axis=2)
        return (c_st, n_st, m_new), h

    init = (jnp.zeros((bsz, nh, dk, dv), jnp.float32),
            jnp.zeros((bsz, nh, dk), jnp.float32),
            jnp.zeros((bsz, nh), jnp.float32))
    _, h = lax.scan(step, init, (_chunk(q), _chunk(k), _chunk(v), _chunk(i_pre), _chunk(log_f)))
    return _unchunk(h)

def _split_cols(u):
    outs, start = [], 0
    for width in IN_SIZES:
        outs.append(u[..., start:start + width])
        start += width
    return outs

def token_mixers(h, pos, w_in, ret_norm_g, ssd_conv_w, ssd_conv_b, ssd_dt_bias, ssd_a_log, ssd_d,
                 ssd_norm_g, gla_w_alpha, gla_b_alpha, gla_norm_g, ml_conv_w, ml_conv_b, ml_b_i,
                 ml_b_f, ml_norm_g, w_branch, w_out):
    bsz, seq, _ = h.shape
    u = h @ w_in
    (rq, rk, rv, rg, sz, sxbc, sdt, gq, gk, gv, gr, ga,
     mqk, mv, mo, mi, mf, mgate) = _split_cols(u)

    def heads(t, nh):
        return t.reshape(bsz, seq, nh, -1)

    log_gamma = jnp.log1p(-jnp.exp2(-5.0 - jnp.arange(RET_HEADS, dtype=jnp.float32)))
    q = rotary(heads(rq, RET_HEADS), pos)
    k = rotary(heads(rk, RET_HEADS), pos) * (RET_DK ** -0.5)
    o = retention_scan(q, k, heads(rv, RET_HEADS), log_gamma)
    y_ret = (head_rmsnorm(o, ret_norm_g).reshape(bsz, seq, MIX_W) * jax.nn.silu(rg)).astype(h.dtype)

    xbc = jax.nn.silu(causal_dwconv(sxbc, ssd_conv_w, ssd_conv_b))
    sx = xbc[..., :MIX_W]
    sb = xbc[..., MIX_W:MIX_W + SSD_GROUPS * SSD_N].reshape(bsz, seq, SSD_GROUPS, SSD_N)
    sc = xbc[..., MIX_W + SSD_GROUPS * SSD_N:].reshape(bsz, seq, SSD_GROUPS, SSD_N)
    rep = SSD_HEADS // SSD_GROUPS
    bh = jnp.repeat(sb, rep, axis=2)
    ch = jnp.repeat(sc, rep, axis=2)
    dt = jax.nn.softplus(sdt.astype(jnp.float32) + ssd_dt_bias.astype(jnp.float32))
    a = -jnp.exp(ssd_a_log.astype(jnp.float32))
    xs = heads(sx, SSD_HEADS).astype(jnp.float32)
    y = ssd_scan(xs, dt, bh, ch, a) + ssd_d.astype(jnp.float32)[:, None] * xs
    y_ssd = rmsnorm(y.reshape(bsz, seq, MIX_W) * jax.nn.silu(sz), ssd_norm_g).astype(h.dtype)

    alpha_pre = (ga @ gla_w_alpha + gla_b_alpha).astype(jnp.float32)
    log_alpha = heads(jax.nn.log_sigmoid(alpha_pre) / GLA_TAU, GLA_HEADS)
    q = heads(gq, GLA_HEADS) * (GLA_DK ** -0.5)
    o = gla_scan(q, heads(gk, GLA_HEADS), heads(gv, GLA_HEADS), log_alpha)
    y_gla = (head_rmsnorm(o, gla_norm_g).reshape(bsz, seq, MIX_W) * jax.nn.silu(gr)).astype(h.dtype)

    qk = jax.nn.silu(causal_dwconv(mqk, ml_conv_w, ml_conv_b))
    q = heads(qk[..., :MIX_W], ML_HEADS)
    k = heads(qk[..., MIX_W:], ML_HEADS) * (ML_DK ** -0.5)
    i_pre = mi.astype(jnp.float32) + ml_b_i.astype(jnp.float32)
    log_f = jax.nn.log_sigmoid(mf.astype(jnp.float32) + ml_b_f.astype(jnp.float32))
    o = mlstm_scan(q, k, heads(mv, ML_HEADS), i_pre, log_f)
    y_ml = (head_rmsnorm(o, ml_norm_g).reshape(bsz, seq, MIX_W) * jax.nn.sigmoid(mo)).astype(h.dtype)

    ybr = jnp.stack([y_ret, y_ssd, y_gla, y_ml], axis=2)
    gates = jax.nn.sigmoid(mgate.reshape(bsz, seq, N_BRANCH, D_MODEL))
    merged = jnp.sum(gates * jnp.einsum('bsnv,nvd->bsnd', ybr, w_branch), axis=2)
    return merged @ w_out

def swiglu(h, w1, w3, w2):
    return (jax.nn.silu(h @ w1) * (h @ w3)) @ w2

def moe_ffn(h, router_w, w1, w3, w2):
    logits = (h @ router_w).astype(jnp.float32)
    top_vals, top_idx = lax.top_k(logits, TOP_K)
    top_w = jax.nn.softmax(top_vals, axis=-1)
    gate = jnp.sum(jax.nn.one_hot(top_idx, N_EXPERTS, dtype=jnp.float32) * top_w[..., None], axis=-2)
    out = jnp.zeros_like(h)
    for e in range(N_EXPERTS):
        out = out + gate[..., e:e + 1].astype(h.dtype) * swiglu(h, w1[e], w3[e], w2[e])
    return out

def first_inputs(seed: int = 0) -> dict:
    key = jax.random.key(seed)
    ks = jax.random.split(key, 40)
    f32 = jnp.float32

    def nrm(i, shape, scale):
        return scale * jax.random.normal(ks[i], shape, f32)

    def gain(i, shape):
        return 1.0 + nrm(i, shape, 0.02)

    nl = DEPTH
    nd = (DEPTH + 1) // 2
    nm = DEPTH // 2
    res = (2.0 * DEPTH) ** -0.5
    dt = jnp.exp(jax.random.uniform(ks[8], (nl, SSD_HEADS), f32, math.log(1e-3), math.log(1e-1)))
    return {
        'x': nrm(0, (BATCH, SEQ, D_MODEL), 1.0),
        'mix_norm_g': gain(1, (nl, D_MODEL)),
        'w_in': nrm(2, (nl, D_MODEL, IN_COLS), D_MODEL ** -0.5),
        'ret_norm_g': gain(3, (nl, MIX_W)),
        'ssd_conv_w': nrm(4, (nl, CONV_K, SSD_CONV_CH), CONV_K ** -0.5),
        'ssd_conv_b': nrm(5, (nl, SSD_CONV_CH), 0.02),
        'ssd_dt_bias': dt + jnp.log(-jnp.expm1(-dt)),
        'ssd_a_log': jnp.log(jax.random.uniform(ks[9], (nl, SSD_HEADS), f32, 1.0, 16.0)),
        'ssd_d': 1.0 + nrm(10, (nl, SSD_HEADS), 0.1),
        'ssd_norm_g': gain(11, (nl, MIX_W)),
        'gla_w_alpha': nrm(12, (nl, GLA_RANK, GLA_HEADS * GLA_DK), GLA_RANK ** -0.5),
        'gla_b_alpha': nrm(13, (nl, GLA_HEADS * GLA_DK), 0.1),
        'gla_norm_g': gain(14, (nl, MIX_W)),
        'ml_conv_w': nrm(15, (nl, CONV_K, 2 * MIX_W), CONV_K ** -0.5),
        'ml_conv_b': nrm(16, (nl, 2 * MIX_W), 0.02),
        'ml_b_i': nrm(17, (nl, ML_HEADS), 0.1),
        'ml_b_f': jnp.linspace(3.0, 6.0, ML_HEADS, dtype=f32)[None, :] + nrm(18, (nl, ML_HEADS), 0.1),
        'ml_norm_g': gain(19, (nl, MIX_W)),
        'w_branch': nrm(20, (nl, N_BRANCH, MIX_W, D_MODEL), MIX_W ** -0.5),
        'w_out': nrm(21, (nl, D_MODEL, D_MODEL), res * D_MODEL ** -0.5),
        'ffn_norm_g': gain(22, (nl, D_MODEL)),
        'ffn_w1': nrm(23, (nd, D_MODEL, D_FF), D_MODEL ** -0.5),
        'ffn_w3': nrm(24, (nd, D_MODEL, D_FF), D_MODEL ** -0.5),
        'ffn_w2': nrm(25, (nd, D_FF, D_MODEL), res * D_FF ** -0.5),
        'router_w': nrm(26, (nm, D_MODEL, N_EXPERTS), D_MODEL ** -0.5),
        'moe_w1': nrm(27, (nm, N_EXPERTS, D_MODEL, EXPERT_FF), D_MODEL ** -0.5),
        'moe_w3': nrm(28, (nm, N_EXPERTS, D_MODEL, EXPERT_FF), D_MODEL ** -0.5),
        'moe_w2': nrm(29, (nm, N_EXPERTS, EXPERT_FF, D_MODEL), res * EXPERT_FF ** -0.5),
        'final_norm_g': gain(30, (D_MODEL,)),
    }

def first_block(x, mix_norm_g, w_in, ret_norm_g, ssd_conv_w, ssd_conv_b, ssd_dt_bias, ssd_a_log, ssd_d,
              ssd_norm_g, gla_w_alpha, gla_b_alpha, gla_norm_g, ml_conv_w, ml_conv_b, ml_b_i, ml_b_f,
              ml_norm_g, w_branch, w_out, ffn_norm_g, ffn_w1, ffn_w3, ffn_w2, router_w, moe_w1, moe_w3,
              moe_w2, final_norm_g):
    pos = jnp.arange(x.shape[1], dtype=jnp.int32)
    for l in range(DEPTH):
        h = rmsnorm(x, mix_norm_g[l])
        x = x + token_mixers(h, pos, w_in[l], ret_norm_g[l], ssd_conv_w[l], ssd_conv_b[l], ssd_dt_bias[l],
                             ssd_a_log[l], ssd_d[l], ssd_norm_g[l], gla_w_alpha[l], gla_b_alpha[l],
                             gla_norm_g[l], ml_conv_w[l], ml_conv_b[l], ml_b_i[l], ml_b_f[l], ml_norm_g[l],
                             w_branch[l], w_out[l]).astype(x.dtype)
        h = rmsnorm(x, ffn_norm_g[l])
        if l % 2 == 0:
            x = x + swiglu(h, ffn_w1[l // 2], ffn_w3[l // 2], ffn_w2[l // 2]).astype(x.dtype)
        else:
            x = x + moe_ffn(h, router_w[l // 2], moe_w1[l // 2], moe_w3[l // 2], moe_w2[l // 2]).astype(x.dtype)
    return rmsnorm(x, final_norm_g)


MIX_WIDTH = D_MODEL
ATTN_WIDTH = MIX_WIDTH // 2
POOL_WIDTH = MIX_WIDTH - ATTN_WIDTH
HEAD_DIM = 64
N_HEADS = ATTN_WIDTH // HEAD_DIM
N_KV_HEADS = 2
GROUP = N_HEADS // N_KV_HEADS
KV_WIDTH = N_KV_HEADS * HEAD_DIM
WINDOW = 128
BLOCK = 128
ROT_DIM = HEAD_DIM // 4
ROPE_THETA = 500000.0
POOL_WINDOWS = (2, 4, 8, 16)
N_POOL_GROUPS = len(POOL_WINDOWS)
POOL_GROUP_WIDTH = POOL_WIDTH // N_POOL_GROUPS
IN_WIDTH = ATTN_WIDTH + 2 * KV_WIDTH + POOL_WIDTH
D_FF_2 = ((int(np.ceil(8 * D_MODEL / 3)) + 255) // 256) * 256
N_MOD = 6
NEG_INF = -1e30


def rms_norm(x, g):
    xf = x.astype(jnp.float32)
    y = xf * lax.rsqrt(jnp.mean(xf * xf, axis=-1, keepdims=True) + EPS)
    return (y * g.astype(jnp.float32)).astype(x.dtype)

def partial_rotary(t, positions):
    inv_freq = ROPE_THETA ** (-jnp.arange(0, ROT_DIM, 2, dtype=jnp.float32) / ROT_DIM)
    ang = positions.astype(jnp.float32)[:, :, None] * inv_freq
    cos = jnp.cos(ang)[:, :, None, :]
    sin = jnp.sin(ang)[:, :, None, :]
    tf = t.astype(jnp.float32)
    half = ROT_DIM // 2
    t1, t2, rest = tf[..., :half], tf[..., half:ROT_DIM], tf[..., ROT_DIM:]
    rot = jnp.concatenate([t1 * cos - t2 * sin, t2 * cos + t1 * sin, rest], axis=-1)
    return rot.astype(t.dtype)

def sliding_window_attention_with_sinks(q, k, v, sinks):
    B, S = q.shape[0], q.shape[1]
    nb = S // BLOCK
    qb = q.reshape(B, nb, BLOCK, N_KV_HEADS, GROUP, HEAD_DIM)
    kb = k.reshape(B, nb, BLOCK, N_KV_HEADS, HEAD_DIM)
    vb = v.reshape(B, nb, BLOCK, N_KV_HEADS, HEAD_DIM)
    pad = ((0, 0), (1, 0), (0, 0), (0, 0), (0, 0))
    k_cat = jnp.concatenate([jnp.pad(kb, pad)[:, :-1], kb], axis=2)
    v_cat = jnp.concatenate([jnp.pad(vb, pad)[:, :-1], vb], axis=2)
    scores = jnp.einsum("bnqkgd,bnskd->bnkgqs", qb, k_cat).astype(jnp.float32)
    scores = scores * (HEAD_DIM ** -0.5)
    qi = jnp.arange(BLOCK)[:, None]
    kj = jnp.arange(2 * BLOCK)[None, :]
    diff = qi + BLOCK - kj
    blk = jnp.arange(nb)[:, None, None]
    key_abs = blk * BLOCK + kj[None] - BLOCK
    valid = (diff[None] >= 0) & (diff[None] < WINDOW) & (key_abs >= 0)
    scores = jnp.where(valid[None, :, None, None], scores, NEG_INF)
    sink = jnp.broadcast_to(
        sinks.astype(jnp.float32).reshape(1, 1, N_KV_HEADS, GROUP, 1, 1),
        scores.shape[:-1] + (1,))
    probs = jax.nn.softmax(jnp.concatenate([scores, sink], axis=-1), axis=-1)[..., :-1]
    out = jnp.einsum("bnkgqs,bnskd->bnqkgd", probs.astype(v.dtype), v_cat)
    return out.reshape(B, S, N_HEADS * HEAD_DIM)

def causal_pool_mixer(u, pool_w, pool_scale):
    S = u.shape[1]
    t = jnp.arange(S, dtype=jnp.float32)[None, :, None]
    outs = []
    for gi, w in enumerate(POOL_WINDOWS):
        ug = u[..., gi * POOL_GROUP_WIDTH:(gi + 1) * POOL_GROUP_WIDTH].astype(jnp.float32)
        cs = jnp.pad(jnp.cumsum(ug, axis=1), ((0, 0), (1, 0), (0, 0)))
        upper = cs[:, 1:]
        lower = jnp.pad(cs, ((0, 0), (w - 1, 0), (0, 0)))[:, :S]
        count = jnp.minimum(t + 1.0, float(w))
        pooled = (upper - lower) / count - ug
        outs.append(jnp.einsum("bsc,cd->bsd", pooled.astype(u.dtype), pool_w[gi]))
    return jnp.concatenate(outs, axis=-1) * pool_scale

def second_inputs(seed: int = 0) -> dict:
    key = jax.random.key(seed)
    ks = jax.random.split(key, 20)
    f32 = jnp.float32
    def nrm(k, shape, scale):
        return jax.random.normal(k, shape, f32) * scale
    x = jax.random.normal(ks[0], (BATCH, SEQ, D_MODEL), f32)
    c = jax.random.normal(ks[1], (BATCH, D_MODEL), f32)
    offsets = jax.random.randint(ks[2], (BATCH, 1), 0, 4096, dtype=jnp.int32)
    positions = (offsets + jnp.arange(SEQ, dtype=jnp.int32)[None, :]).astype(jnp.int32)
    return {
        "x": x,
        "c": c,
        "positions": positions,
        "ada_w": nrm(ks[3], (DEPTH, D_MODEL, N_MOD * D_MODEL), D_MODEL ** -0.5),
        "ada_b": nrm(ks[4], (DEPTH, N_MOD * D_MODEL), 0.02),
        "w_in": nrm(ks[5], (DEPTH, D_MODEL, IN_WIDTH), D_MODEL ** -0.5),
        "b_in": nrm(ks[6], (DEPTH, IN_WIDTH), 0.02),
        "sinks": nrm(ks[7], (DEPTH, N_HEADS), 1.0),
        "pool_w": nrm(ks[8], (DEPTH, N_POOL_GROUPS, POOL_GROUP_WIDTH, POOL_GROUP_WIDTH), POOL_GROUP_WIDTH ** -0.5),
        "pool_scale": 1.0 + nrm(ks[9], (DEPTH, POOL_WIDTH), 0.1),
        "w_out": nrm(ks[10], (DEPTH, MIX_WIDTH, D_MODEL), MIX_WIDTH ** -0.5),
        "w_gate": nrm(ks[11], (DEPTH, D_MODEL, D_FF_2), D_MODEL ** -0.5),
        "w_up": nrm(ks[12], (DEPTH, D_MODEL, D_FF_2), D_MODEL ** -0.5),
        "w_down": nrm(ks[13], (DEPTH, D_FF_2, D_MODEL), D_FF_2 ** -0.5),
        "g_pre_mix": 1.0 + nrm(ks[14], (DEPTH, D_MODEL), 0.02),
        "g_post_mix": 1.0 + nrm(ks[15], (DEPTH, D_MODEL), 0.02),
        "g_pre_ffn": 1.0 + nrm(ks[16], (DEPTH, D_MODEL), 0.02),
        "g_post_ffn": 1.0 + nrm(ks[17], (DEPTH, D_MODEL), 0.02),
    }

def second_block(x, c, positions, ada_w, ada_b, w_in, b_in, sinks, pool_w, pool_scale,
              w_out, w_gate, w_up, w_down, g_pre_mix, g_post_mix, g_pre_ffn, g_post_ffn):
    B, S = x.shape[0], x.shape[1]
    c_act = jax.nn.silu(c)
    for l in range(DEPTH):
        mod = c_act @ ada_w[l] + ada_b[l]
        shift_m, scale_m, gate_m, shift_f, scale_f, gate_f = [
            m[:, None, :] for m in jnp.split(mod, N_MOD, axis=-1)]

        h = rms_norm(x, g_pre_mix[l]) * (1.0 + scale_m) + shift_m
        proj = h @ w_in[l] + b_in[l]
        q, k, v, u = jnp.split(
            proj, [ATTN_WIDTH, ATTN_WIDTH + KV_WIDTH, ATTN_WIDTH + 2 * KV_WIDTH], axis=-1)
        q = partial_rotary(q.reshape(B, S, N_HEADS, HEAD_DIM), positions)
        k = partial_rotary(k.reshape(B, S, N_KV_HEADS, HEAD_DIM), positions)
        v = v.reshape(B, S, N_KV_HEADS, HEAD_DIM)
        attn_out = sliding_window_attention_with_sinks(q, k, v, sinks[l])
        pool_out = causal_pool_mixer(u, pool_w[l], pool_scale[l])
        mix = jnp.concatenate([attn_out, pool_out], axis=-1) @ w_out[l]
        x = x + gate_m * rms_norm(mix, g_post_mix[l])

        h = rms_norm(x, g_pre_ffn[l]) * (1.0 + scale_f) + shift_f
        f = (jax.nn.silu(h @ w_gate[l]) * (h @ w_up[l])) @ w_down[l]
        x = x + gate_f * rms_norm(f, g_post_ffn[l])
    return x


def setup_inputs(seed=0):
    out = dict(first_inputs(seed))
    for name, value in second_inputs(seed + 1).items():
        if name != "x":
            out[name + "_2"] = value
    return out


def reference(
    x, mix_norm_g, w_in, ret_norm_g, ssd_conv_w, ssd_conv_b, ssd_dt_bias, ssd_a_log, ssd_d,
    ssd_norm_g, gla_w_alpha, gla_b_alpha, gla_norm_g, ml_conv_w, ml_conv_b, ml_b_i, ml_b_f,
    ml_norm_g, w_branch, w_out, ffn_norm_g, ffn_w1, ffn_w3, ffn_w2, router_w, moe_w1, moe_w3,
    moe_w2, final_norm_g, c_2, positions_2, ada_w_2, ada_b_2, w_in_2, b_in_2, sinks_2, pool_w_2,
    pool_scale_2, w_out_2, w_gate_2, w_up_2, w_down_2, g_pre_mix_2, g_post_mix_2, g_pre_ffn_2,
    g_post_ffn_2,
):
    x = first_block(
        x, mix_norm_g, w_in, ret_norm_g, ssd_conv_w, ssd_conv_b, ssd_dt_bias, ssd_a_log, ssd_d,
        ssd_norm_g, gla_w_alpha, gla_b_alpha, gla_norm_g, ml_conv_w, ml_conv_b, ml_b_i, ml_b_f,
        ml_norm_g, w_branch, w_out, ffn_norm_g, ffn_w1, ffn_w3, ffn_w2, router_w, moe_w1,
        moe_w3, moe_w2, final_norm_g,
    )
    return second_block(
        x, c_2, positions_2, ada_w_2, ada_b_2, w_in_2, b_in_2, sinks_2, pool_w_2, pool_scale_2,
        w_out_2, w_gate_2, w_up_2, w_down_2, g_pre_mix_2, g_post_mix_2, g_pre_ffn_2,
        g_post_ffn_2,
    )


_drawn_inputs = setup_inputs


def setup_inputs(seed=0):
    import zlib

    import numpy as np

    out = dict(_drawn_inputs(seed))
    spreads = {}
    factors = {'ret_norm_g': 7.205,
     'ssd_conv_b': 3.326,
     'ssd_norm_g': 4.197,
     'gla_b_alpha': 3.688,
     'gla_norm_g': 4.197,
     'ml_conv_b': 4.495,
     'ml_b_i': 64.0,
     'ml_norm_g': 8.0,
     'ffn_norm_g': 2.792,
     'b_in_2': 4.612,
     'g_pre_mix_2': 3.868,
     'g_post_mix_2': 4.072,
     'g_pre_ffn_2': 3.47,
     'g_post_ffn_2': 4.366}
    for name, (base, spread) in spreads.items():
        noise = np.random.default_rng([zlib.crc32(name.encode()), seed]).standard_normal(out[name].shape)
        drawn = base * np.exp(spread * noise) if base else spread * noise
        out[name] = jnp.asarray(drawn.astype(out[name].dtype))
    for name, factor in factors.items():
        out[name] = (out[name] * factor).astype(out[name].dtype)
    return out
```

```python
from contextlib import ExitStack

import numpy as np
import concourse.bass as bass
from concourse import mybir

F32 = mybir.dt.float32
I32 = mybir.dt.int32
ALU = mybir.AluOpType
ACT = mybir.ActivationFunctionType
AXX = mybir.AxisListType.X

P = 128
T = 256
NT = T // P
D = 1024
KD = D // P
DEPTH = 2
MIX = D // 4
NB = 4
NH = 4
HD = MIX // NH
EPS = 1e-6
FF = 2816
NFF = FF // P
NE = 8
BANK = 512
SC = T + P
GLA_DK = MIX // (2 * NH)
GLA_TAU = 16.0
CONV_K = 4
NSX, NMQ = 6, 4
PAD = CONV_K - 1
MOD = 6 * D
QH, KVH = 8, 2
ROT = HD // 4
WINDOWS = (2, 4, 8, 16)
GLA_LEVELS = (64, 32, 16, 8, 4, 2, 1)

COLS = {}
_at = 0
for _name, _n in (("rq", 256), ("rk", 256), ("rv", 256), ("rg", 256), ("sz", 256), ("sxbc", 768),
                  ("sdt", 4), ("gq", 128), ("gk", 128), ("gv", 256), ("gr", 256), ("ga", 16),
                  ("mqk", 512), ("mv", 256), ("mo", 256), ("mi", 4), ("mf", 4), ("mgate", 4096)):
    COLS[_name] = _at
    _at += _n

SLOT = KD * 528
NSLOT = 4
SCRATCH = 15700
DSLOT = 2 * D
NDSLOT = 4


class Mark:

    def __init__(self, sem, value):
        self.sem, self.value = sem, value


class Queue:

    def __init__(self, sem, wait_ge, chained):
        self.sem, self.wait_ge, self.chained = sem, wait_ge, chained
        self.count, self.steps, self.seen, self.last = 0, [], {}, None

    def wait(self, *marks):
        for m in marks:
            if m is not None and self.seen.get(m.sem, 0) < m.value:
                self.seen[m.sem] = m.value
                self.steps.append((self.wait_ge, (m.sem, m.value), {}, None, 0))

    def run(self, op, *args, after=(), mark=True, own=None, **kw):
        if self.chained if own is None else own:
            self.wait(self.last)
        self.wait(*after)
        if not mark:
            self.steps.append((op, args, kw, None, 0))
            return None
        self.count += 1
        self.steps.append((op, args, kw, self.sem, 1))
        self.last = Mark(self.sem, self.count)
        return self.last

    def dma(self, op, out, in_, sem, after=()):
        self.wait(*after)
        sem[1] += 16
        self.steps.append((op, (out, in_), {}, sem[0], 16))
        return Mark(sem[0], sem[1])

    def play(self):
        for op, args, kw, sem, by in self.steps:
            i = op(*args, **kw)
            if sem is not None:
                i.then_inc(sem, by)


class Slots:

    def __init__(self, items):
        self.free = [(item, ()) for item in items]

    def take(self):
        return self.free.pop(0)

    def give(self, item, *marks):
        self.free.append((item, marks))


def program(nc, a, out, taps=None):
    with ExitStack() as ctx:
        def sb(name, n, dt=F32, rows=P):
            return ctx.enter_context(nc.sbuf_tensor(name, [rows, n], dt))

        def sem(name):
            return ctx.enter_context(nc.semaphore(name))

        PE = Queue(sem("tensor_done"), nc.tensor.wait_ge, False)
        S = Queue(sem("scalar_done"), nc.scalar.wait_ge, True)
        V = Queue(sem("vector_done"), nc.vector.wait_ge, True)
        G = Queue(sem("gpsimd_done"), nc.gpsimd.wait_ge, True)
        SP = Queue(sem("sync_done"), nc.sync.wait_ge, False)
        tt, ts, stt = nc.vector.tensor_tensor, nc.vector.tensor_scalar, nc.vector.scalar_tensor_tensor
        vcopy, act, mm = nc.vector.tensor_copy, nc.scalar.activation, nc.tensor.matmul

        x = sb("x", NT * D)
        xn = sb("xn", NT * D)
        hT = sb("hT", KD * T)
        ring = sb("ring", NSLOT * SLOT)
        gates = sb("gates", NT * NB * D)
        cst = sb("cst", a["const"].shape[1])
        lmask = sb("lmask", a["lmask"].shape[1], I32)
        cols = sb("cols", a["cols"].shape[1])
        rows_t = sb("rows_t", 4 * MIX + NH)
        scratch = sb("scratch", SCRATCH)
        small = sb("small", 640)
        banks = [ctx.enter_context(nc.psum_tensor(f"bank{i}", [P, BANK], F32)) for i in range(8)]
        x3 = x[:, :].rearrange("p (t d) -> p t d", t=NT)
        xn3 = xn[:, :].rearrange("p (t d) -> p t d", t=NT)
        h3 = hT[:, :].rearrange("p (k t) -> p k t", k=KD)
        g3 = gates[:, :].rearrange("p (t n) -> p t n", t=NT)

        at = [0]

        def region(n):
            at[0] += n
            assert at[0] <= SCRATCH, at[0]
            return scratch[:, at[0] - n:at[0]]

        s_at = [0]

        def tiny(n):
            s_at[0] += n
            assert s_at[0] <= 640
            return small[:, s_at[0] - n:s_at[0]]

        def const(name):
            o, n = CONST[name]
            return cst[:, o:o + n]

        def col(name, l, i=0, n=1, rows=P):
            o = COLUMN[(name, l)] + i
            return cols[0:rows, o:o + n]

        wslots = Slots([(ring[:, i * SLOT:(i + 1) * SLOT], [sem(f"weights{i}_in"), 0]) for i in range(NSLOT)])
        dslots = Slots([(gates[:, i * DSLOT:(i + 1) * DSLOT], [sem(f"down{i}_in"), 0]) for i in range(NDSLOT)])

        class Weights:

            def __init__(self, slots):
                (self.slot, self.freed), self.slots = slots.take(), slots
                self.ap, self.cell = self.slot
                self.mark = None

            def into(self, dst, src):
                self.mark = SP.dma(nc.sync.dma_start, dst, src, self.cell, after=self.freed)

            def done(self, *marks):
                self.slots.give(self.slot, *marks)

        def load_cols(w, c0, n):
            u = Weights(wslots)
            dst = u.ap[:, 0:KD * n].rearrange("p (k n) -> p k n", k=KD)
            u.into(dst, w[:, c0:c0 + n].rearrange("(k p) n -> p k n", p=P))
            return u, dst

        pool = Slots(banks)

        def evacuated(bank, *marks):
            pool.give(bank, *marks)

        def group(dst, pairs, after=(), start=True, stop=True):
            PE.wait(*after)
            m = None
            for i, (l_, r_) in enumerate(pairs):
                last = i == len(pairs) - 1
                m = PE.run(mm, dst, l_, r_, start=start and i == 0, stop=stop and last, mark=last)
            return m

        s_const, s_rows, s_x, s_out, s_att = ([sem(n), 0] for n in (
            "constants_in", "row_parameters_in", "x_in", "result_out", "attention_tables_in"))
        x_in = SP.dma(nc.sync.dma_start, x3, a["x"].rearrange("o (t p) d -> p (o t) d", p=P), s_x)
        cm = S.dma(nc.scalar.dma_start, cst[:, :], a["const"], s_const)
        cm = S.dma(nc.scalar.dma_start, cols[:, :], a["cols"], s_const)
        cm = S.dma(nc.scalar.dma_start, lmask[:, :], a["lmask"], s_const)
        for q in (PE, V, S, G):
            q.wait(cm)
        V.wait(x_in)
        S.wait(x_in)
        ident = const("ident")

        stat = tiny(16)

        def join():
            lasts = [q.last for q in (PE, V, S, G)]
            for q in (PE, V, S, G):
                q.wait(*lasts)

        def inverse_root(dst, sums, n, ready):
            G.run(nc.gpsimd.tensor_scalar, dst, sums, 1.0 / n, EPS, ALU.mult, ALU.add, after=[ready])
            return G.run(nc.gpsimd.tensor_tensor, dst, dst, const("power").broadcast_to(list(dst.shape)), ALU.pow)

        def rms(src3, dst3, ready=()):
            m = None
            for t in range(NT):
                m = S.run(act, dst3[:, t, :], src3[:, t, :], ACT.Square, accum_out=stat[:, t:t + 1], after=ready)
            V.wait(inverse_root(stat[:, 4:6], stat[:, 0:2], D, m))
            for t in range(NT):
                m = V.run(ts, dst3[:, t, :], src3[:, t, :], stat[:, 4 + t:5 + t], None, ALU.mult, own=(t == 0))
            return m

        def to_features(src3, n, dst, ready, scale=None):
            marks = []
            for k in range(0, n, 2):
                bank, freed = pool.take()
                PE.wait(*freed, ready)
                m = None
                for j in range(2):
                    for t in range(NT):
                        c = (2 * j + t) * P
                        m = PE.run(nc.tensor.transpose, bank[:, c:c + P], src3[:, t, (k + j) * P:(k + j + 1) * P],
                                   ident, mark=(j == 1 and t == NT - 1))
                if scale is None:
                    d = V.run(vcopy, dst[:, k:k + 2, :], bank[:, :].rearrange("p (k t) -> p k t", k=2),
                              after=[m], own=False)
                else:
                    for j in range(2):
                        d = V.run(ts, dst[:, k + j, :], bank[:, j * T:(j + 1) * T], scale(k + j), None, ALU.mult,
                                  after=[m], own=False)
                evacuated(bank, d)
                marks.append(d)
            return marks[-1]

        def tap(name, ap):
            if taps is not None and name in taps:
                join()
                SP.wait(*[q.last for q in (PE, V, S, G)])
                m = SP.dma(nc.sync.dma_start, taps[name], ap, s_out)
                SP.wait(m)
                for q in (PE, V, S, G):
                    q.wait(m)

        tail = [scratch[:, SCRATCH - (i + 1) * T:SCRATCH - i * T] for i in range(6)]
        ups, gateds = Slots(tail[0:3]), Slots(tail[3:6])

        def feed_forward(hsrc, n, w1, w3, w2, ready, pool_a, pool_y):
            nt = n // P
            ys = []
            for _ in range(nt * 2):
                ys.append(pool_y.take())
            PE.wait(*[m for _, f in ys for m in f], ready)
            pending = []
            ymark = None

            def down(f, gt, gmark, w2u, w2ap, w2last):
                nonlocal ymark
                PE.wait(gmark, w2u.mark)
                for t in range(nt):
                    for hf in range(2):
                        last = t == nt - 1 and hf == 1
                        m = PE.run(mm, ys[2 * t + hf][0][:, :], gt[:, t * P:(t + 1) * P],
                                   w2ap[:, hf * BANK:(hf + 1) * BANK], start=f == 0, stop=f == NFF - 1, mark=last)
                ymark = m
                gateds.give(gt, m)
                if w2last:
                    w2u.done(m)

            for f2 in range(NFF // 2):
                u = Weights(wslots)
                w13 = u.ap[:, 0:KD * 4 * P].rearrange("p (w k n) -> p w k n", w=2, k=KD)
                for w, src in enumerate((w1, w3)):
                    u.into(w13[:, w], src[:, f2 * 2 * P:(f2 + 1) * 2 * P].rearrange("(k p) n -> p k n", p=P))
                du = Weights(dslots)
                w2v = du.ap.rearrange("p (f n) -> p f n", f=2)
                du.into(w2v, w2[f2 * 2 * P:(f2 + 1) * 2 * P, :].rearrange("(f p) n -> p f n", p=P))
                for j in range(2):
                    f = 2 * f2 + j
                    bank, freed = pool_a.take()
                    PE.wait(*freed, u.mark)
                    for w in range(2):
                        m = group(bank[:, w * n:(w + 1) * n],
                                  [(w13[:, w, k, j * P:(j + 1) * P], hsrc[:, k, :]) for k in range(KD)])
                    if j == 1:
                        u.done(m)
                    sg, f1 = ups.take()
                    gt, f2_ = gateds.take()
                    s = S.run(act, sg[:, 0:n], bank[:, 0:n], ACT.Silu, after=[m, *f1], own=False)
                    g = V.run(tt, gt[:, 0:n], sg[:, 0:n], bank[:, n:2 * n], ALU.mult, after=[s, *f2_], own=False)
                    ups.give(sg, g)
                    pool_a.give(bank, g)
                    pending.append((f, gt, g, du, w2v[:, j, :], j == 1))
                    if len(pending) > 1:
                        down(*pending.pop(0))
            while pending:
                down(*pending.pop(0))
            return ys, ymark

        at[0] = 0
        obuf = region(NT * MIX)
        rv, silrg, silsz, gv, silgr, sigmo = (region(NT * MIX) for _ in range(6))
        mva = region(NT * NH * (HD + 1))
        padded = region((NSX + NMQ) * (T + PAD))
        conv = region((NSX + NMQ) * T)
        rqk = padded[:, NH * SC:NH * SC + 4 * T]
        qk0 = region(4 * T)
        glaq, glak, glaG, glaE = (region(T) for _ in range(4))
        osq = region(2 * T)
        glaX = [osq[:, 0:T], osq[:, T:2 * T]]
        tok3 = lambda ap: ap.rearrange("p (t n) -> p t n", t=NT)
        heads = lambda ap: ap.rearrange("p (t h n) -> p t h n", t=NT, h=NH)
        pad3 = padded.rearrange("p (c t) -> p c t", t=T + PAD)
        conv3 = conv.rearrange("p (c t) -> p c t", t=T)
        rqk3 = rqk.rearrange("p (c t) -> p c t", t=T)
        scoresA = padded[:, 0:NH * SC]
        scoresB = region(NH * SC)
        rowbuf = region(9 * T)
        r_ = lambda i, n=NH: rowbuf[0:n, i * T:(i + 1) * T]
        DT, ACS, LF, BC, CJ, NM, TMP, TMP2, GA = range(9)
        MX = LF
        tokcol = tiny(4 * NT * NH)
        tc4 = tokcol.rearrange("p (r t h) -> p r t h", r=4, t=NT)
        ss8, rs8, den8 = tiny(NT * NH), tiny(NT * NH), tiny(NT * NH)
        ones_row = const("ones")
        yT = xn[:, :].rearrange("p (b c t) -> p b c t", b=NB, c=2)

        def softplus_rows(dst, src, tmp, tmp2):
            v = V.run(stt, tmp, src, -1.0, src, ALU.mult, ALU.min)
            s = S.run(act, tmp2, tmp, ACT.Exp, after=[v])
            s = S.run(act, tmp2, tmp2, ACT.Ln, bias=1.0)
            return V.run(stt, dst, src, 0.0, tmp2, ALU.max, ALU.add, after=[s])

        for l in range(DEPTH):
            win = a["w_in"][l]
            rm = S.dma(nc.scalar.dma_start, rows_t[:, :],
                       a["rows1"][l:l + 1, :].broadcast_to([P, 4 * MIX + NH]), s_rows)
            V.wait(rm)
            G.wait(rm)
            m = rms(x3, xn3)
            hm = to_features(xn3, KD, h3, m, scale=lambda k: col("mix_g", l, k))
            tap(f"hT{l}", h3)

            def project_tokens(u, w, c0, n, t, bank_cols=None):
                bank, freed = pool.take()
                m = group(bank[:, 0:n], [(h3[:, k, t * P:(t + 1) * P], w[:, k, c0:c0 + n]) for k in range(KD)],
                          after=[*freed, u.mark, hm])
                return bank, m

            def project_features(u, w, places, rows=P):
                bank, freed = pool.take()
                PE.wait(*freed, u.mark, hm)
                for i, c in enumerate(places):
                    m = group(bank[0:rows, i * T:(i + 1) * T],
                              [(w[:, k, c:c + rows], h3[:, k, :]) for k in range(KD)])
                return bank, m

            if l == 0:
                V.run(nc.vector.memset, heads(mva)[:, :, :, HD:HD + 1], 1.0)
            V.run(nc.vector.memset, pad3[:, :, 0:PAD], 0.0)

            u, w = load_cols(win, COLS["rv"], 512)
            for t in range(NT):
                bank, m = project_tokens(u, w, 0, 512, t)
                s = S.run(act, tok3(silrg)[:, t], bank[:, MIX:2 * MIX], ACT.Silu, after=[m], own=False)
                s = S.run(act, tok3(rv)[:, t], bank[:, 0:MIX], ACT.Copy, own=False)
                evacuated(bank, s)
            u.done(m)
            u, w = load_cols(win, COLS["sz"], MIX)
            for t in range(NT):
                bank, m = project_tokens(u, w, 0, MIX, t)
                s = S.run(act, tok3(silsz)[:, t], bank[:, 0:MIX], ACT.Silu, after=[m], own=False)
                evacuated(bank, s)
            u.done(m)
            conv_in = []

            def to_pad(bank, m, first):
                return V.run(vcopy, pad3[:, first:first + 2, PAD:], bank[:, :].rearrange("p (c t) -> p c t", c=2),
                             after=[m], own=False)

            u, w = load_cols(win, COLS["sxbc"], 512)
            for i in range(2):
                bank, m = project_features(u, w, [2 * i * P, (2 * i + 1) * P])
                v = to_pad(bank, m, 2 * i)
                evacuated(bank, v)
            u.done(m)
            u, w = load_cols(win, COLS["sxbc"] + 512, 516)
            bank, m = project_features(u, w, [0, P])
            v = to_pad(bank, m, 4)
            evacuated(bank, v)
            bank, m = project_features(u, w, [260, 260 + P])
            s = S.run(act, glaq, bank[:, 0:T], ACT.Copy, scale=GLA_DK ** -0.5, after=[m], own=False)
            s = S.run(act, glak, bank[:, T:2 * T], ACT.Copy, own=False)
            evacuated(bank, s)
            bank, m = project_features(u, w, [256], rows=NH)
            v = V.run(ts, r_(DT), bank[0:NH, 0:T], col("dt_bias", l, rows=NH), None, ALU.add, after=[m], own=False)
            evacuated(bank, v)
            u.done(m)
            u, w = load_cols(win, COLS["mqk"], 512)
            for i in range(2):
                bank, m = project_features(u, w, [2 * i * P, (2 * i + 1) * P])
                v = to_pad(bank, m, NSX + 2 * i)
                evacuated(bank, v)
            u.done(m)

            def convolve(c, name, i, n):
                dst = conv3[:, c, :]
                v = V.run(ts, dst, pad3[:, c, 0:T], col(name + "_w", l, i), col(name + "_b", l, i),
                          ALU.mult, ALU.add)
                for k in range(1, CONV_K):
                    v = V.run(stt, dst, pad3[:, c, k:k + T], col(name + "_w", l, k * n + i), dst,
                              ALU.mult, ALU.add)
                return S.run(act, dst, dst, ACT.Silu, after=[v], own=False)

            for c in range(NSX):
                convolve(c, "ssd_conv", c, NSX)
            u, w = load_cols(win, COLS["gv"], 528)
            for t in range(NT):
                bank, m = project_tokens(u, w, 0, 512, t)
                s = S.run(act, tok3(silgr)[:, t], bank[:, MIX:2 * MIX], ACT.Silu, after=[m], own=False)
                s = S.run(act, tok3(gv)[:, t], bank[:, 0:MIX], ACT.Copy, own=False)
                evacuated(bank, s)
            bank, m = project_features(u, w, [512], rows=16)
            s = S.run(act, r_(GA, 16), bank[0:16, 0:T], ACT.Copy, after=[m], own=False)
            evacuated(bank, s)
            u.done(m)
            ga_mark = s
            for c in range(NMQ):
                conv_done = convolve(NSX + c, "ml_conv", c, NMQ)
            u, w = load_cols(win, COLS["mv"], 520)
            for t in range(NT):
                bank, m = project_tokens(u, w, 0, 512, t)
                s = S.run(act, tok3(sigmo)[:, t], bank[:, MIX:2 * MIX], ACT.Tanh, scale=0.5, after=[m], own=False)
                s = S.run(act, heads(mva)[:, t, :, 0:HD],
                          bank[:, 0:MIX].rearrange("p (h n) -> p h n", h=NH), ACT.Copy, own=False)
                evacuated(bank, s)
            silu_done = s
            bank, m = project_features(u, w, [512], rows=NH)
            bank2, m2 = project_features(u, w, [516], rows=NH)
            v = V.run(ts, r_(CJ), bank[0:NH, 0:T], col("b_i", l, rows=NH), None, ALU.add, after=[m], own=False)
            evacuated(bank, v)
            v = V.run(ts, r_(LF), bank2[0:NH, 0:T], col("b_f", l, rows=NH), -1.0, ALU.add, ALU.mult,
                      after=[m2], own=False)
            evacuated(bank2, v)
            u.done(m2)
            u, w = load_cols(win, COLS["rq"], 512)
            rot_raw = qk0.rearrange("p (c t) -> p c t", t=T)
            for i in range(2):
                bank, m = project_features(u, w, [2 * i * P, (2 * i + 1) * P])
                s = S.run(act, rot_raw[:, 2 * i:2 * i + 2, :], bank[:, :].rearrange("p (c t) -> p c t", c=2),
                          ACT.Copy, after=[m], own=False)
                evacuated(bank, s)
            u.done(m)
            qk_raw = s
            grow = lambda i: rows_t[:, i * MIX:(i + 1) * MIX]
            V.run(tt, tok3(silrg), tok3(silrg), grow(0).unsqueeze(1).broadcast_to([P, NT, MIX]), ALU.mult,
                  after=[silu_done])
            V.run(tt, tok3(silgr), tok3(silgr), grow(2).unsqueeze(1).broadcast_to([P, NT, MIX]), ALU.mult)
            V.run(ts, sigmo, sigmo, 1.0, 0.5, ALU.add, ALU.mult)
            V.run(tt, tok3(sigmo), tok3(sigmo), grow(3).unsqueeze(1).broadcast_to([P, NT, MIX]), ALU.mult)
            tap(f"conv{l}", conv)

            def scores(qt, kt, rows, bank, after=()):
                PE.wait(*after)
                PE.run(mm, bank[:, 0:T], kt[rows, 0:P], qt[rows, 0:T], start=True, stop=True, mark=False)
                return PE.run(mm, bank[:, T:SC], kt[rows, P:T], qt[rows, P:T], start=True, stop=True)

            def apply_scores(sc, v4, after, width=HD):
                outs = []
                PE.wait(*after)
                for t in range(NT):
                    bank, freed = pool.take()
                    PE.wait(*freed)
                    o = bank[:, 0:NH * width].rearrange("p (h n) -> p h n", h=NH)
                    for h in range(NH):
                        if t == 0:
                            m = group(o[:, h, :], [(sc[:, h, 0:P], v4[:, 0, h, :])])
                        else:
                            m = group(o[:, h, :], [(sc[:, h, P:T], v4[:, 0, h, :]), (sc[:, h, T:SC], v4[:, 1, h, :])])
                    outs.append((bank, o, m))
                return outs

            def head_norm(src, side, b, src_marks=(), lone=False):
                n = 1 if lone else NH
                w_ = MIX // n
                s4 = src.rearrange("p (t h n) -> p t h n", t=NT, h=n)
                V.run(tt, osq, src, src, ALU.mult, after=src_marks)
                V.run(nc.vector.tensor_reduce, ss8[:, 0:NT * n], osq.rearrange("p (g n) -> p g n", n=w_),
                      AXX, ALU.add)
                V.wait(inverse_root(rs8[:, 0:NT * n], ss8[:, 0:NT * n], w_, V.last))
                g_ = src.rearrange("p (g n) -> p g n", n=w_)
                V.run(tt, g_, g_, rs8[:, 0:NT * n].unsqueeze(2).broadcast_to([P, NT * n, w_]), ALU.mult)
                v = V.run(tt, src, src, side, ALU.mult)
                bank, freed = pool.take()
                PE.wait(*freed, v)
                for c in range(2):
                    for t in range(NT):
                        m = PE.run(nc.tensor.transpose, bank[:, (2 * c + t) * P:(2 * c + t + 1) * P],
                                   tok3(src)[:, t, c * P:(c + 1) * P], ident, mark=(c == 1 and t == 1))
                v = V.run(vcopy, yT[:, b], bank[:, :].rearrange("p (c t) -> p c t", c=2), after=[m])
                evacuated(bank, v)
                return v

            def mixers():
                softplus_rows(r_(DT), r_(DT), r_(TMP), r_(TMP2))
                s = S.run(act, small[0:NH, 600:601], col("a_log", l, rows=NH), ACT.Exp)
                V.run(ts, r_(TMP), r_(DT), small[0:NH, 600:601], -1.0, ALU.mult, ALU.mult, after=[s])
                dm = V.run(nc.vector.tensor_tensor_scan, r_(ACS), ones_row[0:NH, :], r_(TMP), 0.0, ALU.mult, ALU.add)
                yield
                softplus_rows(r_(LF), r_(LF), r_(TMP), r_(TMP2))
                V.run(ts, r_(LF), r_(LF), -1.0, None, ALU.mult)
                V.run(nc.vector.tensor_tensor_scan, r_(BC), ones_row[0:NH, :], r_(LF), 0.0, ALU.mult, ALU.add)
                V.run(tt, r_(CJ), r_(CJ), r_(BC), ALU.subtract)
                V.run(nc.vector.tensor_tensor_scan, r_(MX), ones_row[0:NH, :], r_(CJ), 0.0, ALU.mult, ALU.max)
                V.run(tt, r_(TMP), r_(BC), r_(MX), ALU.add)
                v = V.run(ts, r_(NM), r_(MX), -1.0, None, ALU.mult)
                s = S.run(act, r_(TMP2), r_(TMP), ACT.Exp, scale=-1.0, after=[v])
                bank, freed = pool.take()
                PE.wait(*freed, v, s)
                for i, r in enumerate((ACS, DT, CJ, TMP2)):
                    for t in range(NT):
                        c = (i * NT + t) * NH
                        m = PE.run(nc.tensor.transpose, bank[:, c:c + NH], rowbuf[0:NH, r * T + t * P:r * T + (t + 1) * P],
                                   ident[0:NH, 0:NH], mark=(i == 3 and t == 1))
                v = V.run(vcopy, tokcol, bank[:, 0:4 * NT * NH], after=[m])
                evacuated(bank, v)
                yield

                PE.wait(qk_raw)
                for i in range(2):
                    bank, freed = pool.take()
                    PE.wait(*freed)
                    m = PE.run(mm, bank[:, :], const("rot"), qk0[:, i * 2 * T:(i + 1) * 2 * T], start=True, stop=True)
                    both = lambda n: const(n).unsqueeze(1).broadcast_to([P, 2, T])
                    V.run(tt, rqk3[:, 2 * i:2 * i + 2, :], bank[:, :].rearrange("p (c t) -> p c t", c=2), both("sin"),
                          ALU.mult, after=[m])
                    evacuated(bank, V.last)
                    V.run(tt, rot_raw[:, 2 * i:2 * i + 2, :], rot_raw[:, 2 * i:2 * i + 2, :], both("cos"), ALU.mult)
                    v = V.run(tt, rqk3[:, 2 * i:2 * i + 2, :], rqk3[:, 2 * i:2 * i + 2, :],
                              rot_raw[:, 2 * i:2 * i + 2, :], ALU.add)
                    yield
                scB = scoresB.rearrange("p (h n) -> p h n", h=NH)
                dec = const("decay").rearrange("p (h n) -> p h n", h=NH)
                PE.wait(v)
                for h in range(NH):
                    bank, freed = pool.take()
                    rows = slice((h % 2) * HD, (h % 2 + 1) * HD)
                    m = scores(rqk3[:, h // 2, :], rqk3[:, 2 + h // 2, :], rows, bank, after=freed)
                    v = V.run(tt, scB[:, h, :], bank[:, 0:SC], dec[:, h, :], ALU.mult, after=[m], own=(h == 0))
                    evacuated(bank, v)
                outs = apply_scores(scB, heads(rv), [v])
                for t, (bank, o, m) in enumerate(outs):
                    s = S.run(act, tok3(obuf)[:, t], bank[:, 0:MIX], ACT.Copy, after=[m], own=False)
                    evacuated(bank, s)
                yield
                head_norm(obuf, silrg, 0, [s])
                yield
                tap(f"yret{l}", yT[:, 0])

                xs, xdt = qk0[:, 0:NT * MIX], qk0[:, NT * MIX:2 * NT * MIX]
                bank, freed = pool.take()
                PE.wait(*freed, conv_done)
                for t in range(NT):
                    for c in range(2):
                        m = PE.run(nc.tensor.transpose, bank[:, (2 * t + c) * P:(2 * t + c + 1) * P],
                                   conv3[:, c, t * P:(t + 1) * P], ident, mark=(c == 1 and t == 1))
                v = V.run(vcopy, xs, bank[:, :], after=[m])
                evacuated(bank, v)
                dtc = tc4[:, 1].unsqueeze(3).broadcast_to([P, NT, NH, HD])
                for t in range(NT):
                    V.run(tt, heads(xdt)[:, t], heads(xs)[:, t], dtc[:, t], ALU.mult)
                yield
                scA = scoresA.rearrange("p (h n) -> p h n", h=NH)

                def decays(dst, row, colid):
                    op = ALU.subtract if colid == 0 else ALU.add
                    for h2 in range(2):
                        bank, freed = pool.take()
                        PE.wait(*freed)
                        for j in range(2):
                            m = PE.run(mm, bank[:, j * T:(j + 1) * T],
                                       ident[0:NH, 2 * h2 + j:2 * h2 + j + 1].broadcast_to([NH, P]), row,
                                       start=True, stop=True, mark=(j == 1))
                        for j in range(2):
                            h = 2 * h2 + j
                            V.run(ts, dst[:, h, 0:T], bank[:, j * T:(j + 1) * T], tc4[:, colid, 0, h:h + 1], 0.0,
                                  op, ALU.min, after=[m], own=False)
                            v = V.run(ts, dst[:, h, T:SC], bank[:, j * T + P:(j + 1) * T], tc4[:, colid, 1, h:h + 1],
                                      0.0, op, ALU.min, own=False)
                        evacuated(bank, v)
                    return v

                PE.wait(dm)
                v = decays(scA, r_(ACS), 0)
                s = S.run(act, scoresA, scoresA, ACT.Exp, after=[v])
                yield
                for g in range(2):
                    bank, freed = pool.take()
                    m = scores(conv3[:, 4 + g, :], conv3[:, 2 + g, :], slice(0, P), bank, after=freed)
                    v = V.run(tt, scB[:, g, :], bank[:, 0:SC], const("tri"), ALU.mult, after=[m])
                    evacuated(bank, v)
                    V.run(tt, scA[:, 2 * g:2 * g + 2, :], scA[:, 2 * g:2 * g + 2, :],
                          scB[:, g, :].unsqueeze(1).broadcast_to([P, 2, SC]), ALU.mult, after=[s])
                outs = apply_scores(scA, heads(xdt), [V.last])
                drow = rows_t[:, 4 * MIX:4 * MIX + NH].unsqueeze(2).broadcast_to([P, NH, HD])
                for t, (bank, o, m) in enumerate(outs):
                    V.run(tt, heads(obuf)[:, t], heads(xs)[:, t], drow, ALU.mult)
                    v = V.run(tt, heads(obuf)[:, t], heads(obuf)[:, t], o, ALU.add, after=[m])
                    evacuated(bank, v)
                V.run(tt, obuf, obuf, silsz, ALU.mult)
                yield
                V.run(vcopy, tok3(silsz), grow(1).unsqueeze(1).broadcast_to([P, NT, MIX]))
                head_norm(obuf, silsz, 1, lone=True)
                yield
                tap(f"yssd{l}", yT[:, 1])

                v = decays(scA, r_(NM), 2)
                s = S.run(act, scoresA, scoresA, ACT.Exp, after=[v])
                yield
                V.run(stt, scA, scA, HD ** -0.5, const("tri").unsqueeze(1).broadcast_to([P, NH, SC]), ALU.mult,
                      ALU.mult, after=[s])
                for h in range(NH):
                    bank, freed = pool.take()
                    rows = slice((h % 2) * HD, (h % 2 + 1) * HD)
                    m = scores(conv3[:, NSX + h // 2, :], conv3[:, NSX + 2 + h // 2, :], rows, bank, after=freed)
                    v = V.run(tt, scA[:, h, :], scA[:, h, :], bank[:, 0:SC], ALU.mult, after=[m], own=(h == 0))
                    evacuated(bank, v)
                outs = apply_scores(scA, mva.rearrange("p (t h n) -> p t h n", t=NT, h=NH), [v], width=HD + 1)
                yield
                d3 = den8.rearrange("p (t h) -> p t h", t=NT)
                for t, (bank, o, m) in enumerate(outs):
                    V.run(vcopy, ss8[:, 0:NH], o[:, :, HD], after=[m])
                    V.run(stt, d3[:, t], ss8[:, 0:NH], -1.0, ss8[:, 0:NH], ALU.mult, ALU.max)
                    V.run(tt, d3[:, t], d3[:, t], tc4[:, 3, t], ALU.max)
                    V.run(nc.vector.reciprocal, d3[:, t], d3[:, t])
                    v = V.run(tt, heads(obuf)[:, t], o[:, :, 0:HD], d3[:, t].unsqueeze(2).broadcast_to([P, NH, HD]),
                              ALU.mult)
                    evacuated(bank, v)
                head_norm(obuf, sigmo, 3)
                yield
                tap(f"yml{l}", yT[:, 3])

                bank, freed = pool.take()
                m = group(bank[:, 0:T], [(cols[0:16, COLUMN[("w_alpha", l)]:COLUMN[("w_alpha", l)] + P], r_(GA, 16))],
                          after=[*freed, ga_mark])
                v = V.run(ts, glaG, bank[:, 0:T], col("b_alpha", l), -1.0, ALU.add, ALU.mult, after=[m])
                evacuated(bank, v)
                softplus_rows(glaE, glaG, glaX[0], glaX[1])
                V.run(ts, glaE, glaE, -1.0 / GLA_TAU, None, ALU.mult)
                V.run(nc.vector.tensor_tensor_scan, glaG, ones_row, glaE, 0.0, ALU.mult, ALU.add)
                yield
                V.run(nc.vector.memset, scB[:, :, 0:P], 0.0)
                V.run(nc.vector.memset, scB[:, :, T:SC], 0.0)
                lm3 = lmask[:, :].rearrange("p (l n) -> p l n", n=P)
                reads = [None, None]

                def level_scores(kt, qt, li, after):
                    PE.wait(*after)
                    own = [pool.take() for _ in range(NH)]
                    PE.wait(*[f for _, freed in own for f in freed])
                    blocks = [(0, slice(0, P), slice(P, T))] if li is None else [
                        (t, slice(t * P, (t + 1) * P), slice(t * P, (t + 1) * P)) for t in range(NT)]
                    marks = []
                    for b, kc, qc in blocks:
                        for h in range(NH):
                            rows = slice(h * GLA_DK, (h + 1) * GLA_DK)
                            marks.append(PE.run(mm, own[h][0][:, b * P:(b + 1) * P], kt[rows, kc], qt[rows, qc],
                                                start=True, stop=True, tile_position=(h * GLA_DK, 0),
                                                mark=(b == len(blocks) - 1)))
                    for h in range(NH):
                        bank, m = own[h][0], marks[-NH + h]
                        if li is None:
                            v = V.run(vcopy, scB[:, h, P:T], bank[:, 0:P], after=[m], own=False)
                        else:
                            dst = scB[:, h, :].rearrange("p (b n) -> p b n", n=P)[:, ::2, :]
                            v = V.run(nc.vector.copy_predicated, dst, lm3[:, li, :].unsqueeze(1).broadcast_to([P, NT, P]),
                                      bank[:, 0:T].rearrange("p (b n) -> p b n", n=P), after=[m], own=(h == 0))
                        evacuated(bank, v)
                    return marks[-1]

                level_scores(glak, glaq, len(GLA_LEVELS), [V.last])
                yield
                for i, half in enumerate((P,) + GLA_LEVELS):
                    buf = glaX[i % 2]
                    n = T // (2 * half)
                    view = lambda ap: ap.rearrange("p (n s c) -> p n s c", n=n, s=2)
                    ref = view(glaG)[:, :, 0, half - 1:half].broadcast_to([P, n, half])
                    V.run(tt, view(glaE)[:, :, 1, :], view(glaG)[:, :, 1, :], ref, ALU.subtract)
                    v = V.run(tt, view(glaE)[:, :, 0, :], ref, view(glaG)[:, :, 0, :], ALU.subtract, own=False)
                    s = S.run(act, glaE, glaE, ACT.Exp, after=[v])
                    V.run(tt, view(buf)[:, :, 1, :], view(glaE)[:, :, 1, :], view(glaq)[:, :, 1, :], ALU.mult,
                          after=[s, reads[i % 2]])
                    v = V.run(tt, view(buf)[:, :, 0, :], view(glaE)[:, :, 0, :], view(glak)[:, :, 0, :], ALU.mult,
                              own=False)
                    reads[i % 2] = level_scores(buf, buf, None if half == P else i - 1, [v])
                    yield
                outs = apply_scores(scB, heads(gv), [V.last])
                for t, (bank, o, m) in enumerate(outs):
                    s = S.run(act, tok3(obuf)[:, t], bank[:, 0:MIX], ACT.Copy, after=[m], own=False)
                    evacuated(bank, s)
                yield
                head_norm(obuf, silgr, 2, [s])
                tap(f"ygla{l}", yT[:, 2])

            def gate_projections():
                for c in range(NB * D // BANK):
                    u, w = load_cols(win, COLS["mgate"] + c * BANK, BANK)
                    for t in range(NT):
                        bank, m = project_tokens(u, w, 0, BANK, t)
                        s = S.run(act, g3[:, t, c * BANK:(c + 1) * BANK], bank[:, :], ACT.Copy, after=[m], own=False)
                        evacuated(bank, s)
                        if t == NT - 1:
                            u.done(m)
                        yield

            mix_steps, gate_steps = mixers(), gate_projections()
            more = True
            while more:
                more = next(mix_steps, 0) is None
                next(gate_steps, 0)
            for _ in gate_steps:
                pass

            s = None
            for t in range(NT):
                for n in range(NB):
                    s = S.run(act, g3[:, t, n * D:(n + 1) * D], g3[:, t, n * D:(n + 1) * D], ACT.Sigmoid,
                              own=(t == 0 and n == 0))
            V.wait(s)
            wb = []
            for hf in range(2):
                u = Weights(wslots)
                dst = u.ap[:, 0:2 * NB * BANK].rearrange("p (k n) -> p k n", k=2 * NB)
                u.into(dst, a["w_branch"][l].rearrange("b (c p) n -> p (b c) n", p=P)[:, :, hf * BANK:(hf + 1) * BANK])
                wb.append((u, dst))
            PE.wait(V.last)
            for hf, (u, w) in enumerate(wb):
                for t in range(NT):
                    for n in range(NB):
                        bank, freed = pool.take()
                        m = group(bank[:, :], [(yT[:, n, c, t * P:(t + 1) * P], w[:, 2 * n + c, :]) for c in range(2)],
                                  after=[*freed, u.mark])
                        dst = g3[:, t, n * D + hf * BANK:n * D + (hf + 1) * BANK]
                        v = V.run(tt, dst, dst, bank[:, :], ALU.mult, after=[m], own=False)
                        evacuated(bank, v)
                        acc = g3[:, t, hf * BANK:(hf + 1) * BANK]
                        if n > 0:
                            V.run(tt, acc, acc, dst, ALU.add)
                u.done(m)
            tap(f"merged{l}", g3[:, :, 0:D])
            mT = to_features(g3[:, :, 0:D], KD, h3, V.last)
            for hf in range(2):
                u, w = load_cols(a["w_out"][l], hf * BANK, BANK)
                for t in range(NT):
                    bank, freed = pool.take()
                    m = group(bank[:, :], [(h3[:, k, t * P:(t + 1) * P], w[:, k, :]) for k in range(KD)],
                              after=[*freed, u.mark, mT])
                    xo = x3[:, t, hf * BANK:(hf + 1) * BANK]
                    v = V.run(tt, xo, xo, bank[:, :], ALU.add, after=[m], own=False)
                    evacuated(bank, v)
                u.done(m)
            tap(f"xmix{l}", x3)
            join()
            for i in range(len(dslots.free)):
                dslots.free[i] = (dslots.free[i][0], (V.last, PE.last))

            m = rms(x3, xn3, ready=[V.last])
            hm = to_features(xn3, KD, h3, m, scale=lambda k: col("ffn_g", l, k))
            join()
            pool_y, pool_a = Slots(banks[0:4]), Slots(banks[4:8])
            if l % 2 == 0:
                ys, ym = feed_forward(h3, T, a["ffn_w1"][0], a["ffn_w3"][0], a["ffn_w2"][0], hm, pool_a, pool_y)
                for i, (bank, _) in enumerate(ys):
                    t, hf = divmod(i, 2)
                    xo = x3[:, t, hf * BANK:(hf + 1) * BANK]
                    v = V.run(tt, xo, xo, bank[0][:, :] if isinstance(bank, tuple) else bank[:, :], ALU.add,
                              after=[ym], own=False)
            else:
                bank, freed = pool_a.take()
                for t in range(NT):
                    m = group(bank[:, t * NE:(t + 1) * NE],
                              [(h3[:, k, t * P:(t + 1) * P], col("router", 0, k * NE, NE)) for k in range(KD)],
                              after=[*freed])
                lg, top, gate8 = tiny(NT * NE), tiny(NT * NE), tiny(NT * NE)
                idx = ctx.enter_context(nc.sbuf_tensor("idx", [P, NT * NE], mybir.dt.uint32))
                idf, w12, g8b = tiny(NT * NE), tiny(8), tiny(NE)
                v = V.run(vcopy, lg, bank[:, 0:NT * NE], after=[m])
                pool_a.give(bank, v)
                for t in range(NT):
                    e8 = slice(t * NE, (t + 1) * NE)
                    V.run(nc.vector.max, top[:, e8], lg[:, e8])
                    V.run(nc.vector.max_index, idx[:, e8], top[:, e8], lg[:, e8])
                    V.run(vcopy, idf[:, e8], idx[:, e8])
                    v = V.run(tt, w12[:, 0:1], top[:, t * NE + 1:t * NE + 2], top[:, t * NE:t * NE + 1], ALU.subtract)
                    s = S.run(act, w12[:, 1:2], w12[:, 0:1], ACT.Exp, after=[v])
                    V.run(ts, w12[:, 2:3], w12[:, 1:2], 1.0, None, ALU.add, after=[s])
                    V.run(nc.vector.reciprocal, w12[:, 3:4], w12[:, 2:3])
                    V.run(tt, w12[:, 4:5], w12[:, 3:4], w12[:, 1:2], ALU.mult)
                    V.run(ts, gate8[:, e8], const("iota8"), idf[:, t * NE:t * NE + 1], w12[:, 3:4],
                          ALU.is_equal, ALU.mult)
                    V.run(ts, g8b, const("iota8"), idf[:, t * NE + 1:t * NE + 2], w12[:, 4:5], ALU.is_equal, ALU.mult)
                    V.run(tt, gate8[:, e8], gate8[:, e8], g8b, ALU.add)
                tap("gate8", gate8)
                for e in range(NE):
                    ys, ym = feed_forward(h3, T, a["moe_w1"][0, e], a["moe_w3"][0, e], a["moe_w2"][0, e], hm,
                                          pool_a, pool_y)
                    for i, (bank, _) in enumerate(ys):
                        t, hf = divmod(i, 2)
                        xo = x3[:, t, hf * BANK:(hf + 1) * BANK]
                        v = V.run(stt, xo, bank[:, :], gate8[:, t * NE + e:t * NE + e + 1], xo, ALU.mult, ALU.add,
                                  after=[ym], own=(i == 0))
                        pool_y.give(bank, v)
            tap(f"xffn{l}", x3)
            join()
            pool.free = [(b, ()) for b in banks]

        fg = scratch[:, 0:D]
        rm = S.dma(nc.scalar.dma_start, fg, a["rows2"][0:1, 0:D].broadcast_to([P, D]), s_rows)
        rms(x3, xn3)
        v = V.run(tt, x3, xn3, fg.unsqueeze(1).broadcast_to([P, NT, D]), ALU.mult, after=[rm])
        tap("first", x3)
        join()

        at[0] = NT * MIX
        mod = region(MOD)
        cbc = region(KD * P)
        cs_, sn_, ang = region(T), region(T), region(T)
        qraw, qrot = region(6 * T), region(6 * T)
        vtok = region(NT * KVH * HD)
        grow2 = region(D)
        m3 = mod.rearrange("p (s d) -> p s d", s=6)
        ga = [0]

        def gregion(n):
            ga[0] += n
            assert ga[0] <= NT * NB * D
            return gates[:, ga[0] - n:ga[0]]

        prob = gregion(QH * T)
        probT = gregion(QH * T)
        utok = gregion(NT * 4 * P)
        att_tables = gregion(4 * SC + 2 * P + T)
        poolm, rot2 = att_tables[:, 0:4 * SC], att_tables[:, 4 * SC:4 * SC + P]
        causal, banded = att_tables[:, 4 * SC + P:4 * SC + 2 * P], att_tables[:, 4 * SC + 2 * P:]
        pooled = gregion(4 * T)
        mixT = xn[:, :].rearrange("p (k t) -> p k t", k=KD)

        posi = region(T).bitcast(I32)
        rm = S.dma(nc.scalar.dma_start, posi, a["positions"].broadcast_to([P, T]), s_rows)
        posf = cs_
        V.run(vcopy, posf, posi, after=[rm])
        V.run(ts, ang, posf, const("invf"), None, ALU.mult)
        TWO_PI = 2 * np.pi
        C1 = 6.28125
        C2 = float(np.float32(np.round((TWO_PI - C1) * 2 ** 20) / 2 ** 20))
        C3 = float(TWO_PI - C1 - C2)
        MAGIC = 1.5 * 2 ** 23

        def reduced(dst, shift, fn_mark=None):
            k_, r = grow2[:, 0:T], grow2[:, T:2 * T]
            V.run(ts, k_, ang, 1.0 / TWO_PI, shift / TWO_PI, ALU.mult, ALU.add)
            V.run(ts, k_, k_, MAGIC, None, ALU.add)
            V.run(ts, k_, k_, MAGIC, None, ALU.subtract)
            V.run(stt, r, k_, -C1, ang, ALU.mult, ALU.add)
            V.run(stt, r, k_, -C2, r, ALU.mult, ALU.add)
            V.run(stt, r, k_, -C3, r, ALU.mult, ALU.add)
            V.run(ts, r, r, shift, float(np.float32(np.pi)), ALU.add, ALU.min)
            v = V.run(ts, r, r, -float(np.float32(np.pi)), None, ALU.max)
            return S.run(act, dst, r, ACT.Sin, after=[v])

        s = reduced(sn_, 0.0)
        V.wait(s)
        s = reduced(cs_, float(np.pi / 2))
        V.wait(s)
        V.run(ts, sn_, sn_, const("rotrow"), None, ALU.mult)
        V.run(ts, cs_, cs_, const("rotrow"), const("restrow"), ALU.mult, ALU.add)
        tap("rope", cs_)
        cc = tiny(KD)
        S.run(act, cc, col("c", 0, 0, KD), ACT.Silu)
        cb_mark = V.run(vcopy, cbc.rearrange("p (k m) -> p k m", k=KD), cc.unsqueeze(2).broadcast_to([P, KD, P]),
                        after=[S.last])
        ones1 = const("ones")[0:1, 0:P]
        sink8, mx8, sm8, nb8 = tiny(QH), tiny(QH), tiny(QH), tiny(QH)
        brow = [region(BANK) for _ in range(2)]
        assert at[0] <= SCRATCH - 6 * T
        s_brow = [[sem(f"bias_row{i}_in"), 0] for i in range(2)]
        bread = [None, None]
        bn = [0]

        def bias_row(src, n):
            i = bn[0] % 2
            bn[0] += 1
            m = SP.dma(nc.sync.dma_start, brow[i][0:1, 0:n], src, s_brow[i], after=[bread[i]])
            return i, brow[i][0:1, 0:n], m

        for l in range(DEPTH):
            for c in range(MOD // BANK):
                u, w = load_cols(a["ada_w"][l], c * BANK, BANK)
                bi, br, bm = bias_row(a["ada_b"][l:l + 1, c * BANK:(c + 1) * BANK], BANK)
                bank, freed = pool.take()
                m = group(bank[:, :], [(cbc[:, k * P:(k + 1) * P], w[:, k, :]) for k in range(KD)] + [(ones1, br)],
                          after=[*freed, u.mark, bm, cb_mark])
                bread[bi] = m
                u.done(m)
                s = S.run(act, mod[:, c * BANK:(c + 1) * BANK], bank[:, :], ACT.Copy, after=[m], own=False)
                evacuated(bank, s)
            V.wait(s)
            for i, (part, pre) in enumerate(((1, True), (2, False), (4, True), (5, False))):
                rm = S.dma(nc.scalar.dma_start, grow2, a["rows2"][1 + 4 * l + i:2 + 4 * l + i, 0:D].broadcast_to([P, D]),
                           s_rows, after=[V.last])
                if pre:
                    V.run(stt, m3[:, part, :], m3[:, part, :], 1.0, grow2, ALU.add, ALU.mult, after=[rm])
                else:
                    V.run(tt, m3[:, part, :], m3[:, part, :], grow2, ALU.mult, after=[rm])
            tap(f"mod{l}", mod)

            def modulated(scale_part, shift_part):
                rms(x3, xn3, ready=[V.last])
                V.run(tt, xn3, xn3, m3[:, scale_part, :].unsqueeze(1).broadcast_to([P, NT, D]), ALU.mult)
                m = V.run(tt, xn3, xn3, m3[:, shift_part, :].unsqueeze(1).broadcast_to([P, NT, D]), ALU.add)
                return to_features(xn3, KD, h3, m)

            hm = modulated(1, 0)
            win = a["w_in2"][l]
            rm = S.dma(nc.scalar.dma_start, att_tables, a["poolm"], s_att)
            rm = S.dma(nc.scalar.dma_start, sink8, a["sinks"][l:l + 1, :].broadcast_to([P, QH]), s_att, after=[V.last])
            V.wait(rm)
            PE.wait(rm)
            qraw3, qrot3 = (z.rearrange("p (c t) -> p c t", t=T) for z in (qraw, qrot))
            u, w = load_cols(win, 0, 512)
            for i in range(4):
                bank, freed = pool.take()
                m = group(bank[:, 0:T], [(w[:, k, i * P:(i + 1) * P], h3[:, k, :]) for k in range(KD)],
                          after=[*freed, u.mark, hm])
                v = V.run(ts, qraw3[:, i, :], bank[:, 0:T], col("b_q", l, i), None, ALU.add, after=[m], own=False)
                evacuated(bank, v)
            u.done(m)
            u = Weights(wslots)
            kw = u.ap[:, 0:KD * 2 * P].rearrange("p (k n) -> p k n", k=KD)
            for j in range(2):
                for r in range(2):
                    c = 512 + j * HD
                    u.into(kw[:, :, (2 * j + r) * HD:(2 * j + r + 1) * HD],
                           win[:, c:c + HD].rearrange("(k p) n -> p k n", p=P))
            for i in range(2):
                bank, freed = pool.take()
                m = group(bank[:, 0:T], [(kw[:, k, i * P:(i + 1) * P], h3[:, k, :]) for k in range(KD)],
                          after=[*freed, u.mark])
                v = V.run(ts, qraw3[:, 4 + i, :], bank[:, 0:T], col("b_k", l, i), None, ALU.add, after=[m], own=False)
                evacuated(bank, v)
            u.done(m)
            kmark = v
            vt3 = vtok.rearrange("p (t n) -> p t n", t=NT)
            ut3 = utok.rearrange("p (t n) -> p t n", t=NT)
            for c0, n, dst in ((640, P, vt3), (768, BANK, ut3)):
                u, w = load_cols(win, c0, n)
                bi, br, bm = bias_row(a["b_in2"][l:l + 1, c0:c0 + n], n)
                for t in range(NT):
                    bank, freed = pool.take()
                    m = group(bank[:, 0:n], [(h3[:, k, t * P:(t + 1) * P], w[:, k, :]) for k in range(KD)] + [(ones1, br)],
                              after=[*freed, u.mark, bm])
                    s = S.run(act, dst[:, t, :], bank[:, 0:n], ACT.Copy, after=[m], own=False)
                    evacuated(bank, s)
                bread[bi] = m
                u.done(m)
            vu_mark = s
            PE.wait(kmark)
            for i in range(3):
                bank, freed = pool.take()
                m = group(bank[:, :], [(rot2, qraw[:, 2 * i * T:2 * (i + 1) * T])], after=freed)
                two = lambda z: z.unsqueeze(1).broadcast_to([P, 2, T])
                v = V.run(tt, qrot3[:, 2 * i:2 * i + 2, :], bank[:, :].rearrange("p (c t) -> p c t", c=2), two(sn_),
                          ALU.mult, after=[m])
                evacuated(bank, v)
                V.run(tt, qraw3[:, 2 * i:2 * i + 2, :], qraw3[:, 2 * i:2 * i + 2, :], two(cs_), ALU.mult)
                v = V.run(tt, qrot3[:, 2 * i:2 * i + 2, :], qrot3[:, 2 * i:2 * i + 2, :], qraw3[:, 2 * i:2 * i + 2, :],
                          ALU.add)
            tap(f"qrot{l}", qrot)
            PE.wait(v)
            u = Weights(wslots)
            pw = u.ap[:, 0:4 * P].rearrange("p (g n) -> p g n", g=4)
            u.into(pw, a["pool_w"][l].rearrange("g p n -> p g n"))
            pm3 = poolm.rearrange("p (g n) -> p g n", g=4)
            PE.wait(vu_mark)
            for g in range(4):
                bank, freed = pool.take()
                PE.wait(*freed)
                group(bank[:, 0:P], [(ut3[:, 0, g * P:(g + 1) * P], pm3[:, g, 0:P])])
                m = group(bank[:, P:T], [(ut3[:, 0, g * P:(g + 1) * P], pm3[:, g, P:T]),
                                         (ut3[:, 1, g * P:(g + 1) * P], pm3[:, g, T:SC])])
                s = S.run(act, pooled[:, g * T:(g + 1) * T], bank[:, 0:T], ACT.Copy, after=[m], own=False)
                evacuated(bank, s)
                bank, freed = pool.take()
                m = group(bank[:, 0:T], [(pw[:, g, :], pooled[:, g * T:(g + 1) * T])], after=[*freed, u.mark, s])
                v = V.run(ts, mixT[:, 4 + g, :], bank[:, 0:T], col("pool_scale", l, g), None, ALU.mult, after=[m], own=False)
                evacuated(bank, v)
            u.done(m)
            pr3 = prob.rearrange("p (h n) -> p h n", h=QH)
            pT3 = probT.rearrange("p (h n) -> p h n", h=QH)
            pv = None
            for t in range(NT):
                nk = (t + 1) * P
                for h4 in range(QH // 4):
                    for odd in range(2):
                        bank, freed = pool.take()
                        PE.wait(*freed)
                        rows = slice(odd * HD, (odd + 1) * HD)
                        for j in range(2):
                            m = PE.run(mm, bank[:, j * T:j * T + nk], qrot3[rows, 2 * h4 + j, t * P:(t + 1) * P],
                                       qrot3[rows, 4 + h4, 0:nk], start=True, stop=True, mark=(j == 1))
                        b3 = bank[:, :].rearrange("p (j n) -> p j n", j=2)[:, :, 0:nk]
                        v = V.run(stt, pr3[:, 4 * h4 + odd:4 * h4 + odd + 3:2, 0:nk], b3, HD ** -0.5,
                                  (banded[:, 0:nk] if t else causal).unsqueeze(1).broadcast_to([P, 2, nk]),
                                  ALU.mult, ALU.add, after=[m, pv], own=False)
                        evacuated(bank, v)
                V.run(nc.vector.tensor_reduce, mx8, pr3[:, :, 0:nk], AXX, ALU.max)
                V.run(tt, mx8, mx8, sink8, ALU.max)
                v = V.run(ts, nb8, mx8, -1.0, None, ALU.mult)
                for h in range(QH):
                    s = S.run(act, pr3[:, h, 0:nk], pr3[:, h, 0:nk], ACT.Exp, bias=nb8[:, h:h + 1],
                              accum_out=sm8[:, h:h + 1], after=[v], own=False)
                v = V.run(tt, mx8, sink8, mx8, ALU.subtract)
                s = S.run(act, mx8, mx8, ACT.Exp, after=[v])
                V.run(tt, sm8, sm8, mx8, ALU.add, after=[s])
                rden = V.run(nc.vector.reciprocal, sm8, sm8)
                for h2 in range(QH // 2):
                    bank, freed = pool.take()
                    PE.wait(*freed, s)
                    for j in range(2):
                        for kt in range(t + 1):
                            m = PE.run(nc.tensor.transpose, bank[:, j * T + kt * P:j * T + (kt + 1) * P],
                                       pr3[:, 2 * h2 + j, kt * P:(kt + 1) * P], ident, mark=(j == 1 and kt == t))
                    b3 = bank[:, :].rearrange("p (j n) -> p j n", j=2)[:, :, 0:nk]
                    v = V.run(vcopy, pT3[:, 2 * h2:2 * h2 + 2, 0:nk], b3, after=[m, pv], own=False)
                    evacuated(bank, v)
                pv = m
                bank, freed = pool.take()
                PE.wait(*freed, v)
                for h in range(QH):
                    kv = slice((h // 4) * HD, (h // 4 + 1) * HD)
                    m = group(bank[:, h * HD:(h + 1) * HD],
                              [(pT3[:, h, kt * P:(kt + 1) * P], vt3[:, kt, kv]) for kt in range(t + 1)])
                pv = m
                o2 = obuf
                v = V.run(tt, o2.rearrange("p (h n) -> p h n", h=QH), bank[:, :].rearrange("p (h n) -> p h n", h=QH),
                          sm8.unsqueeze(2).broadcast_to([P, QH, HD]), ALU.mult, after=[m, rden])
                evacuated(bank, v)
                bank, freed = pool.take()
                PE.wait(*freed, v)
                for c in range(4):
                    m = PE.run(nc.tensor.transpose, bank[:, c * P:(c + 1) * P], obuf[:, c * P:(c + 1) * P], ident,
                               mark=(c == 3))
                v = V.run(vcopy, mixT[:, 0:4, t * P:(t + 1) * P], bank[:, :].rearrange("p (c n) -> p c n", c=4),
                          after=[m])
                evacuated(bank, v)
            tap(f"mixT{l}", mixT)
            join()
            for i in range(len(dslots.free)):
                dslots.free[i] = (dslots.free[i][0], (V.last, PE.last))

            def add_normed(ysrc, gate_part, after):
                for t, hf, bank in ysrc:
                    s = S.run(act, xn3[:, t, hf * BANK:(hf + 1) * BANK], bank[:, :], ACT.Copy, after=after, own=False)
                sqs = scratch_sq
                for t in range(NT):
                    m = S.run(act, sqs[:, t * D:(t + 1) * D], xn3[:, t, :], ACT.Square, accum_out=stat[:, t:t + 1])
                V.wait(inverse_root(stat[:, 4:6], stat[:, 0:2], D, m))
                for t in range(NT):
                    V.run(stt, xn3[:, t, :], xn3[:, t, :], stat[:, 4 + t:5 + t], m3[:, gate_part, :], ALU.mult, ALU.mult)
                V.run(tt, x3, x3, xn3, ALU.add)
                return V.last

            scratch_sq = hT[:, :]
            ysrc = []
            for hf in range(2):
                u, w = load_cols(a["w_out2"][l], hf * BANK, BANK)
                for t in range(NT):
                    bank, freed = pool.take()
                    m = group(bank[:, :], [(mixT[:, k, t * P:(t + 1) * P], w[:, k, :]) for k in range(KD)],
                              after=[*freed, u.mark])
                    ysrc.append((t, hf, bank))
                u.done(m)
            add_normed(ysrc, 2, [m])
            tap(f"x2mix{l}", x3)
            join()
            hm = modulated(4, 3)
            join()
            pool_y, pool_a = Slots(banks[0:4]), Slots(banks[4:8])
            ys, ym = feed_forward(h3, T, a["w_gate"][l], a["w_up"][l], a["w_down"][l], hm, pool_a, pool_y)
            add_normed([(i // 2, i % 2, b) for i, (b, _) in enumerate(ys)], 5, [ym])
            join()
            tap(f"x2ffn{l}", x3)
            pool.free = [(b, ()) for b in banks]

        om = SP.dma(nc.sync.dma_start, out.rearrange("o (t p) d -> p (o t) d", p=P), x3, s_out, after=[V.last])
        SP.wait(om)

        with nc.Block() as block:
            @block.sync
            def _(_e):
                SP.play()

            @block.scalar
            def _(_e):
                S.play()

            @block.vector
            def _(_e):
                V.play()

            @block.tensor
            def _(_e):
                PE.play()

            @block.gpsimd
            def _(_e):
                G.play()


CONST, COLUMN = {}, {}


def constant_tables():
    parts, at = [], 0
    p = np.arange(P)

    def add(name, table):
        nonlocal at
        table = np.broadcast_to(np.asarray(table, np.float32), (P, np.shape(table)[-1]))
        CONST[name] = (at, table.shape[1])
        at += table.shape[1]
        parts.append(table)

    add("ident", np.eye(P))
    half = HD // 2
    rot = np.zeros((P, P))
    for m in range(P):
        if m % HD < half:
            rot[m + half, m] = -1.0
        else:
            rot[m - half, m] = 1.0
    add("rot", rot)
    inv = (np.float32(10000.0) ** (-np.arange(half, dtype=np.float32) / np.float32(half))).astype(np.float32)
    ang = np.arange(T, dtype=np.float32)[None, :] * inv[p % half][:, None]
    add("cos", np.cos(ang.astype(np.float64)))
    add("sin", np.sin(ang.astype(np.float64)))
    i = np.concatenate([np.arange(T), np.arange(P, T)])
    j = np.concatenate([np.zeros(T), np.full(P, P)])[None, :] + p[:, None]
    lag = i[None, :] - j
    tri = lag >= 0
    log_gamma = np.log1p(-np.exp2(-5.0 - np.arange(NH)))
    add("decay", np.concatenate([np.where(tri, np.exp(np.maximum(lag, 0) * g), 0) * HD ** -0.5 for g in log_gamma], 1))
    add("tri", tri)
    add("ones", np.ones((P, T)))
    add("power", np.full((P, 1), -0.5))
    add("iota8", np.arange(NE)[None, :])
    hr = ROT // 2
    rot2 = np.zeros((P, P))
    for m in range(P):
        r = m % HD
        if r < hr:
            rot2[m + hr, m] = -1.0
        elif r < ROT:
            rot2[m - hr, m] = 1.0
    inv2 = (np.float32(500000.0) ** (-np.arange(0, ROT, 2, dtype=np.float32) / np.float32(ROT))).astype(np.float32)
    add("invf", np.where(p % HD < ROT, inv2[(p % HD) % hr], 0.0)[:, None])
    add("rotrow", (p % HD < ROT).astype(np.float32)[:, None])
    add("restrow", (p % HD >= ROT).astype(np.float32)[:, None])
    q = p[:, None]
    d = q + P - np.arange(T)[None, :]
    k_, q_ = p[:, None], p[None, :]
    masks = [(k_ // (2 * b) == q_ // (2 * b)) & (k_ % (2 * b) < b) & (q_ % (2 * b) >= b) for b in GLA_LEVELS]
    masks.append(k_ == q_)
    causal = np.where(np.arange(P)[None, :] <= q, 0.0, -1e30)
    band = np.where((d >= 0) & (d < P), 0.0, -1e30)
    pm = []
    for w in WINDOWS:
        avg = np.where((lag >= 0) & (lag < w), 1.0 / np.minimum(i + 1, w)[None, :], 0.0) - (lag == 0)
        pm.append(avg)
    return (np.concatenate(parts, 1).astype(np.float32), np.concatenate(masks, 1).astype(np.int32),
            np.concatenate(pm + [rot2, causal, band], 1).astype(np.float32))


def column_parameters(v):
    parts, at = [], 0

    def add(name, l, table):
        nonlocal at
        if table.shape[0] < P:
            table = np.concatenate([table, np.zeros((P - table.shape[0], table.shape[1]), table.dtype)], 0)
        COLUMN[(name, l)] = at
        at += table.shape[1]
        parts.append(table)

    chunks = lambda r: r.reshape(-1, P).T
    for l in range(DEPTH):
        add("mix_g", l, chunks(v["mix_norm_g"][l]))
        add("ffn_g", l, chunks(v["ffn_norm_g"][l]))
        add("ssd_conv_w", l, chunks(v["ssd_conv_w"][l].reshape(-1)))
        add("ssd_conv_b", l, chunks(v["ssd_conv_b"][l]))
        add("ml_conv_w", l, chunks(v["ml_conv_w"][l].reshape(-1)))
        add("ml_conv_b", l, chunks(v["ml_conv_b"][l]))
        add("b_alpha", l, chunks(v["gla_b_alpha"][l]))
        add("w_alpha", l, v["gla_w_alpha"][l])
        for name, key in (("dt_bias", "ssd_dt_bias"), ("a_log", "ssd_a_log"), ("b_i", "ml_b_i"), ("b_f", "ml_b_f")):
            add(name, l, v[key][l].reshape(NH, 1))
        add("b_q", l, chunks(v["b_in_2"][l, 0:512]))
        k = v["b_in_2"][l, 512:640].reshape(2, HD)
        add("b_k", l, np.concatenate([k, k], 1).T)
        add("pool_scale", l, chunks(v["pool_scale_2"][l]))
    add("router", 0, v["router_w"][0].reshape(KD, P, NE).transpose(1, 0, 2).reshape(P, KD * NE))
    add("c", 0, chunks(v["c_2"][0]))
    return np.concatenate(parts, 1)


def arrange(v):
    const, lmask, poolm = constant_tables()
    rows1 = np.concatenate([v["ret_norm_g"], v["ssd_norm_g"], v["gla_norm_g"], v["ml_norm_g"], v["ssd_d"]], 1)
    rows2 = [v["final_norm_g"]]
    for l in range(DEPTH):
        rows2 += [v[n][l] for n in ("g_pre_mix_2", "g_post_mix_2", "g_pre_ffn_2", "g_post_ffn_2")]
    arrays = {
        "const": const, "lmask": lmask, "poolm": poolm, "cols": column_parameters(v), "rows1": rows1,
        "rows2": np.stack(rows2), "x": v["x"], "positions": v["positions_2"], "ada_w": v["ada_w_2"],
        "ada_b": v["ada_b_2"], "w_in2": v["w_in_2"], "b_in2": v["b_in_2"], "sinks": v["sinks_2"],
        "pool_w": v["pool_w_2"], "w_out2": v["w_out_2"], "w_gate": v["w_gate_2"], "w_up": v["w_up_2"],
        "w_down": v["w_down_2"],
    }
    for n in ("w_in", "w_branch", "w_out", "ffn_w1", "ffn_w3", "ffn_w2", "moe_w1", "moe_w3", "moe_w2"):
        arrays[n] = v[n]
    return {n: np.ascontiguousarray(z) for n, z in arrays.items()}


def kernel(**inputs):
    import concourse.bacc as bacc
    from concourse.bass_utils import run_bass_kernel_spmd

    arrays = arrange({n: np.asarray(z) for n, z in inputs.items()})
    nc = bacc.Bacc("TRN2", target_bir_lowering=False, num_devices=1)
    aps = {n: nc.dram_tensor("in_" + n, z.shape, mybir.dt.from_np(z.dtype), kind="ExternalInput").ap()
           for n, z in arrays.items()}
    out = nc.dram_tensor("out_y", (1, T, D), F32, kind="ExternalOutput").ap()
    program(nc, aps, out)
    r = run_bass_kernel_spmd(nc, [{"in_" + n: z for n, z in arrays.items()}], core_ids=[0])
    return r.results[0]["out_y"]
```

```python
from contextlib import ExitStack

import numpy as np
import concourse.bass as bass
from concourse import mybir

F32 = mybir.dt.float32
I32 = mybir.dt.int32
U8 = mybir.dt.uint8
F32R = mybir.dt.float32r
ALU = mybir.AluOpType
ACT = mybir.ActivationFunctionType
AXX = mybir.AxisListType.X

P = 128
T = 256
NT = T // P
D = 1024
KD = D // P
DEPTH = 2
MIX = D // 4
NB = 4
NH = 4
HD = MIX // NH
EPS = 1e-6
FF = 2816
NFF = FF // P
NE = 8
BANK = 512
SC = T + P
GLA_DK = MIX // (2 * NH)
GLA_TAU = 16.0
CONV_K = 4
NSX, NMQ = 6, 4
PAD = CONV_K - 1
MOD = 6 * D
QH, KVH = 8, 2
ROT = HD // 4
WINDOWS = (2, 4, 8, 16)
GLA_LEVELS = (64, 32, 16, 8, 4, 2, 1)

COLS = {}
_at = 0
for _name, _n in (("rq", 256), ("rk", 256), ("rv", 256), ("rg", 256), ("sz", 256), ("sxbc", 768),
                  ("sdt", 4), ("gq", 128), ("gk", 128), ("gv", 256), ("gr", 256), ("ga", 16),
                  ("mqk", 512), ("mv", 256), ("mo", 256), ("mi", 4), ("mf", 4), ("mgate", 4096)):
    COLS[_name] = _at
    _at += _n

PIECE = 2048
NRAW = 5
NSPLIT = 3
AHEAD = 2


class Mark:

    def __init__(self, sem, value):
        self.sem, self.value = sem, value


class Either:

    def __init__(self, flag, limit, ways):
        self.flag, self.limit, self.ways = flag, limit, ways


class Queue:

    def __init__(self, sem, engine, chained):
        self.sem, self.engine, self.wait_ge, self.chained = sem, engine, engine.wait_ge, chained
        self.count, self.steps, self.seen, self.last = 0, [], {}, None

    def wait(self, *marks):
        for m in marks:
            if m is not None and self.seen.get(m.sem, 0) < m.value:
                self.seen[m.sem] = m.value
                self.steps.append((self.wait_ge, (m.sem, m.value), {}, None, 0))

    def run(self, op, *args, after=(), mark=True, own=None, **kw):
        if self.chained if own is None else own:
            self.wait(self.last)
        self.wait(*after)
        if not mark:
            self.steps.append((op, args, kw, None, 0))
            return None
        self.count += 1
        self.steps.append((op, args, kw, self.sem, 1))
        self.last = Mark(self.sem, self.count)
        return self.last

    def dma(self, op, out, in_, sem, after=()):
        self.wait(*after)
        sem[1] += 16
        self.steps.append((op, (out, in_), {}, sem[0], 16))
        return Mark(sem[0], sem[1])

    def play(self, steps=None):
        for step in self.steps if steps is None else steps:
            if isinstance(step, Either):
                value = self.engine.value_load(step.flag)
                with self.engine.If(value < step.limit):
                    self.play(step.ways[0])
                with self.engine.Else():
                    self.play(step.ways[1])
                continue
            op, args, kw, sem, by = step
            i = op(*args, **kw)
            if sem is not None:
                i.then_inc(sem, by)


class Slots:

    def __init__(self, items):
        self.free = [(item, ()) for item in items]

    def take(self):
        return self.free.pop(0)

    def give(self, item, *marks):
        self.free.append((item, marks))


def program(nc, a, out, taps=None):
    with ExitStack() as ctx:
        def sb(stage, name, n, dt=F32):
            return stage.enter_context(nc.sbuf_tensor(name, [P, n], dt))[:, :]

        def sem(name):
            return ctx.enter_context(nc.semaphore(name))

        PE = Queue(sem("tensor_done"), nc.tensor, False)
        S = Queue(sem("scalar_done"), nc.scalar, True)
        V = Queue(sem("vector_done"), nc.vector, True)
        G = Queue(sem("gpsimd_done"), nc.gpsimd, True)
        SP = Queue(sem("sync_done"), nc.sync, False)
        tt, ts, stt = nc.vector.tensor_tensor, nc.vector.tensor_scalar, nc.vector.scalar_tensor_tensor
        vcopy, act, mm = nc.vector.tensor_copy, nc.scalar.activation, nc.tensor.matmul
        scan, reduce = nc.vector.tensor_tensor_scan, nc.vector.tensor_reduce
        tok3 = lambda ap: ap.rearrange("p (t n) -> p t n", t=NT)
        heads = lambda ap: ap.rearrange("p (t h n) -> p t h n", t=NT, h=NH)
        tiles = lambda ap: ap.rearrange("p (c t) -> p c t", t=T)
        rep = lambda ap, n: ap.unsqueeze(1).broadcast_to([P, n, ap.shape[-1]])

        x = sb(ctx, "x", NT * D)
        xn = sb(ctx, "xn", NT * D)
        hThi = sb(ctx, "hThi", KD * T, F32R)
        hTlo = sb(ctx, "hTlo", KD * T, F32R)
        raw = sb(ctx, "raw", NRAW * PIECE)
        whi = sb(ctx, "whi", NSPLIT * PIECE, F32R)
        wlo = sb(ctx, "wlo", NSPLIT * PIECE, F32R)
        cst = sb(ctx, "cst", a["const"].shape[1])
        lmask = sb(ctx, "lmask", a["lmask"].shape[1], U8)
        cols = sb(ctx, "cols", a["cols"].shape[1])
        rows_t = sb(ctx, "rows_t", 4 * MIX + NH)
        small = sb(ctx, "small", 420)
        banks = [ctx.enter_context(nc.psum_tensor(f"bank{i}", [P, BANK], F32)) for i in range(8)]
        x3, xn3 = tok3(x), tok3(xn)
        hi3, lo3 = tiles(hThi), tiles(hTlo)
        used = [0]

        def tiny(n):
            used[0] += n
            assert used[0] <= 420
            return small[:, used[0] - n:used[0]]

        def const(name):
            o, n = CONST[name]
            return cst[:, o:o + n]

        def col(name, l, i=0, n=1, rows=P):
            o = COLUMN[(name, l)] + i
            return cols[0:rows, o:o + n]

        plan = []

        def chunk_rows(w, k0, nk, c0, n):
            return w[k0 * P:(k0 + nk) * P, c0:c0 + n].rearrange("(k p) n -> p k n", p=P)

        def plan_half(key, w, c0, lo_on="V"):
            for k0 in (0, 4):
                plan.append((key, lo_on, PIECE, [(lambda ap: ap.rearrange("p (k n) -> p k n", k=4),
                                                  chunk_rows(w, k0, 4, c0, BANK))]))

        def plan_full(key, w, c0, lo_on="V"):
            plan.append((key, lo_on, PIECE, [(lambda ap: ap.rearrange("p (k n) -> p k n", k=KD),
                                              chunk_rows(w, 0, KD, c0, 2 * P))]))

        def plan_rows(key, w, r0, lo_on="V"):
            plan.append((key, lo_on, PIECE, [(lambda ap: ap.rearrange("p (c n) -> p c n", c=2),
                                              w[r0:r0 + 2 * P, :].rearrange("(c p) n -> p c n", p=P))]))

        def plan_strips(key, w, strips):
            n, loads, at = sum(m for _, m in strips), [], 0
            for c0, m in strips:
                loads.append((lambda ap, at=at, m=m: ap[:, 0:KD * n].rearrange("p (k n) -> p k n", k=KD)[:, :, at:at + m],
                              chunk_rows(w, 0, KD, c0, m)))
                at += m
            plan.append((key, "V", KD * n, loads))

        def plan_ff(key, *nets):
            todo = [(net, c) for net in nets for c in range(FF // (2 * P))]
            for i in range(len(todo) + 2):
                if i < len(todo):
                    (w1, w3, _), c = todo[i]
                    for k0 in (0, 4):
                        view = lambda ap, w: ap.rearrange("p (k w n) -> p k w n", k=4, w=2)[:, :, w, :]
                        plan.append((key, "V", PIECE, [
                            (lambda ap, view=view: view(ap, 0), chunk_rows(w1, k0, 4, c * 2 * P, 2 * P)),
                            (lambda ap, view=view: view(ap, 1), chunk_rows(w3, k0, 4, c * 2 * P, 2 * P))]))
                if i >= 2:
                    (_, _, w2), c = todo[i - 2]
                    plan_rows(key, w2, c * 2 * P)

        raws = Slots([(raw[:, i * PIECE:(i + 1) * PIECE], [sem(f"piece{i}_in"), 0]) for i in range(NRAW)])
        splits = Slots([(whi[:, i * PIECE:(i + 1) * PIECE], wlo[:, i * PIECE:(i + 1) * PIECE]) for i in range(NSPLIT)])
        ready, counts = [], {"split": 0, "used": 0}

        def split_next():
            key, lo_on, n, loads = plan[counts["split"]]
            counts["split"] += 1
            (dst, cell), freed = raws.take()
            for view, src in loads:
                m = SP.dma(nc.sync.dma_start, view(dst), src, cell, after=freed)
            (hi, lo), parted = splits.take()
            s = S.run(act, hi[:, 0:n], dst[:, 0:n], ACT.Copy, after=[m, *parted], own=False)
            q, sub = (V, tt) if lo_on == "V" else (G, nc.gpsimd.tensor_tensor)
            v = q.run(sub, lo[:, 0:n], dst[:, 0:n], hi[:, 0:n].bitcast(F32), ALU.subtract, after=[s, m, *parted],
                      own=False)
            raws.give((dst, cell), v)
            ready.append((key, (hi, lo), v))

        def piece(key):
            counts["used"] += 1
            while counts["split"] < min(counts["used"] + AHEAD, len(plan)):
                split_next()
            k, parts, m = ready.pop(0)
            assert k == key, (k, key)
            PE.wait(m)
            return parts

        def finished(parts, m):
            splits.give(parts, m)

        pool = Slots(banks)

        def group(dst, pairs, after=(), start=True, stop=True):
            PE.wait(*after)
            m = None
            for i, (l_, r_) in enumerate(pairs):
                last = i == len(pairs) - 1
                m = PE.run(mm, dst, l_, r_, start=start and i == 0, stop=stop and last, mark=last)
            return m

        def product(dst, quads, start=True, stop=True):
            return group(dst, [z for (lh, ll), (rh, rl) in quads for z in ((lh, rh), (lh, rl), (ll, rh))],
                         start=start, stop=stop)

        s_const, s_rows, s_x, s_out, s_att = ([sem(n), 0] for n in (
            "constants_in", "row_parameters_in", "x_in", "result_out", "attention_tables_in"))
        x_in = SP.dma(nc.sync.dma_start, x3, a["x"].rearrange("o (t p) d -> p (o t) d", p=P), s_x)
        cm = S.dma(nc.scalar.dma_start, cst, a["const"], s_const)
        cm = S.dma(nc.scalar.dma_start, cols, a["cols"], s_const)
        wide = xn[:, 0:lmask.shape[1]].bitcast(I32)
        cm = S.dma(nc.scalar.dma_start, wide, a["lmask"], s_const)
        for q in (PE, V, S, G):
            q.wait(cm)
        S.wait(V.run(vcopy, lmask, wide))
        V.wait(x_in)
        S.wait(x_in)
        ident = const("ident")
        stat = tiny(16)

        def marks():
            return [q.last for q in (PE, V, S, G)]

        def join():
            lasts = marks()
            for q in (PE, V, S, G):
                q.wait(*lasts)

        def tap(name, ap):
            if taps is not None and name in taps:
                join()
                SP.wait(*marks())
                m = SP.dma(nc.sync.dma_start, taps[name], ap, s_out)
                SP.wait(m)
                for q in (PE, V, S, G):
                    q.wait(m)

        def inverse_root(dst, sums, n, ready_):
            G.run(nc.gpsimd.tensor_scalar, dst, sums, 1.0 / n, EPS, ALU.mult, ALU.add, after=[ready_])
            return G.run(nc.gpsimd.tensor_tensor, dst, dst, const("power").broadcast_to(list(dst.shape)), ALU.pow)

        def rms(src3, dst3, after=()):
            for t in range(NT):
                m = S.run(act, dst3[:, t, :], src3[:, t, :], ACT.Square, accum_out=stat[:, t:t + 1], after=after)
            V.wait(inverse_root(stat[:, 4:6], stat[:, 0:2], D, m))
            for t in range(NT):
                m = V.run(ts, dst3[:, t, :], src3[:, t, :], stat[:, 4 + t:5 + t], None, ALU.mult, own=(t == 0))
            return m

        def to_parts(hi, lo, src, m, scale=None):
            s = S.run(act, hi, src, ACT.Copy, after=[m], own=False, **({} if scale is None else {"scale": scale}))
            if scale is None:
                return V.run(tt, lo, src, hi.bitcast(F32), ALU.subtract, after=[m, s], own=False)
            return V.run(stt, lo, src, scale, hi.bitcast(F32), ALU.mult, ALU.subtract, after=[m, s], own=False)

        def to_features(src3, m, scale=None, reads=()):
            S.wait(*reads)
            V.wait(*reads)
            for k in range(0, KD, 2):
                bank, freed = pool.take()
                PE.wait(*freed, m)
                for j in range(2):
                    for t in range(NT):
                        c = (2 * j + t) * P
                        p_ = PE.run(nc.tensor.transpose, bank[:, c:c + P], src3[:, t, (k + j) * P:(k + j + 1) * P],
                                    ident, mark=(j == 1 and t == NT - 1))
                if scale is None or isinstance(scale, float):
                    v = to_parts(hi3[:, k:k + 2, :], lo3[:, k:k + 2, :], tiles(bank[:, :]), p_, scale)
                else:
                    for j in range(2):
                        s = S.run(act, hi3[:, k + j, :], bank[:, j * T:(j + 1) * T], ACT.Copy, scale=scale(k + j),
                                  after=[p_], own=False)
                    for j in range(2):
                        v = V.run(stt, lo3[:, k + j, :], bank[:, j * T:(j + 1) * T], scale(k + j),
                                  hi3[:, k + j, :].bitcast(F32), ALU.mult, ALU.subtract, after=[s], own=False)
                pool.give(bank, v)
            return v

        def stat_tokens(k, t):
            return hi3[:, k, t * P:(t + 1) * P], lo3[:, k, t * P:(t + 1) * P]

        def project_tokens(key, hm):
            out_ = []
            for half in range(2):
                parts = piece(key)
                w = [z.rearrange("p (k n) -> p k n", k=4) for z in parts]
                PE.wait(hm)
                for t in range(NT):
                    if half == 0:
                        bank, freed = pool.take()
                        PE.wait(*freed)
                        out_.append([bank, None])
                    out_[t][1] = product(out_[t][0][:, :], [(stat_tokens(4 * half + k, t), (w[0][:, k], w[1][:, k]))
                                                            for k in range(4)], start=half == 0, stop=half == 1)
                finished(parts, out_[-1][1])
            return out_

        def project_features(w, c, hm, bank, at, rows=P):
            PE.wait(hm)
            return product(bank[0:rows, at:at + T], [((w[0][:, k, c:c + rows], w[1][:, k, c:c + rows]),
                                                      (hi3[:, k, :], lo3[:, k, :])) for k in range(KD)])

        def full(parts, n=2 * P):
            return [z[:, 0:KD * n].rearrange("p (k n) -> p k n", k=KD) for z in parts]

        def feed_forward(stage, key, nt, nets, pool_a, pool_y, tag="", between=lambda: None):
            sil = Slots([sb(stage, f"silu{i}_{key}{tag}", nt * 2 * P) for i in range(2)])
            gts = Slots([sb(stage, f"gated{i}_{key}{tag}", nt * 2 * P) for i in range(2)])
            gparts = Slots([(sb(stage, f"gatedThi{i}_{key}{tag}", 2 * nt * P, F32R),
                             sb(stage, f"gatedTlo{i}_{key}{tag}", 2 * nt * P, F32R)) for i in range(2)])
            nchunk = FF // (2 * P)
            todo = [(net, c) for net in nets for c in range(nchunk)]
            gated, turned, ys = {}, {}, []
            for i in range(len(todo) + 2):
                if i < len(todo):
                    (tokens, tokens_ready, _), c = todo[i]
                    ups = []
                    for half in range(2):
                        parts = piece(key)
                        w = [z.rearrange("p (k n) -> p k n", k=4) for z in parts]
                        if c == 0:
                            PE.wait(tokens_ready())
                        for t in range(nt):
                            if half == 0:
                                bank, freed = pool_a.take()
                                PE.wait(*freed)
                                ups.append([bank, None])
                            ups[t][1] = product(ups[t][0][:, :], [(tokens(4 * half + k, t), (w[0][:, k], w[1][:, k]))
                                                                  for k in range(4)], start=half == 0, stop=half == 1)
                        finished(parts, ups[-1][1])
                    sg, f1 = sil.take()
                    gt, f2 = gts.take()
                    S.wait(*f1)
                    V.wait(*f2)
                    for t, (bank, m) in enumerate(ups):
                        cs = slice(t * 2 * P, (t + 1) * 2 * P)
                        s = S.run(act, sg[:, cs], bank[:, 0:2 * P], ACT.Silu, after=[m], own=False)
                        v = V.run(tt, gt[:, cs], sg[:, cs], bank[:, 2 * P:4 * P], ALU.mult, after=[s, m], own=False)
                        pool_a.give(bank, v)
                    sil.give(sg, v)
                    gated[i] = (gt, v)
                if i >= 2:
                    (_, _, finish), c = todo[i - 2]
                    if c == 0:
                        ys = [(t, hf, *pool_y.take()) for t in range(nt) for hf in range(2)]
                        PE.wait(*[m for y in ys for m in y[3]])
                    parts = piece(key)
                    w = [z.rearrange("p (c n) -> p c n", c=2) for z in parts]
                    g_parts, gm = turned.pop(i - 2)
                    PE.wait(gm)
                    g3 = [z.rearrange("p (c t) -> p c t", c=2) for z in g_parts]
                    for t, hf, bank, _ in ys:
                        ts_, cs = slice(t * P, (t + 1) * P), slice(hf * BANK, (hf + 1) * BANK)
                        m = product(bank[:, :], [((g3[0][:, j, ts_], g3[1][:, j, ts_]), (w[0][:, j, cs], w[1][:, j, cs]))
                                                 for j in range(2)], start=c == 0, stop=c == nchunk - 1)
                    finished(parts, m)
                    gparts.give(g_parts, m)
                    if c == nchunk - 1:
                        finish([(t, hf, bank) for t, hf, bank, _ in ys], m)
                if 1 <= i <= len(todo):
                    gt, v = gated.pop(i - 1)
                    g_parts, freed = gparts.take()
                    bank, bank_freed = pool_a.take()
                    PE.wait(v, *bank_freed)
                    for j in range(2):
                        for t in range(nt):
                            m = PE.run(nc.tensor.transpose, bank[:, (j * nt + t) * P:(j * nt + t + 1) * P],
                                       gt[:, t * 2 * P + j * P:t * 2 * P + (j + 1) * P], ident,
                                       mark=(j == 1 and t == nt - 1))
                    gts.give(gt, m)
                    S.wait(*freed)
                    V.wait(*freed)
                    v = to_parts(*g_parts, bank[:, 0:2 * nt * P], m)
                    pool_a.give(bank, v)
                    turned[i - 1] = (g_parts, v)
                between()

        def either(flag, limit, flag_ready, ways):
            queues = (PE, S, V, G, SP)
            for q in queues:
                q.wait(flag_ready)
            start = [(q.steps, q.count, dict(q.seen), q.last) for q in queues]
            rings = [(r_, list(r_.free)) for r_ in (raws, splits)]
            cells = [item[1] for item, _ in raws.free]
            cell_counts = [c_[1] for c_ in cells]
            ready_before, counts_before = list(ready), dict(counts)
            ends = []
            for way in ways:
                for q, (_, count, seen, last) in zip(queues, start):
                    q.steps, q.count, q.seen, q.last = [], count, dict(seen), last
                for r_, free in rings:
                    r_.free = list(free)
                for c_, n in zip(cells, cell_counts):
                    c_[1] = n
                ready[:] = ready_before
                counts.update(counts_before)
                way()
                join()
                ends.append(([q.steps for q in queues], [q.count for q in queues], [c_[1] for c_ in cells],
                             dict(counts)))
            assert ends[0][2:] == ends[1][2:]
            final = {}
            for i, (q, (steps, _, seen, _)) in enumerate(zip(queues, start)):
                q.count = max(end[1][i] for end in ends)
                q.last = Mark(q.sem, q.count)
                final[q.sem] = q.last
                for end in ends:
                    if q.count > end[1][i]:
                        end[0][i].append((q.engine.sem_inc, (q.sem, q.count - end[1][i]), {}, None, 0))
                q.steps, q.seen = steps + [Either(flag, limit, [end[0][i] for end in ends])], dict(seen)
            late = lambda marks_: tuple(m if m is None else final.get(m.sem, m) for m in marks_)
            for r_ in (raws, splits):
                r_.free = [(item, late(marks_)) for item, marks_ in r_.free]
            ready[:] = [(key, parts, *late([m])) for key, parts, m in ready]

        def experts(l, normed, gain):
            with ExitStack() as stage:
                hf32 = sb(stage, "router_tokens", KD * T)
                h3 = tiles(hf32)
                for k in range(0, KD, 2):
                    bank, freed = pool.take()
                    PE.wait(*freed, normed)
                    for j in range(2):
                        for t in range(NT):
                            p_ = PE.run(nc.tensor.transpose, bank[:, (2 * j + t) * P:(2 * j + t + 1) * P],
                                        xn3[:, t, (k + j) * P:(k + j + 1) * P], ident, mark=(j == 1 and t == 1))
                    for j in range(2):
                        v = V.run(ts, h3[:, k + j, :], bank[:, j * T:(j + 1) * T], gain(k + j), None, ALU.mult,
                                  after=[p_], own=False)
                    pool.give(bank, v)
                bank, freed = pool.take()
                PE.wait(*freed, v)
                for t in range(NT):
                    m = group(bank[:, t * NE:(t + 1) * NE],
                              [(h3[:, k, t * P:(t + 1) * P], col("router", 0, k * NE, NE)) for k in range(KD)])
                xhi, xlo = tok3(hThi), tok3(hTlo)
                s = S.run(act, hThi, xn, ACT.Copy, after=[normed], own=False)
                G.run(nc.gpsimd.tensor_tensor, hTlo, xn, hThi.bitcast(F32), ALU.subtract, after=[s, normed])
                lg, top, gate8, taken = tiny(NT * NE), tiny(NT * NE), tiny(NT * NE), tiny(NT * NE)
                idx = stage.enter_context(nc.sbuf_tensor("idx", [P, NT * NE], mybir.dt.uint32))
                idf, w12 = tiny(NT * NE), tiny(NT * 6)
                v = V.run(vcopy, lg, bank[:, 0:NT * NE], after=[m])
                pool.give(bank, v)
                for t in range(NT):
                    e8 = slice(t * NE, (t + 1) * NE)
                    V.run(nc.vector.max, top[:, e8], lg[:, e8])
                    V.run(nc.vector.max_index, idx[:, e8], top[:, e8], lg[:, e8])
                V.run(vcopy, idf, idx[:, :])
                w3_, top3 = (z.rearrange("p (t n) -> p t n", t=NT) for z in (w12, top))
                v = V.run(tt, w3_[:, :, 0], top3[:, :, 1], top3[:, :, 0], ALU.subtract)
                s = S.run(act, w3_[:, :, 1], w3_[:, :, 0], ACT.Exp, after=[v])
                V.run(ts, w3_[:, :, 2], w3_[:, :, 1], 1.0, None, ALU.add, after=[s])
                V.run(nc.vector.reciprocal, w3_[:, :, 3], w3_[:, :, 2])
                V.run(tt, w3_[:, :, 4], w3_[:, :, 3], w3_[:, :, 1], ALU.mult)
                for t in range(NT):
                    e8 = slice(t * NE, (t + 1) * NE)
                    V.run(ts, taken[:, e8], const("iota8"), idf[:, t * NE:t * NE + 1], None, ALU.is_equal)
                    V.run(ts, gate8[:, e8], taken[:, e8], w3_[:, t, 3:4], None, ALU.mult)
                    V.run(ts, lg[:, e8], const("iota8"), idf[:, t * NE + 1:t * NE + 2], None, ALU.is_equal)
                    V.run(stt, gate8[:, e8], lg[:, e8], w3_[:, t, 4:5], gate8[:, e8], ALU.mult, ALU.add)
                    v = V.run(tt, taken[:, e8], taken[:, e8], lg[:, e8], ALU.add)
                tri, slot_of = const("tri"), tiny(NT * NE)
                counted, most = tiny(NE), tiny(1)
                bank, freed = pool.take()
                group(bank[:, 0:NE], [(tri[:, 0:P], taken[:, 0:NE])], after=[*freed, v])
                group(bank[:, NE:2 * NE], [(tri[:, P:T], taken[:, 0:NE]), (tri[:, T:SC], taken[:, NE:2 * NE])])
                m = group(bank[0:1, 2 * NE:3 * NE], [(const("ones")[:, 0:1], taken[:, 0:NE]),
                                                     (const("ones")[:, 0:1], taken[:, NE:2 * NE])])
                V.run(reduce, most[0:1, :], bank[0:1, 2 * NE:3 * NE], AXX, ALU.max, after=[m])
                flag = stage.enter_context(nc.sbuf_tensor("most_tokens", [P, 1], I32))
                V.run(vcopy, flag[0:1, :], most[0:1, :])
                v = V.run(tt, slot_of, taken, bank[:, 0:NT * NE], ALU.mult)
                pool.give(bank, v)
                tap("gate8", gate8)
                join()
                gate = lambda t, e: gate8[:, t * NE + e:t * NE + e + 1]
                either(flag[0:1, :], P + 1, v, [lambda: sparse_experts(gate, slot_of, xhi, xlo, gain),
                                                lambda: dense_experts(gate, xn3, gain)])

        def dense_experts(gate, tokens3, gain):
            pool.free = [(b, ()) for b in banks]
            with ExitStack() as stage:
                hm = to_features(tokens3, V.last, scale=gain, reads=[PE.last])
                join()
                pool_y = Slots(banks[0:4])

                def finish(e):
                    def add_gated(ys, ym):
                        V.wait(V.last)
                        for t, hf, bank in ys:
                            xo = x3[:, t, hf * BANK:(hf + 1) * BANK]
                            v = V.run(stt, xo, bank[:, :], gate(t, e), xo, ALU.mult, ALU.add, after=[ym], own=False)
                            pool_y.give(bank, v)
                    return add_gated

                feed_forward(stage, "moe", NT, [(stat_tokens, lambda: hm, finish(e)) for e in range(NE)],
                             Slots(banks[4:8]), pool_y, tag="_dense")

        def sparse_experts(gate, slot_of, xhi, xlo, gain):
            with ExitStack() as stage:
                one = lambda name, n, dt=F32: sb(stage, name, n, dt)
                pick, put = one("pick", NT * NE * P, F32R), one("put", NE * T, F32R)
                pick4 = pick.rearrange("p (t e n) -> p t e n", t=NT, e=NE)
                put3 = put.rearrange("p (e t) -> p e t", e=NE)
                gathered = [(one(f"slots_hi{i}", KD * 2 * P, F32R), one(f"slots_lo{i}", KD * 2 * P, F32R))
                            for i in range(2)]
                yhi, ylo = one("outputs_hi", D, F32R), one("outputs_lo", D, F32R)
                pool_y, pool_a, side = Slots(banks[0:2]), Slots(banks[2:6]), Slots(banks[6:8])
                for t in range(NT):
                    v = V.run(tt, pick4[:, t], rep(const("slots"), NE),
                              slot_of[:, t * NE:(t + 1) * NE].unsqueeze(2).broadcast_to([P, NE, P]), ALU.is_equal)
                picked = v
                slots_ready, slots_read, y_read = {}, {}, [None]

                def gather(pair):
                    hi, lo = (z.rearrange("p (k n) -> p k n", k=KD) for z in gathered[pair % 2])
                    before = slots_read.get(pair - 2)
                    PE.wait(picked)
                    for k in range(0, KD, 2):
                        bank, freed = side.take()
                        PE.wait(*freed, G.last)
                        for j in range(2):
                            fs = slice((k + j) * P, (k + j + 1) * P)
                            m = group(bank[:, j * T:(j + 1) * T],
                                      [(z[:, t, fs], pick4[:, t, 2 * pair:2 * pair + 2, :])
                                       for t in range(NT) for z in (xhi, xlo)])
                        S.wait(before)
                        V.wait(before)
                        for j in range(2):
                            s = S.run(act, hi[:, k + j, :], bank[:, j * T:(j + 1) * T], ACT.Copy, scale=gain(k + j),
                                      after=[m], own=False)
                        for j in range(2):
                            v = V.run(stt, lo[:, k + j, :], bank[:, j * T:(j + 1) * T], gain(k + j),
                                      hi[:, k + j, :].bitcast(F32), ALU.mult, ALU.subtract, after=[s], own=False)
                        side.give(bank, v)
                        slots_ready[pair] = v
                        yield

                def make_put(pair):
                    bank, freed = side.take()
                    PE.wait(*freed)
                    for j in range(2):
                        for t in range(NT):
                            m = PE.run(nc.tensor.transpose, bank[:, (2 * j + t) * P:(2 * j + t + 1) * P],
                                       pick4[:, t, 2 * pair + j, :].bitcast(F32), ident, mark=(j == 1 and t == 1))
                    s = S.run(act, put3[:, 2 * pair:2 * pair + 2, :], tiles(bank[:, :]), ACT.Copy, after=[m], own=False)
                    side.give(bank, s)
                    put_ready[pair] = s
                    yield

                put_ready = {}

                def scatter(e, y_ready):
                    PE.wait(y_ready, put_ready[e // 2])
                    for t in range(NT):
                        for hf in range(2):
                            cs = slice(hf * BANK, (hf + 1) * BANK)
                            bank, freed = side.take()
                            m = group(bank[:, :], [(put3[:, e, t * P:(t + 1) * P], z[:, cs]) for z in (yhi, ylo)],
                                      after=freed)
                            xo = x3[:, t, cs]
                            v = V.run(stt, xo, bank[:, :], gate(t, e), xo, ALU.mult, ALU.add, after=[m], own=False)
                            side.give(bank, v)
                        y_read[0] = m
                        yield

                todo = []

                def between():
                    if todo and next(todo[0], 0) is not None:
                        todo.pop(0)
                        between()

                def finish(e):
                    def put_back(ys, ym):
                        slots_read[e // 2] = ym
                        S.wait(y_read[0])
                        V.wait(y_read[0])
                        for _, hf, bank in ys:
                            cs = slice(hf * BANK, (hf + 1) * BANK)
                            v = to_parts(yhi[:, cs], ylo[:, cs], bank[:, :], ym)
                            pool_y.give(bank, v)
                        todo.append(scatter(e, v))
                        if e % 2 == 1 and e // 2 + 2 < NE // 2:
                            todo.append(gather(e // 2 + 2))
                    return put_back

                def tokens(e):
                    z3 = [z.rearrange("p (k n) -> p k n", k=KD) for z in gathered[(e // 2) % 2]]
                    return lambda k, t: tuple(z[:, k, (e % 2) * P:(e % 2 + 1) * P] for z in z3)

                for _ in gather(0):
                    pass
                todo += [make_put(i) for i in range(NE // 2)] + [gather(1)]
                feed_forward(stage, "moe", 1, [(tokens(e), lambda e=e: slots_ready[e // 2], finish(e)) for e in range(NE)],
                             pool_a, pool_y, tag="_sparse", between=between)
                while todo:
                    between()

        order = (0, 1, 3, 2)
        branch_items = ["p1", "g0", "p2", "g1", "a0", "p3", "g2", "a1", "g3", "a2"]

        def plan_project(l, b):
            w = a["w_in"][l]
            if b == 0:
                plan_full("p0", w, COLS["rq"])
                plan_full("p0", w, COLS["rk"])
                plan_half("p0", w, COLS["rv"])
            elif b == 1:
                for i in range(3):
                    plan_full("p1", w, COLS["sxbc"] + i * 2 * P)
                plan_full("p1", w, COLS["sz"])
            elif b == 2:
                plan_full("p2", w, COLS["mqk"])
                plan_full("p2", w, COLS["mqk"] + 2 * P)
                plan_half("p2", w, COLS["mv"])
            else:
                plan_full("p3", w, COLS["gq"])
                plan_half("p3", w, COLS["gv"])

        for l in range(DEPTH):
            plan_strips("z", a["w_in"][l], [(COLS["sdt"], NH), (COLS["ga"], 16), (COLS["mi"], 2 * NH)])
            plan_project(l, 0)
            for item in branch_items + ["a3"]:
                b = int(item[1])
                if item[0] == "p":
                    plan_project(l, b)
                elif item[0] == "g":
                    for hf in range(2):
                        plan_half(item, a["w_in"][l], COLS["mgate"] + order[b] * D + hf * BANK, lo_on="G")
                else:
                    plan_rows(item, a["w_branch"][l][order[b]], 0)
            for hf in range(2):
                plan_half("wout", a["w_out"][l], hf * BANK)
            if l % 2 == 0:
                plan_ff("ffn", (a["ffn_w1"][l // 2], a["ffn_w3"][l // 2], a["ffn_w2"][l // 2]))
            else:
                plan_ff("moe", *[(a["moe_w1"][l // 2, e], a["moe_w3"][l // 2, e], a["moe_w2"][l // 2, e])
                                 for e in range(NE)])
        for l in range(DEPTH):
            for c in range(MOD // BANK):
                plan_half("ada", a["ada_w"][l], c * BANK)
            plan_full("q2", a["w_in2"][l], 0)
            plan_full("q2", a["w_in2"][l], 2 * P)
            plan.append(("kv2", "V", PIECE, [(lambda ap: ap.rearrange("p (k n) -> p k n", k=KD),
                                              chunk_rows(a["w_in2"][l], 0, KD, 512, 2 * P))]))
            plan_half("u2", a["w_in2"][l], 768)
            for hf in range(2):
                plan_half("wout2", a["w_out2"][l], hf * BANK)
            plan_ff("ffn2", (a["w_gate"][l], a["w_up"][l], a["w_down"][l]))

        tokcol = tiny(4 * NT * NH)
        tc4 = tokcol.rearrange("p (r t h) -> p r t h", r=4, t=NT)
        ss8, rs8, den8, aneg = tiny(NT * NH), tiny(NT * NH), tiny(NT * NH), tiny(1)
        ones_row = const("ones")

        for l in range(DEPTH):
            stage = ExitStack()
            one = lambda name, n, dt=F32: sb(stage, f"{name}_{l}", n, dt)
            gate_t = [one(f"gate_tanh{i}", NT * D) for i in range(2)]
            y_parts = [(one(f"yhi{i}", 2 * T, F32R), one(f"ylo{i}", 2 * T, F32R)) for i in range(2)]
            obuf, osq = one("obuf", NT * MIX), one("osq", NT * MIX)
            scA_, scB_ = one("scoresA", NH * SC), one("scoresB", NH * SC)
            scA, scB = (z.rearrange("p (h n) -> p h n", h=NH) for z in (scA_, scB_))
            rowbuf = one("rowbuf", 8 * T)
            arenas = [one("arena0", 3092), one("arena1", 4626)]
            row = lambda i: rowbuf[0:NH, i * T:(i + 1) * T]
            DT, ACS, LF, BC, CJ, NM, TMP, TMP2 = range(8)
            MX = LF
            gate_feat = one("gate_feat", T)
            merged3 = xn3

            def carve(b, *sizes):
                at, out_ = 0, []
                for n in sizes:
                    out_.append(arenas[b % 2][:, at:at + n])
                    at += n
                return out_

            rv, rg, rqk, rot_raw = carve(0, NT * MIX, NT * MIX, 4 * T, 4 * T)
            pad1, conv1, sz, xs, xdt = carve(1, 6 * (T + PAD), 6 * T, NT * MIX, NT * MIX, NT * MIX)
            mva, mo, pad2, conv2 = carve(2, NT * NH * (HD + 1), NT * MIX, 4 * (T + PAD), 4 * T)
            gv, gr, glaq, glak, glaG, glaE, glaX0, glaX1 = carve(3, NT * MIX, NT * MIX, *[T] * 6)
            branch_done = {}

            rm = S.dma(nc.scalar.dma_start, rows_t, a["rows1"][l:l + 1, :].broadcast_to([P, 4 * MIX + NH]), s_rows,
                       after=[V.last])
            V.wait(rm)
            grow = lambda i: rep(rows_t[:, i * MIX:(i + 1) * MIX], NT)
            m = rms(x3, xn3)
            hm = to_features(xn3, m, scale=lambda k: col("mix_g", l, k), reads=[PE.last])
            tap(f"hT{l}", hThi.bitcast(F32))

            def twice_silu(dst, tanh, src, after=()):
                s = S.run(act, tanh, src, ACT.Tanh, scale=0.5, after=after, own=False)
                return V.run(stt, dst, tanh, 1.0, src, ALU.add, ALU.mult, after=[s, *after], own=False)

            parts = piece("z")
            w = full(parts, 28)
            strip_banks = []
            for c, n in ((0, NH), (4, 16), (20, NH), (24, NH)):
                bank, freed = pool.take()
                PE.wait(*freed)
                strip_banks.append((bank, project_features(w, c, hm, bank, 0, rows=n)))
            finished(parts, strip_banks[-1][1])
            (b_dt, m_dt), (b_ga, m_ga), (b_i, m_i), (b_f, m_f) = strip_banks
            v = V.run(ts, row(DT), b_dt[0:NH, 0:T], col("dt_bias", l, rows=NH), None, ALU.add, after=[m_dt], own=False)
            pool.give(b_dt, v)
            s = S.run(act, gate_feat[0:16, :], b_ga[0:16, 0:T], ACT.Copy, after=[m_ga], own=False)
            pool.give(b_ga, s)
            v = V.run(ts, row(CJ), b_i[0:NH, 0:T], col("b_i", l, rows=NH), None, ALU.add, after=[m_i], own=False)
            pool.give(b_i, v)
            v = V.run(ts, row(LF), b_f[0:NH, 0:T], col("b_f", l, rows=NH), -1.0, ALU.add, ALU.mult, after=[m_f], own=False)
            pool.give(b_f, v)
            bank, freed = pool.take()
            m = group(bank[:, 0:T], [(cols[0:16, COLUMN[("w_alpha", l)]:COLUMN[("w_alpha", l)] + P], gate_feat[0:16, :])],
                      after=[*freed, s])
            zalpha = osq[:, 0:T]
            v = V.run(ts, zalpha, bank[:, 0:T], col("b_alpha", l), -1.0, ALU.add, ALU.mult, after=[m])
            pool.give(bank, v)

            def gate_side(dst, bank, m, c0, t, after=()):
                d = tok3(dst)[:, t]
                return twice_silu(d, d, bank[:, c0:c0 + MIX], after=[m, *after])

            def project(b):
                before = branch_done.get(b - 2, [])
                S.wait(*before)
                V.wait(*before)
                if b == 0:
                    for i in range(2):
                        parts = piece("p0")
                        w = full(parts)
                        bank, freed = pool.take()
                        PE.wait(*freed)
                        for j in range(2):
                            m = project_features(w, j * P, hm, bank, j * T)
                        finished(parts, m)
                        s = S.run(act, tiles(rot_raw)[:, 2 * i:2 * i + 2, :], tiles(bank[:, :]), ACT.Copy, after=[m],
                                  own=False)
                        pool.give(bank, s)
                        yield
                    for t, (bank, m) in enumerate(project_tokens("p0", hm)):
                        s = S.run(act, tok3(rv)[:, t], bank[:, 0:MIX], ACT.Copy, after=[m], own=False)
                        v = gate_side(rg, bank, m, MIX, t)
                        pool.give(bank, v)
                    yield
                elif b == 1:
                    V.run(nc.vector.memset, pad1.rearrange("p (c t) -> p c t", c=6)[:, :, 0:PAD], 0.0)
                    for i in range(3):
                        parts = piece("p1")
                        yield from conv_in(parts, pad1.rearrange("p (c t) -> p c t", c=6), tiles(conv1), 2 * i,
                                           "ssd_conv", NSX)
                    parts = piece("p1")
                    w = full(parts)
                    for t in range(NT):
                        bank, freed = pool.take()
                        PE.wait(*freed)
                        m = product(bank[:, 0:MIX], [(stat_tokens(k, t), (w[0][:, k, :], w[1][:, k, :]))
                                                     for k in range(KD)])
                        v = gate_side(sz, bank, m, 0, t)
                        pool.give(bank, v)
                    finished(parts, m)
                    yield
                elif b == 2:
                    V.run(nc.vector.memset, pad2.rearrange("p (c t) -> p c t", c=4)[:, :, 0:PAD], 0.0)
                    V.run(nc.vector.memset, heads(mva)[:, :, :, HD:HD + 1], 1.0)
                    for i in range(2):
                        parts = piece("p2")
                        yield from conv_in(parts, pad2.rearrange("p (c t) -> p c t", c=4), tiles(conv2), 2 * i,
                                           "ml_conv", NMQ)
                    for t, (bank, m) in enumerate(project_tokens("p2", hm)):
                        s = S.run(act, heads(mva)[:, t, :, 0:HD], bank[:, 0:MIX].rearrange("p (h n) -> p h n", h=NH),
                                  ACT.Copy, after=[m], own=False)
                        s = S.run(act, tok3(mo)[:, t], bank[:, MIX:2 * MIX], ACT.Tanh, scale=0.5, own=False)
                        pool.give(bank, s)
                    yield
                else:
                    parts = piece("p3")
                    w = full(parts)
                    bank, freed = pool.take()
                    PE.wait(*freed)
                    for j in range(2):
                        m = project_features(w, j * P, hm, bank, j * T)
                    finished(parts, m)
                    s = S.run(act, glaq, bank[:, 0:T], ACT.Copy, scale=GLA_DK ** -0.5, after=[m], own=False)
                    s = S.run(act, glak, bank[:, T:2 * T], ACT.Copy, own=False)
                    pool.give(bank, s)
                    yield
                    for t, (bank, m) in enumerate(project_tokens("p3", hm)):
                        s = S.run(act, tok3(gv)[:, t], bank[:, 0:MIX], ACT.Copy, after=[m], own=False)
                        v = gate_side(gr, bank, m, MIX, t)
                        pool.give(bank, v)
                    yield

            def conv_in(parts, pad3, conv3, first, name, n):
                w = full(parts)
                bank, freed = pool.take()
                PE.wait(*freed)
                for j in range(2):
                    m = project_features(w, j * P, hm, bank, j * T)
                finished(parts, m)
                s = S.run(act, pad3[:, first:first + 2, PAD:], tiles(bank[:, :]), ACT.Copy, after=[m], own=False)
                pool.give(bank, s)
                yield
                for c in (first, first + 1):
                    dst = conv3[:, c, :]
                    s = S.run(act, dst, pad3[:, c, 0:T], ACT.Identity, scale=col(name + "_w", l, c),
                              bias=col(name + "_b", l, c), after=[V.last])
                    for k in range(1, CONV_K):
                        v = V.run(stt, dst, pad3[:, c, k:k + T], col(name + "_w", l, k * n + c), dst, ALU.mult,
                                  ALU.add, after=[s])
                    twice_silu(dst, pad3[:, c, PAD:], dst, after=[v])

            def scores(qt, kt, rows, bank, after=()):
                PE.wait(*after)
                PE.run(mm, bank[:, 0:T], kt[rows, 0:P], qt[rows, 0:T], start=True, stop=True, mark=False)
                return PE.run(mm, bank[:, T:SC], kt[rows, P:T], qt[rows, P:T], start=True, stop=True)

            def apply_scores(sc, v4, after, width=HD):
                outs = []
                PE.wait(*after)
                for t in range(NT):
                    bank, freed = pool.take()
                    PE.wait(*freed)
                    o = bank[:, 0:NH * width].rearrange("p (h n) -> p h n", h=NH)
                    for h in range(NH):
                        if t == 0:
                            m = group(o[:, h, :], [(sc[:, h, 0:P], v4[:, 0, h, :])])
                        else:
                            m = group(o[:, h, :], [(sc[:, h, P:T], v4[:, 0, h, :]), (sc[:, h, T:SC], v4[:, 1, h, :])])
                    outs.append((bank, o, m))
                return outs

            def head_norm(src, side, b, after=(), lone=False, half=0.5):
                n = 1 if lone else NH
                w_ = MIX // n
                V.run(tt, osq, src, src, ALU.mult, after=after)
                V.run(reduce, ss8[:, 0:NT * n], osq.rearrange("p (g n) -> p g n", n=w_), AXX, ALU.add)
                V.run(tt, src, src, side, ALU.mult)
                V.wait(inverse_root(rs8[:, 0:NT * n], ss8[:, 0:NT * n], w_, V.last))
                g_ = src.rearrange("p (g n) -> p g n", n=w_)
                v = V.run(tt, g_, g_, rs8[:, 0:NT * n].unsqueeze(2).broadcast_to([P, NT * n, w_]), ALU.mult)
                bank, freed = pool.take()
                PE.wait(*freed, v)
                for c in range(2):
                    for t in range(NT):
                        m = PE.run(nc.tensor.transpose, bank[:, (2 * c + t) * P:(2 * c + t + 1) * P],
                                   tok3(src)[:, t, c * P:(c + 1) * P], ident, mark=(c == 1 and t == 1))
                while done["merged"] < b - 2:
                    advance()
                S.wait(y_read.get(b - 2))
                V.wait(y_read.get(b - 2))
                v = to_parts(*y_parts[b % 2], bank[:, :], m, scale=half)
                pool.give(bank, v)
                branch_done[b] = marks()
                y_ready[b] = v

            y_ready, y_read = {}, {}

            def softplus(dst, src, tmp, tmp2):
                v = V.run(stt, tmp, src, -1.0, src, ALU.mult, ALU.min)
                s = S.run(act, tmp2, tmp, ACT.Exp, after=[v])
                s = S.run(act, tmp2, tmp2, ACT.Ln, bias=1.0)
                return V.run(stt, dst, src, 0.0, tmp2, ALU.max, ALU.add, after=[s])

            def decays(dst, r_, colid):
                op = ALU.subtract if colid == 0 else ALU.add
                for h2 in range(2):
                    bank, freed = pool.take()
                    PE.wait(*freed)
                    for j in range(2):
                        m = PE.run(mm, bank[:, j * T:(j + 1) * T],
                                   ident[0:NH, 2 * h2 + j:2 * h2 + j + 1].broadcast_to([NH, P]), r_,
                                   start=True, stop=True, mark=(j == 1))
                    for j in range(2):
                        h = 2 * h2 + j
                        V.run(ts, dst[:, h, 0:T], bank[:, j * T:(j + 1) * T], tc4[:, colid, 0, h:h + 1], 0.0,
                              op, ALU.min, after=[m], own=(h == 0))
                        v = V.run(ts, dst[:, h, T:SC], bank[:, j * T + P:(j + 1) * T], tc4[:, colid, 1, h:h + 1],
                                  0.0, op, ALU.min, own=False)
                    pool.give(bank, v)
                    s = S.run(act, dst[:, 2 * h2:2 * h2 + 2, :], dst[:, 2 * h2:2 * h2 + 2, :], ACT.Exp, after=[v],
                              own=False)
                return s

            def retention():
                for i in range(2):
                    bank, freed = pool.take()
                    PE.wait(*freed)
                    m = PE.run(mm, bank[:, :], const("rot"), rot_raw[:, i * 2 * T:(i + 1) * 2 * T], start=True, stop=True)
                    two, raw3, out3 = slice(2 * i, 2 * i + 2), tiles(rot_raw), tiles(rqk)
                    V.run(tt, out3[:, two, :], tiles(bank[:, :]), rep(const("sin"), 2), ALU.mult, after=[m])
                    pool.give(bank, V.last)
                    V.run(tt, raw3[:, two, :], raw3[:, two, :], rep(const("cos"), 2), ALU.mult)
                    v = V.run(tt, out3[:, two, :], out3[:, two, :], raw3[:, two, :], ALU.add)
                    yield
                dec = const("decay").rearrange("p (h n) -> p h n", h=NH)
                PE.wait(v)
                r3 = tiles(rqk)
                for h in range(NH):
                    bank, freed = pool.take()
                    rows = slice((h % 2) * HD, (h % 2 + 1) * HD)
                    m = scores(r3[:, h // 2, :], r3[:, 2 + h // 2, :], rows, bank, after=freed)
                    v = V.run(tt, scB[:, h, :], bank[:, 0:SC], dec[:, h, :], ALU.mult, after=[m], own=(h == 0))
                    pool.give(bank, v)
                yield
                outs = apply_scores(scB, heads(rv), [v])
                for t, (bank, o, m) in enumerate(outs):
                    s = S.run(act, tok3(obuf)[:, t], bank[:, 0:MIX], ACT.Copy, after=[m], own=False)
                    pool.give(bank, s)
                V.run(tt, tok3(rg), tok3(rg), grow(0), ALU.mult)
                yield
                head_norm(obuf, rg, 0, [s])
                tap(f"yret{l}", y_parts[0][0].bitcast(F32))

            def ssd():
                c3 = tiles(conv1)
                bank, freed = pool.take()
                PE.wait(*freed, V.last)
                for t in range(NT):
                    for c in range(2):
                        m = PE.run(nc.tensor.transpose, bank[:, (2 * t + c) * P:(2 * t + c + 1) * P],
                                   c3[:, c, t * P:(t + 1) * P], ident, mark=(c == 1 and t == 1))
                s = S.run(act, xs, bank[:, :], ACT.Copy, scale=0.5, after=[m], own=False)
                pool.give(bank, s)
                yield
                s_e = decays(scA, row(ACS), 0)
                yield
                for t in range(NT):
                    V.run(tt, heads(xdt)[:, t], heads(xs)[:, t], tc4[:, 1, t].unsqueeze(2).broadcast_to([P, NH, HD]),
                          ALU.mult, after=[s])
                yield
                for g in range(2):
                    bank, freed = pool.take()
                    m = scores(c3[:, 4 + g, :], c3[:, 2 + g, :], slice(0, P), bank, after=freed)
                    v = V.run(stt, scB[:, g, :], bank[:, 0:SC], 0.25, const("tri"), ALU.mult, ALU.mult, after=[m])
                    pool.give(bank, v)
                    V.run(tt, scA[:, 2 * g:2 * g + 2, :], scA[:, 2 * g:2 * g + 2, :], rep(scB[:, g, :], 2), ALU.mult,
                          after=[s_e])
                yield
                outs = apply_scores(scA, heads(xdt), [V.last])
                drow = rows_t[:, 4 * MIX:4 * MIX + NH].unsqueeze(2).broadcast_to([P, NH, HD])
                for t in range(NT):
                    V.run(tt, heads(obuf)[:, t], heads(xs)[:, t], drow, ALU.mult)
                yield
                for t, (bank, o, m) in enumerate(outs):
                    v = V.run(tt, heads(obuf)[:, t], heads(obuf)[:, t], o, ALU.add, after=[m])
                    pool.give(bank, v)
                V.run(stt, obuf, obuf, 0.5, sz, ALU.mult, ALU.mult)
                V.run(vcopy, tok3(sz), grow(1))
                yield
                head_norm(obuf, sz, 1, lone=True, half=1.0)
                tap(f"yssd{l}", y_parts[1][0].bitcast(F32))

            def mlstm():
                c3 = tiles(conv2)
                PE.wait(V.last)
                s = decays(scA, row(NM), 2)
                yield
                V.run(stt, scA, scA, 0.25 * HD ** -0.5, rep(const("tri"), NH), ALU.mult, ALU.mult, after=[s])
                for h in range(NH):
                    bank, freed = pool.take()
                    rows = slice((h % 2) * HD, (h % 2 + 1) * HD)
                    m = scores(c3[:, h // 2, :], c3[:, 2 + h // 2, :], rows, bank, after=freed)
                    v = V.run(tt, scA[:, h, :], scA[:, h, :], bank[:, 0:SC], ALU.mult, after=[m], own=(h == 0))
                    pool.give(bank, v)
                yield
                outs = apply_scores(scA, mva.rearrange("p (t h n) -> p t h n", t=NT, h=NH), [v], width=HD + 1)
                V.run(stt, tok3(mo), tok3(mo), 1.0, grow(3), ALU.add, ALU.mult)
                yield
                d3 = den8.rearrange("p (t h) -> p t h", t=NT)
                for t, (bank, o, m) in enumerate(outs):
                    V.run(vcopy, ss8[:, 0:NH], o[:, :, HD], after=[m])
                    V.run(stt, d3[:, t], ss8[:, 0:NH], -1.0, ss8[:, 0:NH], ALU.mult, ALU.max)
                    V.run(tt, d3[:, t], d3[:, t], tc4[:, 3, t], ALU.max)
                    V.run(nc.vector.reciprocal, d3[:, t], d3[:, t])
                    v = V.run(tt, heads(obuf)[:, t], o[:, :, 0:HD], d3[:, t].unsqueeze(2).broadcast_to([P, NH, HD]),
                              ALU.mult)
                    pool.give(bank, v)
                yield
                head_norm(obuf, mo, 2)
                tap(f"yml{l}", y_parts[0][0].bitcast(F32))

            def gla():
                V.run(scan, glaG, ones_row, gate_feat, 0.0, ALU.mult, ALU.add)
                V.run(nc.vector.memset, scB[:, :, 0:P], 0.0)
                V.run(nc.vector.memset, scB[:, :, T:SC], 0.0)
                lm3 = lmask.rearrange("p (l n) -> p l n", n=P)
                reads, X = [None, None], [glaX0, glaX1]

                def level_scores(kt, qt, li, after):
                    PE.wait(*after)
                    own = [pool.take() for _ in range(NH)]
                    PE.wait(*[f for _, freed in own for f in freed])
                    blocks = [(0, slice(0, P), slice(P, T))] if li is None else [
                        (t, slice(t * P, (t + 1) * P), slice(t * P, (t + 1) * P)) for t in range(NT)]
                    done = []
                    for b, kc, qc in blocks:
                        for h in range(NH):
                            rows = slice(h * GLA_DK, (h + 1) * GLA_DK)
                            done.append(PE.run(mm, own[h][0][:, b * P:(b + 1) * P], kt[rows, kc], qt[rows, qc],
                                               start=True, stop=True, tile_position=(h * GLA_DK, 0),
                                               mark=(b == len(blocks) - 1)))
                    for h in range(NH):
                        bank, m = own[h][0], done[-NH + h]
                        if li is None:
                            v = V.run(vcopy, scB[:, h, P:T], bank[:, 0:P], after=[m], own=False)
                        else:
                            dst = scB[:, h, :].rearrange("p (b n) -> p b n", n=P)[:, ::2, :]
                            v = V.run(nc.vector.copy_predicated, dst, rep(lm3[:, li, :], NT),
                                      bank[:, 0:T].rearrange("p (b n) -> p b n", n=P), after=[m], own=(h == 0))
                        pool.give(bank, v)
                    return done[-1]

                level_scores(glak, glaq, len(GLA_LEVELS), [V.last, S.last])
                yield
                for i, half in enumerate((P,) + GLA_LEVELS):
                    buf = X[i % 2]
                    n = T // (2 * half)
                    view = lambda ap: ap.rearrange("p (n s c) -> p n s c", n=n, s=2)
                    ref = view(glaG)[:, :, 0, half - 1:half].broadcast_to([P, n, half])
                    V.run(tt, view(glaE)[:, :, 1, :], view(glaG)[:, :, 1, :], ref, ALU.subtract)
                    v = V.run(tt, view(glaE)[:, :, 0, :], ref, view(glaG)[:, :, 0, :], ALU.subtract, own=False)
                    s = S.run(act, glaE, glaE, ACT.Exp, after=[v])
                    V.run(tt, view(buf)[:, :, 1, :], view(glaE)[:, :, 1, :], view(glaq)[:, :, 1, :], ALU.mult,
                          after=[s, reads[i % 2]])
                    v = V.run(tt, view(buf)[:, :, 0, :], view(glaE)[:, :, 0, :], view(glak)[:, :, 0, :], ALU.mult,
                              own=False)
                    reads[i % 2] = level_scores(buf, buf, None if half == P else i - 1, [v])
                    yield
                outs = apply_scores(scB, heads(gv), [V.last])
                for t, (bank, o, m) in enumerate(outs):
                    s = S.run(act, tok3(obuf)[:, t], bank[:, 0:MIX], ACT.Copy, after=[m], own=False)
                    pool.give(bank, s)
                V.run(tt, tok3(gr), tok3(gr), grow(2), ALU.mult)
                yield
                head_norm(obuf, gr, 3, [s])
                tap(f"ygla{l}", y_parts[1][0].bitcast(F32))

            gate_reads = [[], []]

            def gate(b):
                g3 = tok3(gate_t[b % 2])
                S.wait(*gate_reads[b % 2])
                for hf in range(2):
                    for t, (bank, m) in enumerate(project_tokens(f"g{b}", hm)):
                        s = S.run(act, g3[:, t, hf * BANK:(hf + 1) * BANK], bank[:, :], ACT.Tanh, scale=0.5, after=[m],
                                  own=False)
                        pool.give(bank, s)
                    yield
                gate_ready[b] = s

            gate_ready = {}

            def merge(b):
                parts = piece(f"a{b}")
                w = [z.rearrange("p (c n) -> p c n", c=2) for z in parts]
                yp = [tiles(z) for z in y_parts[b % 2]]
                g3 = tok3(gate_t[b % 2])
                PE.wait(y_ready[b])
                for t in range(NT):
                    for hf in range(2):
                        cs = slice(hf * BANK, (hf + 1) * BANK)
                        bank, freed = pool.take()
                        PE.wait(*freed)
                        m = product(bank[:, :], [((yp[0][:, c, t * P:(t + 1) * P], yp[1][:, c, t * P:(t + 1) * P]),
                                                  (w[0][:, c, cs], w[1][:, c, cs])) for c in range(2)])
                        dst = merged3[:, t, cs] if b == 0 else g3[:, t, cs]
                        v = V.run(stt, dst, g3[:, t, cs], 1.0, bank[:, :], ALU.add, ALU.mult,
                                  after=[m, gate_ready[b]], own=False)
                        pool.give(bank, v)
                finished(parts, m)
                y_read[b] = m
                if b > 0:
                    v = V.run(tt, merged3, merged3, g3, ALU.add)
                gate_reads[b % 2] = [v]
                yield

            branches = [retention, ssd, mlstm, gla]
            done = {"p": -1, "core": -1, "merged": -1}
            items = [(z[0], int(z[1])) for z in branch_items]
            current = []

            def advance():
                if not current:
                    if not items:
                        return False
                    kind, b = items[0]
                    if kind == "a" and done["core"] < b:
                        return False
                    items.pop(0)
                    current.append((kind, b, {"p": project, "g": gate, "a": merge}[kind](b)))
                kind, b, steps = current[0]
                if next(steps, 0) is not None:
                    current.clear()
                    if kind in "pa":
                        done["p" if kind == "p" else "merged"] = b
                    return advance()
                return True

            for _ in project(0):
                pass
            softplus(row(DT), row(DT), row(TMP), row(TMP2))
            softplus(row(LF), row(LF), row(TMP), row(TMP2))
            softplus(gate_feat, zalpha, glaE, glaX0)
            V.run(ts, gate_feat, gate_feat, -1.0 / GLA_TAU, None, ALU.mult)
            s = S.run(act, aneg[0:NH, :], col("a_log", l, rows=NH), ACT.Exp)
            V.run(ts, row(TMP), row(DT), aneg[0:NH, :], -1.0, ALU.mult, ALU.mult, after=[s])
            V.run(scan, row(ACS), ones_row[0:NH, :], row(TMP), 0.0, ALU.mult, ALU.add)
            V.run(ts, row(LF), row(LF), -1.0, None, ALU.mult)
            V.run(scan, row(BC), ones_row[0:NH, :], row(LF), 0.0, ALU.mult, ALU.add)
            V.run(tt, row(CJ), row(CJ), row(BC), ALU.subtract)
            V.run(scan, row(MX), ones_row[0:NH, :], row(CJ), 0.0, ALU.mult, ALU.max)
            V.run(tt, row(TMP), row(BC), row(MX), ALU.add)
            v = V.run(ts, row(NM), row(MX), -1.0, None, ALU.mult)
            s = S.run(act, row(TMP2), row(TMP), ACT.Exp, scale=-1.0, after=[v])
            advance()
            bank, freed = pool.take()
            PE.wait(*freed, v, s)
            for i, r_ in enumerate((ACS, DT, CJ, TMP2)):
                for t in range(NT):
                    c = (i * NT + t) * NH
                    m = PE.run(nc.tensor.transpose, bank[:, c:c + NH], row(r_)[:, t * P:(t + 1) * P],
                               ident[0:NH, 0:NH], mark=(i == 3 and t == 1))
            v = V.run(vcopy, tokcol, bank[:, 0:4 * NT * NH], after=[m])
            pool.give(bank, v)

            for b, branch in enumerate(branches):
                while done["p"] < b and b > 0:
                    advance()
                for _ in branch():
                    advance()
                done["core"] = b
            while advance():
                pass
            for _ in merge(3):
                pass
            tap(f"merged{l}", merged3)
            mT = to_features(merged3, V.last, scale=0.5, reads=[PE.last])
            for hf in range(2):
                for t, (bank, m) in enumerate(project_tokens("wout", mT)):
                    xo = x3[:, t, hf * BANK:(hf + 1) * BANK]
                    v = V.run(tt, xo, xo, bank[:, :], ALU.add, after=[m], own=False)
                    pool.give(bank, v)
            tap(f"xmix{l}", x3)
            join()
            stage.close()

            m = rms(x3, xn3)
            ffn_gain = lambda k: col("ffn_g", l, k)
            if l % 2 == 0:
                stage = ExitStack()
                hm = to_features(xn3, m, scale=ffn_gain, reads=[PE.last])
                join()

                def add_outputs(ys, ym):
                    for t, hf, bank in ys:
                        xo = x3[:, t, hf * BANK:(hf + 1) * BANK]
                        V.run(tt, xo, xo, bank[:, :], ALU.add, after=[ym], own=False)

                feed_forward(stage, "ffn", NT, [(stat_tokens, lambda: hm, add_outputs)], Slots(banks[4:8]), Slots(banks[0:4]))
                join()
                stage.close()
            else:
                experts(l, m, ffn_gain)
            tap(f"xffn{l}", x3)
            pool.free = [(b, ()) for b in banks]

        stage2 = ExitStack()
        mod = sb(stage2, "mod", MOD)
        cs_, sn_ = sb(stage2, "rope_cos", T), sb(stage2, "rope_sin", T)
        m3 = mod.rearrange("p (s d) -> p s d", s=6)
        fg = mod[:, 0:D]
        rm = S.dma(nc.scalar.dma_start, fg, a["rows2"][0:1, 0:D].broadcast_to([P, D]), s_rows)
        rms(x3, xn3)
        v = V.run(tt, x3, xn3, rep(fg, NT), ALU.mult, after=[rm])
        tap("first", x3)

        ang, turn, rest = (m3[:, i, 0:T] for i in (2, 3, 4))
        posi = m3[:, 5, 0:T].bitcast(I32)
        rm = S.dma(nc.scalar.dma_start, posi, a["positions"].broadcast_to([P, T]), s_rows, after=[v])
        V.run(vcopy, ang, posi, after=[rm])
        V.run(ts, ang, ang, const("invf"), None, ALU.mult)
        two_pi = 2 * np.pi
        part1 = 6.28125
        part2 = float(np.round((two_pi - part1) * 2 ** 20) / 2 ** 20)
        part3 = float(two_pi - part1 - part2)
        to_integer = 1.5 * 2 ** 23
        pi32 = float(np.float32(np.pi))

        def sine(dst, shift):
            V.run(ts, turn, ang, 1.0 / two_pi, shift / two_pi, ALU.mult, ALU.add)
            V.run(ts, turn, turn, to_integer, None, ALU.add)
            V.run(ts, turn, turn, to_integer, None, ALU.subtract)
            V.run(stt, rest, turn, -part1, ang, ALU.mult, ALU.add)
            V.run(stt, rest, turn, -part2, rest, ALU.mult, ALU.add)
            V.run(stt, rest, turn, -part3, rest, ALU.mult, ALU.add)
            V.run(ts, rest, rest, shift, pi32, ALU.add, ALU.min)
            v = V.run(ts, rest, rest, -pi32, None, ALU.max)
            s = S.run(act, dst, rest, ACT.Sin, after=[v])
            V.wait(s)

        sine(sn_, 0.0)
        sine(cs_, float(np.pi / 2))
        V.run(ts, sn_, sn_, const("rotrow"), None, ALU.mult)
        V.run(ts, cs_, cs_, const("rotrow"), const("restrow"), ALU.mult, ALU.add)
        tap("rope", cs_)
        cc = tiny(KD)
        S.run(act, cc, col("c", 0, 0, KD), ACT.Silu)
        sink8, mx8, sm8, nb8 = tiny(QH), tiny(QH), tiny(QH), tiny(QH)
        join()

        def norm_and_add(banks_in, gate_part, after):
            for t, hf, bank in banks_in:
                S.run(act, xn3[:, t, hf * BANK:(hf + 1) * BANK], bank[:, :], ACT.Copy, after=after, own=False)
            for t in range(NT):
                m = S.run(act, squares[:, t * D:(t + 1) * D], xn3[:, t, :], ACT.Square, accum_out=stat[:, t:t + 1])
            V.wait(inverse_root(stat[:, 4:6], stat[:, 0:2], D, m))
            for t in range(NT):
                V.run(stt, xn3[:, t, :], xn3[:, t, :], stat[:, 4 + t:5 + t], m3[:, gate_part, :], ALU.mult, ALU.mult)
            V.run(tt, x3, x3, xn3, ALU.add)

        def modulated(scale_part, shift_part):
            rms(x3, xn3, after=[V.last])
            V.run(tt, xn3, xn3, rep(m3[:, scale_part, :], NT), ALU.mult)
            m = V.run(tt, xn3, xn3, rep(m3[:, shift_part, :], NT), ALU.add)
            return to_features(xn3, m, reads=[PE.last])

        for l in range(DEPTH):
            stage = ExitStack()
            one = lambda name, n, dt=F32: sb(stage, f"{name}_{l}", n, dt)
            chi, clo = one("chi", KD * P, F32R), one("clo", KD * P, F32R)
            bias = [one(f"ada_bias{i}", BANK) for i in range(2)]
            grow2 = one("gain_row", D)
            s_bias = [[sem(f"ada_bias{i}_in_{l}"), 0] for i in range(2)]
            bias_read = [None, None]
            c3 = [z.rearrange("p (k m) -> p k m", k=KD) for z in (chi, clo)]
            cb = cc.unsqueeze(2).broadcast_to([P, KD, P])
            s = S.run(act, c3[0], cb, ACT.Copy)
            cb_mark = V.run(tt, c3[1], cb, c3[0].bitcast(F32), ALU.subtract, after=[s])
            for c in range(MOD // BANK):
                cs = slice(c * BANK, (c + 1) * BANK)
                bm = SP.dma(nc.sync.dma_start, bias[c % 2], a["ada_b"][l:l + 1, cs].broadcast_to([P, BANK]),
                            s_bias[c % 2], after=[bias_read[c % 2], cb_mark])
                bank, freed = pool.take()
                PE.wait(*freed, cb_mark)
                for half in range(2):
                    parts = piece("ada")
                    w = [z.rearrange("p (k n) -> p k n", k=4) for z in parts]
                    m = product(bank[:, :], [((c3[0][:, 4 * half + k], c3[1][:, 4 * half + k]), (w[0][:, k], w[1][:, k]))
                                             for k in range(4)], start=half == 0, stop=half == 1)
                    finished(parts, m)
                v = V.run(tt, mod[:, cs], bank[:, :], bias[c % 2], ALU.add, after=[m, bm], own=False)
                bias_read[c % 2] = v
                pool.give(bank, v)
            for i, (part, pre) in enumerate(((1, True), (2, False), (4, True), (5, False))):
                rm = S.dma(nc.scalar.dma_start, grow2, a["rows2"][1 + 4 * l + i:2 + 4 * l + i, 0:D].broadcast_to([P, D]),
                           s_rows, after=[V.last])
                if pre:
                    V.run(stt, m3[:, part, :], m3[:, part, :], 1.0, grow2, ALU.add, ALU.mult, after=[rm])
                else:
                    V.run(tt, m3[:, part, :], m3[:, part, :], grow2, ALU.mult, after=[rm])
            tap(f"mod{l}", mod)
            join()
            stage.close()

            stage = ExitStack()
            hm = modulated(1, 0)
            tables_in = one("attention_tables", a["poolm"].shape[1])
            poolm, rot2 = tables_in[:, 0:4 * SC], tables_in[:, 4 * SC:4 * SC + P]
            causal, banded = tables_in[:, 4 * SC + P:4 * SC + 2 * P], tables_in[:, 4 * SC + 2 * P:]
            pw_ = one("pool_weights", 4 * P)
            brow = one("bias_rows", P + BANK)
            qraw, qrot = one("qraw", 6 * T), one("qrot", 6 * T)
            vtok, utok = one("vtok", NT * P), one("utok", NT * BANK)
            prob, probT = one("prob", QH * T), one("probT", QH * T)
            pooled, obuf = one("pooled", 4 * T), one("attended", BANK)
            pw = pw_.rearrange("p (g n) -> p g n", g=4)
            rm = S.dma(nc.scalar.dma_start, tables_in, a["poolm"], s_att)
            rm = S.dma(nc.scalar.dma_start, pw, a["pool_w"][l].rearrange("g p n -> p g n"), s_att)
            rm = S.dma(nc.scalar.dma_start, brow, a["b_in2"][l:l + 1, 640:1280].broadcast_to([P, P + BANK]), s_att)
            rm = S.dma(nc.scalar.dma_start, sink8, a["sinks"][l:l + 1, :].broadcast_to([P, QH]), s_att)
            V.wait(rm)
            PE.wait(rm)
            qraw3, qrot3 = tiles(qraw), tiles(qrot)
            for i in range(2):
                parts = piece("q2")
                w = full(parts)
                bank, freed = pool.take()
                PE.wait(*freed)
                for j in range(2):
                    m = project_features(w, j * P, hm, bank, j * T)
                finished(parts, m)
                for j in range(2):
                    v = V.run(ts, qraw3[:, 2 * i + j, :], bank[:, j * T:(j + 1) * T], col("b_q", l, 2 * i + j), None,
                              ALU.add, after=[m], own=False)
                pool.give(bank, v)
            parts = piece("kv2")
            w = full(parts)
            bank, freed = pool.take()
            PE.wait(*freed)
            m = project_features(w, 0, hm, bank, 0)
            v = V.run(ts, qraw3[:, 4, :], bank[:, 0:T], col("b_k", l), None, ALU.add, after=[m], own=False)
            pool.give(bank, v)
            kmark = v
            vt3, ut3 = tok3(vtok), tok3(utok)
            bank, freed = pool.take()
            PE.wait(*freed)
            for t in range(NT):
                m = product(bank[:, t * P:(t + 1) * P], [(stat_tokens(k, t), (w[0][:, k, P:2 * P], w[1][:, k, P:2 * P]))
                                                         for k in range(KD)])
            finished(parts, m)
            v = V.run(tt, vt3, bank[:, 0:T].rearrange("p (t n) -> p t n", t=NT), rep(brow[:, 0:P], NT), ALU.add,
                      after=[m], own=False)
            pool.give(bank, v)
            bank, freed = pool.take()
            m = group(bank[:, 0:T], [(const("swap"), qraw3[:, 4, :])], after=[*freed, kmark])
            v = V.run(vcopy, qraw3[:, 5, :], bank[:, 0:T], after=[m])
            pool.give(bank, v)
            PE.wait(v)
            for i in range(3):
                bank, freed = pool.take()
                m = group(bank[:, :], [(rot2, qraw[:, 2 * i * T:2 * (i + 1) * T])], after=freed)
                two = slice(2 * i, 2 * i + 2)
                v = V.run(tt, qrot3[:, two, :], tiles(bank[:, :]), rep(sn_, 2), ALU.mult, after=[m])
                pool.give(bank, v)
                V.run(tt, qraw3[:, two, :], qraw3[:, two, :], rep(cs_, 2), ALU.mult)
                v = V.run(tt, qrot3[:, two, :], qrot3[:, two, :], qraw3[:, two, :], ALU.add)
            rotated = v
            tap(f"qrot{l}", qrot)
            for t, (bank, m) in enumerate(project_tokens("u2", hm)):
                v = V.run(tt, ut3[:, t, :], bank[:, :], brow[:, P:P + BANK], ALU.add, after=[m], own=False)
                pool.give(bank, v)
            u_ready = v
            h_read = PE.last

            def pooling():
                pm3 = poolm.rearrange("p (g n) -> p g n", g=4)
                PE.wait(u_ready)
                S.wait(h_read)
                V.wait(h_read)
                for g in range(4):
                    bank, freed = pool.take()
                    PE.wait(*freed)
                    group(bank[:, 0:P], [(ut3[:, 0, g * P:(g + 1) * P], pm3[:, g, 0:P])])
                    m = group(bank[:, P:T], [(ut3[:, 0, g * P:(g + 1) * P], pm3[:, g, P:T]),
                                             (ut3[:, 1, g * P:(g + 1) * P], pm3[:, g, T:SC])])
                    s = S.run(act, pooled[:, g * T:(g + 1) * T], bank[:, 0:T], ACT.Copy, after=[m], own=False)
                    pool.give(bank, s)
                    yield
                    bank, freed = pool.take()
                    m = group(bank[:, 0:T], [(pw[:, g, :], pooled[:, g * T:(g + 1) * T])], after=[*freed, s])
                    v = to_parts(hi3[:, 4 + g, :], lo3[:, 4 + g, :], bank[:, 0:T], m, scale=col("pool_scale", l, g))
                    pool.give(bank, v)
                    yield

            pool_steps = pooling()
            pr3 = prob.rearrange("p (h n) -> p h n", h=QH)
            pT3 = probT.rearrange("p (h n) -> p h n", h=QH)
            pv = None
            PE.wait(rotated)
            for t in range(NT):
                nk = (t + 1) * P
                for h4 in range(QH // 4):
                    for odd in range(2):
                        bank, freed = pool.take()
                        PE.wait(*freed)
                        rows = slice(odd * HD, (odd + 1) * HD)
                        for j in range(2):
                            m = PE.run(mm, bank[:, j * T:j * T + nk], qrot3[rows, 2 * h4 + j, t * P:(t + 1) * P],
                                       qrot3[rows, 4 + (h4 ^ odd), 0:nk], start=True, stop=True, mark=(j == 1))
                        b3 = bank[:, :].rearrange("p (j n) -> p j n", j=2)[:, :, 0:nk]
                        v = V.run(stt, pr3[:, 4 * h4 + odd:4 * h4 + odd + 3:2, 0:nk], b3, HD ** -0.5,
                                  rep(banded[:, 0:nk] if t else causal, 2), ALU.mult, ALU.add, after=[m, pv], own=False)
                        pool.give(bank, v)
                next(pool_steps, 0)
                V.run(reduce, mx8, pr3[:, :, 0:nk], AXX, ALU.max)
                V.run(tt, mx8, mx8, sink8, ALU.max)
                v = V.run(ts, nb8, mx8, -1.0, None, ALU.mult)
                for h in range(QH):
                    s = S.run(act, pr3[:, h, 0:nk], pr3[:, h, 0:nk], ACT.Exp, bias=nb8[:, h:h + 1],
                              accum_out=sm8[:, h:h + 1], after=[v], own=False)
                next(pool_steps, 0)
                next(pool_steps, 0)
                v = V.run(tt, mx8, sink8, mx8, ALU.subtract)
                s = S.run(act, mx8, mx8, ACT.Exp, after=[v])
                V.run(tt, sm8, sm8, mx8, ALU.add, after=[s])
                rden = V.run(nc.vector.reciprocal, sm8, sm8)
                for h2 in range(QH // 2):
                    bank, freed = pool.take()
                    PE.wait(*freed, s)
                    for j in range(2):
                        for kt in range(t + 1):
                            m = PE.run(nc.tensor.transpose, bank[:, j * T + kt * P:j * T + (kt + 1) * P],
                                       pr3[:, 2 * h2 + j, kt * P:(kt + 1) * P], ident, mark=(j == 1 and kt == t))
                    b3 = bank[:, :].rearrange("p (j n) -> p j n", j=2)[:, :, 0:nk]
                    v = V.run(vcopy, pT3[:, 2 * h2:2 * h2 + 2, 0:nk], b3, after=[m, pv], own=False)
                    pool.give(bank, v)
                next(pool_steps, 0)
                bank, freed = pool.take()
                PE.wait(*freed, v)
                for h in range(QH):
                    kv = slice((h // 4) * HD, (h // 4 + 1) * HD)
                    m = group(bank[:, h * HD:(h + 1) * HD],
                              [(pT3[:, h, kt * P:(kt + 1) * P], vt3[:, kt, kv]) for kt in range(t + 1)])
                pv = m
                v = V.run(tt, obuf.rearrange("p (h n) -> p h n", h=QH), bank[:, :].rearrange("p (h n) -> p h n", h=QH),
                          sm8.unsqueeze(2).broadcast_to([P, QH, HD]), ALU.mult, after=[m, rden])
                pool.give(bank, v)
                bank, freed = pool.take()
                PE.wait(*freed, v)
                for c in range(4):
                    m = PE.run(nc.tensor.transpose, bank[:, c * P:(c + 1) * P], obuf[:, c * P:(c + 1) * P], ident,
                               mark=(c == 3))
                v = to_parts(hi3[:, 0:4, t * P:(t + 1) * P], lo3[:, 0:4, t * P:(t + 1) * P],
                             bank[:, :].rearrange("p (c n) -> p c n", c=4), m)
                pool.give(bank, v)
            for _ in pool_steps:
                pass
            tap(f"mixT{l}", hThi.bitcast(F32))
            mixed = V.last
            squares = prob
            banks_in = []
            for hf in range(2):
                for t, (bank, m) in enumerate(project_tokens("wout2", mixed)):
                    banks_in.append((t, hf, bank))
            S.wait(*marks())
            norm_and_add(banks_in, 2, [m])
            for _, _, bank in banks_in:
                pool.give(bank, V.last)
            tap(f"x2mix{l}", x3)
            join()
            stage.close()
            stage = ExitStack()
            hm = modulated(4, 3)
            join()
            squares = sb(stage, f"squares_{l}", NT * D)
            feed_forward(stage, "ffn2", NT, [(stat_tokens, lambda: hm, lambda ys, ym: norm_and_add(ys, 5, [ym]))],
                         Slots(banks[4:8]), Slots(banks[0:4]), tag=l)
            join()
            stage.close()
            tap(f"x2ffn{l}", x3)
            pool.free = [(b, ()) for b in banks]

        om = SP.dma(nc.sync.dma_start, out.rearrange("o (t p) d -> p (o t) d", p=P), x3, s_out, after=[V.last])
        SP.wait(om)
        stage2.close()
        assert counts["used"] == len(plan) and not ready

        with nc.Block() as block:
            @block.sync
            def _(_e):
                SP.play()

            @block.scalar
            def _(_e):
                S.play()

            @block.vector
            def _(_e):
                V.play()

            @block.tensor
            def _(_e):
                PE.play()

            @block.gpsimd
            def _(_e):
                G.play()


CONST, COLUMN = {}, {}


def constant_tables():
    parts, at = [], 0
    p = np.arange(P)

    def add(name, table):
        nonlocal at
        table = np.broadcast_to(np.asarray(table, np.float32), (P, np.shape(table)[-1]))
        CONST[name] = (at, table.shape[1])
        at += table.shape[1]
        parts.append(table)

    add("ident", np.eye(P))
    half = HD // 2
    rot = np.zeros((P, P))
    for m in range(P):
        if m % HD < half:
            rot[m + half, m] = -1.0
        else:
            rot[m - half, m] = 1.0
    add("rot", rot)
    inv = (np.float32(10000.0) ** (-np.arange(half, dtype=np.float32) / np.float32(half))).astype(np.float32)
    ang = np.arange(T, dtype=np.float32)[None, :] * inv[p % half][:, None]
    add("cos", np.cos(ang.astype(np.float64)))
    add("sin", np.sin(ang.astype(np.float64)))
    i = np.concatenate([np.arange(T), np.arange(P, T)])
    j = np.concatenate([np.zeros(T), np.full(P, P)])[None, :] + p[:, None]
    lag = i[None, :] - j
    tri = lag >= 0
    log_gamma = np.log1p(-np.exp2(-5.0 - np.arange(NH)))
    add("decay", np.concatenate([np.where(tri, np.exp(np.maximum(lag, 0) * g), 0) * HD ** -0.5 for g in log_gamma], 1))
    add("tri", tri)
    add("ones", np.ones((P, T)))
    add("power", np.full((P, 1), -0.5))
    add("iota8", np.arange(NE)[None, :])
    add("slots", np.arange(1, P + 1)[None, :])
    swap = np.zeros((P, P))
    swap[(p + HD) % P, p] = 1.0
    add("swap", swap)
    hr = ROT // 2
    rot2 = np.zeros((P, P))
    for m in range(P):
        r = m % HD
        if r < hr:
            rot2[m + hr, m] = -1.0
        elif r < ROT:
            rot2[m - hr, m] = 1.0
    inv2 = (np.float32(500000.0) ** (-np.arange(0, ROT, 2, dtype=np.float32) / np.float32(ROT))).astype(np.float32)
    add("invf", np.where(p % HD < ROT, inv2[(p % HD) % hr], 0.0)[:, None])
    add("rotrow", (p % HD < ROT).astype(np.float32)[:, None])
    add("restrow", (p % HD >= ROT).astype(np.float32)[:, None])
    q = p[:, None]
    d = q + P - np.arange(T)[None, :]
    k_, q_ = p[:, None], p[None, :]
    masks = [(k_ // (2 * b) == q_ // (2 * b)) & (k_ % (2 * b) < b) & (q_ % (2 * b) >= b) for b in GLA_LEVELS]
    masks.append(k_ == q_)
    causal = np.where(np.arange(P)[None, :] <= q, 0.0, -1e30)
    band = np.where((d >= 0) & (d < P), 0.0, -1e30)
    pm = []
    for w in WINDOWS:
        avg = np.where((lag >= 0) & (lag < w), 1.0 / np.minimum(i + 1, w)[None, :], 0.0) - (lag == 0)
        pm.append(avg)
    return (np.concatenate(parts, 1).astype(np.float32), np.concatenate(masks, 1).astype(np.int32),
            np.concatenate(pm + [rot2, causal, band], 1).astype(np.float32))


def column_parameters(v):
    parts, at = [], 0

    def add(name, l, table):
        nonlocal at
        if table.shape[0] < P:
            table = np.concatenate([table, np.zeros((P - table.shape[0], table.shape[1]), table.dtype)], 0)
        COLUMN[(name, l)] = at
        at += table.shape[1]
        parts.append(table)

    chunks = lambda r: r.reshape(-1, P).T
    for l in range(DEPTH):
        add("mix_g", l, chunks(v["mix_norm_g"][l]))
        add("ffn_g", l, chunks(v["ffn_norm_g"][l]))
        add("ssd_conv_w", l, chunks(v["ssd_conv_w"][l].reshape(-1)))
        add("ssd_conv_b", l, chunks(v["ssd_conv_b"][l]))
        add("ml_conv_w", l, chunks(v["ml_conv_w"][l].reshape(-1)))
        add("ml_conv_b", l, chunks(v["ml_conv_b"][l]))
        add("b_alpha", l, chunks(v["gla_b_alpha"][l]))
        add("w_alpha", l, v["gla_w_alpha"][l])
        for name, key in (("dt_bias", "ssd_dt_bias"), ("a_log", "ssd_a_log"), ("b_i", "ml_b_i"), ("b_f", "ml_b_f")):
            add(name, l, v[key][l].reshape(NH, 1))
        add("b_q", l, chunks(v["b_in_2"][l, 0:512]))
        k = chunks(v["b_in_2"][l, 512:640])
        add("b_k", l, k)
        add("pool_scale", l, chunks(v["pool_scale_2"][l]))
    add("router", 0, v["router_w"][0].reshape(KD, P, NE).transpose(1, 0, 2).reshape(P, KD * NE))
    add("c", 0, chunks(v["c_2"][0]))
    return np.concatenate(parts, 1)


def arrange(v):
    const, lmask, poolm = constant_tables()
    rows1 = np.concatenate([v["ret_norm_g"], v["ssd_norm_g"], v["gla_norm_g"], v["ml_norm_g"], v["ssd_d"]], 1)
    rows2 = [v["final_norm_g"]]
    for l in range(DEPTH):
        rows2 += [v[n][l] for n in ("g_pre_mix_2", "g_post_mix_2", "g_pre_ffn_2", "g_post_ffn_2")]
    arrays = {
        "const": const, "lmask": lmask, "poolm": poolm, "cols": column_parameters(v), "rows1": rows1,
        "rows2": np.stack(rows2), "x": v["x"], "positions": v["positions_2"], "ada_w": v["ada_w_2"],
        "ada_b": v["ada_b_2"], "w_in2": v["w_in_2"], "b_in2": v["b_in_2"], "sinks": v["sinks_2"],
        "pool_w": v["pool_w_2"], "w_out2": v["w_out_2"], "w_gate": v["w_gate_2"], "w_up": v["w_up_2"],
        "w_down": v["w_down_2"],
    }
    for n in ("w_in", "w_branch", "w_out", "ffn_w1", "ffn_w3", "ffn_w2", "moe_w1", "moe_w3", "moe_w2"):
        arrays[n] = v[n]
    return {n: np.ascontiguousarray(z) for n, z in arrays.items()}


def kernel(**inputs):
    import concourse.bacc as bacc
    from concourse.bass_utils import run_bass_kernel_spmd

    arrays = arrange({n: np.asarray(z) for n, z in inputs.items()})
    nc = bacc.Bacc("TRN2", target_bir_lowering=False, num_devices=1,
                    dynamic_dma_scratch_size=1024)
    aps = {n: nc.dram_tensor("in_" + n, z.shape, mybir.dt.from_np(z.dtype), kind="ExternalInput").ap()
           for n, z in arrays.items()}
    out = nc.dram_tensor("out_y", (1, T, D), F32, kind="ExternalOutput").ap()
    program(nc, aps, out)
    r = run_bass_kernel_spmd(nc, [{"in_" + n: z for n, z in arrays.items()}], core_ids=[0])
    return r.results[0]["out_y"]
```

```python
from contextlib import ExitStack

import numpy as np
import concourse.bass as bass
from concourse import mybir

F32 = mybir.dt.float32
I32 = mybir.dt.int32
U8 = mybir.dt.uint8
F32R = mybir.dt.float32r
ALU = mybir.AluOpType
ACT = mybir.ActivationFunctionType
AXX = mybir.AxisListType.X

P = 128
T = 256
NT = T // P
D = 1024
KD = D // P
DEPTH = 2
MIX = D // 4
NB = 4
NH = 4
HD = MIX // NH
EPS = 1e-6
FF = 2816
NFF = FF // P
NE = 8
BANK = 512
SC = T + P
GLA_DK = MIX // (2 * NH)
GLA_TAU = 16.0
CONV_K = 4
NSX, NMQ = 6, 4
PAD = CONV_K - 1
MOD = 6 * D
QH, KVH = 8, 2
ROT = HD // 4
WINDOWS = (2, 4, 8, 16)
GLA_LEVELS = (64, 32, 16, 8, 4, 2, 1)

COLS = {}
_at = 0
for _name, _n in (("rq", 256), ("rk", 256), ("rv", 256), ("rg", 256), ("sz", 256), ("sxbc", 768),
                  ("sdt", 4), ("gq", 128), ("gk", 128), ("gv", 256), ("gr", 256), ("ga", 16),
                  ("mqk", 512), ("mv", 256), ("mo", 256), ("mi", 4), ("mf", 4), ("mgate", 4096)):
    COLS[_name] = _at
    _at += _n

PIECE = 2048
NRAW = 5
NSPLIT = 3
AHEAD = 2


class Mark:

    def __init__(self, sem, value):
        self.sem, self.value = sem, value


class Either:

    def __init__(self, flag, limit, ways):
        self.flag, self.limit, self.ways = flag, limit, ways


class Queue:

    def __init__(self, sem, engine, chained):
        self.sem, self.engine, self.wait_ge, self.chained = sem, engine, engine.wait_ge, chained
        self.count, self.steps, self.seen, self.last = 0, [], {}, None

    def wait(self, *marks):
        for m in marks:
            if m is not None and self.seen.get(m.sem, 0) < m.value:
                self.seen[m.sem] = m.value
                self.steps.append((self.wait_ge, (m.sem, m.value), {}, None, 0))

    def run(self, op, *args, after=(), mark=True, own=None, **kw):
        if self.chained if own is None else own:
            self.wait(self.last)
        self.wait(*after)
        if not mark:
            self.steps.append((op, args, kw, None, 0))
            return None
        self.count += 1
        self.steps.append((op, args, kw, self.sem, 1))
        self.last = Mark(self.sem, self.count)
        return self.last

    def dma(self, op, out, in_, sem, after=()):
        self.wait(*after)
        sem[1] += 16
        self.steps.append((op, (out, in_), {}, sem[0], 16))
        return Mark(sem[0], sem[1])

    def play(self, steps=None):
        for step in self.steps if steps is None else steps:
            if isinstance(step, Either):
                value = self.engine.value_load(step.flag)
                with self.engine.If(value < step.limit):
                    self.play(step.ways[0])
                with self.engine.Else():
                    self.play(step.ways[1])
                continue
            op, args, kw, sem, by = step
            i = op(*args, **kw)
            if sem is not None:
                i.then_inc(sem, by)


class Slots:

    def __init__(self, items):
        self.free = [(item, ()) for item in items]

    def take(self):
        return self.free.pop(0)

    def give(self, item, *marks):
        self.free.append((item, marks))


def program(nc, a, out):
    with ExitStack() as ctx:
        def sb(stage, name, n, dt=F32):
            return stage.enter_context(nc.sbuf_tensor(name, [P, n], dt))[:, :]

        def sem(name):
            return ctx.enter_context(nc.semaphore(name))

        PE = Queue(sem("tensor_done"), nc.tensor, False)
        S = Queue(sem("scalar_done"), nc.scalar, True)
        V = Queue(sem("vector_done"), nc.vector, True)
        G = Queue(sem("gpsimd_done"), nc.gpsimd, True)
        SP = Queue(sem("sync_done"), nc.sync, False)
        tt, ts, stt = nc.vector.tensor_tensor, nc.vector.tensor_scalar, nc.vector.scalar_tensor_tensor
        vcopy, act, mm = nc.vector.tensor_copy, nc.scalar.activation, nc.tensor.matmul
        scan, reduce = nc.vector.tensor_tensor_scan, nc.vector.tensor_reduce
        tok3 = lambda ap: ap.rearrange("p (t n) -> p t n", t=NT)
        heads = lambda ap: ap.rearrange("p (t h n) -> p t h n", t=NT, h=NH)
        tiles = lambda ap: ap.rearrange("p (c t) -> p c t", t=T)
        rep = lambda ap, n: ap.unsqueeze(1).broadcast_to([P, n, ap.shape[-1]])

        x = sb(ctx, "x", NT * D)
        xn = sb(ctx, "xn", NT * D)
        hThi = sb(ctx, "hThi", KD * T, F32R)
        hTlo = sb(ctx, "hTlo", KD * T, F32R)
        raw = sb(ctx, "raw", NRAW * PIECE)
        whi = sb(ctx, "whi", NSPLIT * PIECE, F32R)
        wlo = sb(ctx, "wlo", NSPLIT * PIECE, F32R)
        cst = sb(ctx, "cst", a["const"].shape[1])
        lmask = sb(ctx, "lmask", a["lmask"].shape[1], U8)
        cols = sb(ctx, "cols", a["cols"].shape[1])
        rows_t = sb(ctx, "rows_t", 4 * MIX + NH)
        small = sb(ctx, "small", 420)
        flag = sb(ctx, "most_tokens", 1, I32)
        cs_, sn_ = sb(ctx, "rope_cos", T), sb(ctx, "rope_sin", T)
        chi, clo = sb(ctx, "chi", KD * 4, F32R), sb(ctx, "clo", KD * 4, F32R)
        mrow = rows_t[:, 0:3 * P]
        mod_raw = nc.dram_tensor("modulation_raw", (DEPTH, MOD), F32, kind="Internal").ap()
        mod_ready = nc.dram_tensor("modulation_ready", (DEPTH, MOD), F32, kind="Internal").ap()
        banks = [ctx.enter_context(nc.psum_tensor(f"bank{i}", [P, BANK], F32)) for i in range(8)]
        x3, xn3 = tok3(x), tok3(xn)
        hi3, lo3 = tiles(hThi), tiles(hTlo)
        used = [0]

        def tiny(n):
            used[0] += n
            assert used[0] <= 420
            return small[:, used[0] - n:used[0]]

        def const(name):
            o, n = CONST[name]
            return cst[:, o:o + n]

        def col(name, l, i=0, n=1, rows=P):
            o = COLUMN[(name, l)] + i
            return cols[0:rows, o:o + n]

        plan = []

        def chunk_rows(w, k0, nk, c0, n):
            return w[k0 * P:(k0 + nk) * P, c0:c0 + n].rearrange("(k p) n -> p k n", p=P)

        def plan_half(key, w, c0, lo_on="V"):
            for k0 in (0, 4):
                plan.append((key, lo_on, PIECE, [(lambda ap: ap.rearrange("p (k n) -> p k n", k=4),
                                                  chunk_rows(w, k0, 4, c0, BANK))]))

        def plan_full(key, w, c0, lo_on="V"):
            plan.append((key, lo_on, PIECE, [(lambda ap: ap.rearrange("p (k n) -> p k n", k=KD),
                                              chunk_rows(w, 0, KD, c0, 2 * P))]))

        def plan_rows(key, w, r0, lo_on="V"):
            plan.append((key, lo_on, PIECE, [(lambda ap: ap.rearrange("p (c n) -> p c n", c=2),
                                              w[r0:r0 + 2 * P, :].rearrange("(c p) n -> p c n", p=P))]))

        def plan_strips(key, w, strips):
            n, loads, at = sum(m for _, m in strips), [], 0
            for c0, m in strips:
                loads.append((lambda ap, at=at, m=m: ap[:, 0:KD * n].rearrange("p (k n) -> p k n", k=KD)[:, :, at:at + m],
                              chunk_rows(w, 0, KD, c0, m)))
                at += m
            plan.append((key, "V", KD * n, loads))

        def plan_ff(key, *nets):
            todo = [(net, c) for net in nets for c in range(FF // (2 * P))]
            for i in range(len(todo) + 2):
                if i < len(todo):
                    (w1, w3, _), c = todo[i]
                    for k0 in (0, 4):
                        view = lambda ap, w: ap.rearrange("p (k w n) -> p k w n", k=4, w=2)[:, :, w, :]
                        plan.append((key, "V", PIECE, [
                            (lambda ap, view=view: view(ap, 0), chunk_rows(w1, k0, 4, c * 2 * P, 2 * P)),
                            (lambda ap, view=view: view(ap, 1), chunk_rows(w3, k0, 4, c * 2 * P, 2 * P))]))
                if i >= 2:
                    (_, _, w2), c = todo[i - 2]
                    plan_rows(key, w2, c * 2 * P)

        raws = Slots([(raw[:, i * PIECE:(i + 1) * PIECE], [sem(f"piece{i}_in"), 0]) for i in range(NRAW)])
        splits = Slots([(whi[:, i * PIECE:(i + 1) * PIECE], wlo[:, i * PIECE:(i + 1) * PIECE]) for i in range(NSPLIT)])
        ready, counts = [], {"split": 0, "used": 0}

        def split_next():
            key, lo_on, n, loads = plan[counts["split"]]
            counts["split"] += 1
            (dst, cell), freed = raws.take()
            for view, src in loads:
                m = SP.dma(nc.sync.dma_start, view(dst), src, cell, after=freed)
            (hi, lo), parted = splits.take()
            s = S.run(act, hi[:, 0:n], dst[:, 0:n], ACT.Copy, after=[m, *parted], own=False)
            q, sub = (V, tt) if lo_on == "V" else (G, nc.gpsimd.tensor_tensor)
            v = q.run(sub, lo[:, 0:n], dst[:, 0:n], hi[:, 0:n].bitcast(F32), ALU.subtract, after=[s, m, *parted],
                      own=False)
            raws.give((dst, cell), v)
            ready.append((key, (hi, lo), v))

        def piece(key):
            counts["used"] += 1
            while counts["split"] < min(counts["used"] + AHEAD, len(plan)):
                split_next()
            k, parts, m = ready.pop(0)
            assert k == key, (k, key)
            PE.wait(m)
            return parts

        def finished(parts, m):
            splits.give(parts, m)

        pool = Slots(banks)

        def group(dst, pairs, after=(), start=True, stop=True):
            PE.wait(*after)
            m = None
            for i, (l_, r_) in enumerate(pairs):
                last = i == len(pairs) - 1
                m = PE.run(mm, dst, l_, r_, start=start and i == 0, stop=stop and last, mark=last)
            return m

        def product(dst, quads, start=True, stop=True):
            return group(dst, [z for (lh, ll), (rh, rl) in quads for z in ((lh, rh), (lh, rl), (ll, rh))],
                         start=start, stop=stop)

        s_const, s_rows, s_x, s_out, s_att = ([sem(n), 0] for n in (
            "constants_in", "row_parameters_in", "x_in", "result_out", "attention_tables_in"))
        s_pos, s_row, s_mrow, s_mout, s_gain = ([sem(n), 0] for n in (
            "positions_in", "modulation_row_out", "modulation_rows_in", "modulation_out", "final_gain_in"))
        s_mod = [[sem(f"modulation_in_{i}"), 0] for i in range(2)]
        x_in = SP.dma(nc.sync.dma_start, x3, a["x"].rearrange("o (t p) d -> p (o t) d", p=P), s_x)
        cm = S.dma(nc.scalar.dma_start, cst, a["const"], s_const)
        cm = S.dma(nc.scalar.dma_start, cols, a["cols"], s_const)
        wide = xn[:, 0:lmask.shape[1]].bitcast(I32)
        cm = S.dma(nc.scalar.dma_start, wide, a["lmask"], s_const)
        for q in (PE, V, S, G, SP):
            q.wait(cm)
        S.wait(V.run(vcopy, lmask, wide))
        V.wait(x_in)
        S.wait(x_in)
        ident = const("ident")
        stat = tiny(16)
        c4 = [z.rearrange("p (k m) -> p k m", k=KD) for z in (chi, clo)]
        def marks():
            return [q.last for q in (PE, V, S, G)]

        def join():
            lasts = marks()
            for q in (PE, V, S, G):
                q.wait(*lasts)

        def inverse_root(dst, sums, n, ready_):
            G.run(nc.gpsimd.tensor_scalar, dst, sums, 1.0 / n, EPS, ALU.mult, ALU.add, after=[ready_])
            return G.run(nc.gpsimd.tensor_tensor, dst, dst, const("power").broadcast_to(list(dst.shape)), ALU.pow)

        def rms(src3, dst3, after=(None, None)):
            roots = []
            for t in range(NT):
                m = S.run(act, dst3[:, t, :], src3[:, t, :], ACT.Square, accum_out=stat[:, t:t + 1], after=[after[t]])
                roots.append(inverse_root(stat[:, 4 + t:5 + t], stat[:, t:t + 1], D, m))
            return [V.run(ts, dst3[:, t, :], src3[:, t, :], stat[:, 4 + t:5 + t], None, ALU.mult, after=[roots[t]])
                    for t in range(NT)]

        def to_parts(hi, lo, src, m, scale=None):
            s = S.run(act, hi, src, ACT.Copy, after=[m], own=False, **({} if scale is None else {"scale": scale}))
            if scale is None:
                return V.run(tt, lo, src, hi.bitcast(F32), ALU.subtract, after=[m, s], own=False)
            return V.run(stt, lo, src, scale, hi.bitcast(F32), ALU.mult, ALU.subtract, after=[m, s], own=False)

        def to_features(src3, ms, scale=None, reads=()):
            S.wait(*reads)
            V.wait(*reads)
            ends = []
            for t in range(NT):
                ts_ = slice(t * P, (t + 1) * P)
                for k in range(0, KD, 4):
                    bank, freed = pool.take()
                    PE.wait(*freed, ms[t])
                    for j in range(4):
                        p_ = PE.run(nc.tensor.transpose, bank[:, j * P:(j + 1) * P],
                                    src3[:, t, (k + j) * P:(k + j + 1) * P], ident, mark=(j == 3))
                    if scale is None or isinstance(scale, float):
                        v = to_parts(hi3[:, k:k + 4, ts_], lo3[:, k:k + 4, ts_],
                                     bank[:, :].rearrange("p (c n) -> p c n", c=4), p_, scale)
                    else:
                        for j in range(4):
                            s = S.run(act, hi3[:, k + j, ts_], bank[:, j * P:(j + 1) * P], ACT.Copy, scale=scale(k + j),
                                      after=[p_], own=False)
                        for j in range(4):
                            v = V.run(stt, lo3[:, k + j, ts_], bank[:, j * P:(j + 1) * P], scale(k + j),
                                      hi3[:, k + j, ts_].bitcast(F32), ALU.mult, ALU.subtract, after=[s], own=False)
                    pool.give(bank, v)
                ends.append(v)
            return ends

        def stat_tokens(k, t):
            return hi3[:, k, t * P:(t + 1) * P], lo3[:, k, t * P:(t + 1) * P]

        def project_tokens(key, hm):
            out_ = []
            for half in range(2):
                parts = piece(key)
                w = [z.rearrange("p (k n) -> p k n", k=4) for z in parts]
                for t in range(NT):
                    PE.wait(hm[t])
                    if half == 0:
                        bank, freed = pool.take()
                        PE.wait(*freed)
                        out_.append([bank, None])
                    out_[t][1] = product(out_[t][0][:, :], [(stat_tokens(4 * half + k, t), (w[0][:, k], w[1][:, k]))
                                                            for k in range(4)], start=half == 0, stop=half == 1)
                finished(parts, out_[-1][1])
            return out_

        def project_features(w, c, hm, bank, at, rows=P):
            PE.wait(*hm)
            return product(bank[0:rows, at:at + T], [((w[0][:, k, c:c + rows], w[1][:, k, c:c + rows]),
                                                      (hi3[:, k, :], lo3[:, k, :])) for k in range(KD)])

        def full(parts, n=2 * P):
            return [z[:, 0:KD * n].rearrange("p (k n) -> p k n", k=KD) for z in parts]

        def feed_forward(stage, key, nt, nets, pool_a, pool_y, tag="", between=lambda: None):
            sil = Slots([sb(stage, f"silu{i}_{key}{tag}", nt * 2 * P) for i in range(2)])
            gts = Slots([sb(stage, f"gated{i}_{key}{tag}", nt * 2 * P) for i in range(2)])
            gparts = Slots([(sb(stage, f"gatedThi{i}_{key}{tag}", 2 * nt * P, F32R),
                             sb(stage, f"gatedTlo{i}_{key}{tag}", 2 * nt * P, F32R)) for i in range(2)])
            nchunk = FF // (2 * P)
            todo = [(net, c) for net in nets for c in range(nchunk)]
            gated, turned, ys = {}, {}, []
            for i in range(len(todo) + 2):
                if i < len(todo):
                    (tokens, tokens_ready, _), c = todo[i]
                    ups = []
                    for half in range(2):
                        parts = piece(key)
                        w = [z.rearrange("p (k n) -> p k n", k=4) for z in parts]
                        for t in range(nt):
                            if c == 0:
                                PE.wait(tokens_ready()[t])
                            if half == 0:
                                bank, freed = pool_a.take()
                                PE.wait(*freed)
                                ups.append([bank, None])
                            ups[t][1] = product(ups[t][0][:, :], [(tokens(4 * half + k, t), (w[0][:, k], w[1][:, k]))
                                                                  for k in range(4)], start=half == 0, stop=half == 1)
                        finished(parts, ups[-1][1])
                    sg, f1 = sil.take()
                    gt, f2 = gts.take()
                    S.wait(*f1)
                    V.wait(*f2)
                    for t, (bank, m) in enumerate(ups):
                        cs = slice(t * 2 * P, (t + 1) * 2 * P)
                        s = S.run(act, sg[:, cs], bank[:, 0:2 * P], ACT.Silu, after=[m], own=False)
                        v = V.run(tt, gt[:, cs], sg[:, cs], bank[:, 2 * P:4 * P], ALU.mult, after=[s, m], own=False)
                        pool_a.give(bank, v)
                    sil.give(sg, v)
                    gated[i] = (gt, v)
                if i >= 2:
                    (_, _, finish), c = todo[i - 2]
                    if c == 0:
                        ys = [(t, hf, *pool_y.take()) for t in range(nt) for hf in range(2)]
                        PE.wait(*[m for y in ys for m in y[3]])
                    parts = piece(key)
                    w = [z.rearrange("p (c n) -> p c n", c=2) for z in parts]
                    g_parts, gm = turned.pop(i - 2)
                    PE.wait(gm)
                    g3 = [z.rearrange("p (c t) -> p c t", c=2) for z in g_parts]
                    marks_ = []
                    for t, hf, bank, _ in ys:
                        ts_, cs = slice(t * P, (t + 1) * P), slice(hf * BANK, (hf + 1) * BANK)
                        m = product(bank[:, :], [((g3[0][:, j, ts_], g3[1][:, j, ts_]), (w[0][:, j, cs], w[1][:, j, cs]))
                                                 for j in range(2)], start=c == 0, stop=c == nchunk - 1)
                        marks_.append(m)
                    finished(parts, m)
                    gparts.give(g_parts, m)
                    if c == nchunk - 1:
                        finish([(t, hf, bank, m_) for (t, hf, bank, _), m_ in zip(ys, marks_)])
                if 1 <= i <= len(todo):
                    gt, v = gated.pop(i - 1)
                    g_parts, freed = gparts.take()
                    bank, bank_freed = pool_a.take()
                    PE.wait(v, *bank_freed)
                    for j in range(2):
                        for t in range(nt):
                            m = PE.run(nc.tensor.transpose, bank[:, (j * nt + t) * P:(j * nt + t + 1) * P],
                                       gt[:, t * 2 * P + j * P:t * 2 * P + (j + 1) * P], ident,
                                       mark=(j == 1 and t == nt - 1))
                    gts.give(gt, m)
                    S.wait(*freed)
                    V.wait(*freed)
                    v = to_parts(*g_parts, bank[:, 0:2 * nt * P], m)
                    pool_a.give(bank, v)
                    turned[i - 1] = (g_parts, v)
                between()

        def split_banks():
            assert len(pool.free) == 8
            first, second = Slots([]), Slots([])
            first.free, second.free = pool.free[:4], pool.free[4:]
            return first, second

        def rejoin_banks(ring, outputs, m):
            pool.free = ring.free + [(bank, (m,)) for _, _, bank, _ in outputs]

        def either(flag, limit, flag_ready, ways):
            queues = (PE, S, V, G, SP)
            for q in queues:
                q.wait(flag_ready)
            start = [(q.steps, q.count, dict(q.seen), q.last) for q in queues]
            rings = [(r_, list(r_.free)) for r_ in (raws, splits)]
            cells = [item[1] for item, _ in raws.free]
            cell_counts = [c_[1] for c_ in cells]
            ready_before, counts_before = list(ready), dict(counts)
            ends = []
            for way in ways:
                for q, (_, count, seen, last) in zip(queues, start):
                    q.steps, q.count, q.seen, q.last = [], count, dict(seen), last
                for r_, free in rings:
                    r_.free = list(free)
                for c_, n in zip(cells, cell_counts):
                    c_[1] = n
                ready[:] = ready_before
                counts.update(counts_before)
                way()
                join()
                ends.append(([q.steps for q in queues], [q.count for q in queues], [c_[1] for c_ in cells],
                             dict(counts)))
            assert ends[0][2:] == ends[1][2:]
            final = {}
            for i, (q, (steps, _, seen, _)) in enumerate(zip(queues, start)):
                q.count = max(end[1][i] for end in ends)
                q.last = Mark(q.sem, q.count)
                final[q.sem] = q.last
                for end in ends:
                    if q.count > end[1][i]:
                        end[0][i].append((q.engine.sem_inc, (q.sem, q.count - end[1][i]), {}, None, 0))
                q.steps, q.seen = steps + [Either(flag, limit, [end[0][i] for end in ends])], dict(seen)
            late = lambda marks_: tuple(m if m is None else final.get(m.sem, m) for m in marks_)
            for r_ in (raws, splits):
                r_.free = [(item, late(marks_)) for item, marks_ in r_.free]
            ready[:] = [(key, parts, *late([m])) for key, parts, m in ready]

        def experts(l, normed, gain, filler):
            with ExitStack() as stage:
                hf32 = sb(stage, "router_tokens", KD * T)
                h3 = tiles(hf32)
                for k in range(0, KD, 2):
                    bank, freed = pool.take()
                    PE.wait(*freed, *normed)
                    for j in range(2):
                        for t in range(NT):
                            p_ = PE.run(nc.tensor.transpose, bank[:, (2 * j + t) * P:(2 * j + t + 1) * P],
                                        xn3[:, t, (k + j) * P:(k + j + 1) * P], ident, mark=(j == 1 and t == 1))
                    for j in range(2):
                        v = V.run(ts, h3[:, k + j, :], bank[:, j * T:(j + 1) * T], gain(k + j), None, ALU.mult,
                                  after=[p_], own=False)
                    pool.give(bank, v)
                bank, freed = pool.take()
                PE.wait(*freed, v)
                for t in range(NT):
                    m = group(bank[:, t * NE:(t + 1) * NE],
                              [(h3[:, k, t * P:(t + 1) * P], col("router", 0, k * NE, NE)) for k in range(KD)])
                filler()
                xhi, xlo = tok3(hThi), tok3(hTlo)
                s = S.run(act, hThi, xn, ACT.Copy, after=normed, own=False)
                G.run(nc.gpsimd.tensor_tensor, hTlo, xn, hThi.bitcast(F32), ALU.subtract, after=[s, *normed])
                lg, top, gate8, taken = tiny(NT * NE), tiny(NT * NE), tiny(NT * NE), tiny(NT * NE)
                idx = stage.enter_context(nc.sbuf_tensor("idx", [P, NT * NE], mybir.dt.uint32))
                idf, w12 = tiny(NT * NE), tiny(NT * 6)
                v = V.run(vcopy, lg, bank[:, 0:NT * NE], after=[m])
                pool.give(bank, v)
                for t in range(NT):
                    e8 = slice(t * NE, (t + 1) * NE)
                    V.run(nc.vector.max, top[:, e8], lg[:, e8])
                    V.run(nc.vector.max_index, idx[:, e8], top[:, e8], lg[:, e8])
                V.run(vcopy, idf, idx[:, :])
                filler()
                w3_, top3 = (z.rearrange("p (t n) -> p t n", t=NT) for z in (w12, top))
                v = V.run(tt, w3_[:, :, 0], top3[:, :, 1], top3[:, :, 0], ALU.subtract)
                s = S.run(act, w3_[:, :, 1], w3_[:, :, 0], ACT.Exp, after=[v])
                V.run(ts, w3_[:, :, 2], w3_[:, :, 1], 1.0, None, ALU.add, after=[s])
                V.run(nc.vector.reciprocal, w3_[:, :, 3], w3_[:, :, 2])
                V.run(tt, w3_[:, :, 4], w3_[:, :, 3], w3_[:, :, 1], ALU.mult)
                for t in range(NT):
                    e8 = slice(t * NE, (t + 1) * NE)
                    V.run(ts, taken[:, e8], const("iota8"), idf[:, t * NE:t * NE + 1], None, ALU.is_equal)
                    V.run(ts, gate8[:, e8], taken[:, e8], w3_[:, t, 3:4], None, ALU.mult)
                    V.run(ts, lg[:, e8], const("iota8"), idf[:, t * NE + 1:t * NE + 2], None, ALU.is_equal)
                    V.run(stt, gate8[:, e8], lg[:, e8], w3_[:, t, 4:5], gate8[:, e8], ALU.mult, ALU.add)
                    v = V.run(tt, taken[:, e8], taken[:, e8], lg[:, e8], ALU.add)
                tri, slot_of = const("tri"), tiny(NT * NE)
                most = tiny(1)
                bank, freed = pool.take()
                group(bank[:, 0:NE], [(tri[:, 0:P], taken[:, 0:NE])], after=[*freed, v])
                group(bank[:, NE:2 * NE], [(tri[:, P:T], taken[:, 0:NE]), (tri[:, T:SC], taken[:, NE:2 * NE])])
                m = group(bank[0:1, 2 * NE:3 * NE], [(const("ones")[:, 0:1], taken[:, 0:NE]),
                                                     (const("ones")[:, 0:1], taken[:, NE:2 * NE])])
                filler()
                V.run(reduce, most[0:1, :], bank[0:1, 2 * NE:3 * NE], AXX, ALU.max, after=[m])
                V.run(vcopy, flag[0:1, :], most[0:1, :])
                v = V.run(tt, slot_of, taken, bank[:, 0:NT * NE], ALU.mult)
                pool.give(bank, v)
                join()
                gate = lambda t, e: gate8[:, t * NE + e:t * NE + e + 1]
                either(flag[0:1, :], P + 1, v, [lambda: sparse_experts(gate, slot_of, xhi, xlo, gain),
                                                lambda: dense_experts(gate, xn3, gain)])

        def dense_experts(gate, tokens3, gain):
            pool.free = [(b, ()) for b in banks]
            with ExitStack() as stage:
                hm = to_features(tokens3, [V.last] * NT, scale=gain, reads=[PE.last])
                join()
                pool_y = Slots(banks[0:4])

                def finish(e):
                    def add_gated(ys):
                        V.wait(V.last)
                        for t, hf, bank, ym in ys:
                            xo = x3[:, t, hf * BANK:(hf + 1) * BANK]
                            v = V.run(stt, xo, bank[:, :], gate(t, e), xo, ALU.mult, ALU.add, after=[ym], own=False)
                            pool_y.give(bank, v)
                    return add_gated

                feed_forward(stage, "moe", NT, [(stat_tokens, lambda: hm, finish(e)) for e in range(NE)],
                             Slots(banks[4:8]), pool_y, tag="_dense")

        def sparse_experts(gate, slot_of, xhi, xlo, gain):
            with ExitStack() as stage:
                one = lambda name, n, dt=F32: sb(stage, name, n, dt)
                pick, put = one("pick", NT * NE * P, F32R), one("put", NE * T, F32R)
                pick4 = pick.rearrange("p (t e n) -> p t e n", t=NT, e=NE)
                put3 = put.rearrange("p (e t) -> p e t", e=NE)
                gathered = [(one(f"slots_hi{i}", KD * 2 * P, F32R), one(f"slots_lo{i}", KD * 2 * P, F32R))
                            for i in range(2)]
                yhi, ylo = one("outputs_hi", D, F32R), one("outputs_lo", D, F32R)
                pool_y, pool_a, side = Slots(banks[0:2]), Slots(banks[2:6]), Slots(banks[6:8])
                for t in range(NT):
                    v = V.run(tt, pick4[:, t], rep(const("slots"), NE),
                              slot_of[:, t * NE:(t + 1) * NE].unsqueeze(2).broadcast_to([P, NE, P]), ALU.is_equal)
                picked = v
                slots_ready, slots_read, y_read = {}, {}, [None]

                def gather(pair):
                    hi, lo = (z.rearrange("p (k n) -> p k n", k=KD) for z in gathered[pair % 2])
                    before = slots_read.get(pair - 2)
                    PE.wait(picked)
                    for k in range(0, KD, 2):
                        bank, freed = side.take()
                        PE.wait(*freed, G.last)
                        for j in range(2):
                            fs = slice((k + j) * P, (k + j + 1) * P)
                            m = group(bank[:, j * T:(j + 1) * T],
                                      [(z[:, t, fs], pick4[:, t, 2 * pair:2 * pair + 2, :])
                                       for t in range(NT) for z in (xhi, xlo)])
                        S.wait(before)
                        V.wait(before)
                        for j in range(2):
                            s = S.run(act, hi[:, k + j, :], bank[:, j * T:(j + 1) * T], ACT.Copy, scale=gain(k + j),
                                      after=[m], own=False)
                        for j in range(2):
                            v = V.run(stt, lo[:, k + j, :], bank[:, j * T:(j + 1) * T], gain(k + j),
                                      hi[:, k + j, :].bitcast(F32), ALU.mult, ALU.subtract, after=[s], own=False)
                        side.give(bank, v)
                        slots_ready[pair] = v
                        yield

                def make_put(pair):
                    bank, freed = side.take()
                    PE.wait(*freed)
                    for j in range(2):
                        for t in range(NT):
                            m = PE.run(nc.tensor.transpose, bank[:, (2 * j + t) * P:(2 * j + t + 1) * P],
                                       pick4[:, t, 2 * pair + j, :].bitcast(F32), ident, mark=(j == 1 and t == 1))
                    s = S.run(act, put3[:, 2 * pair:2 * pair + 2, :], tiles(bank[:, :]), ACT.Copy, after=[m], own=False)
                    side.give(bank, s)
                    put_ready[pair] = s
                    yield

                put_ready = {}

                def scatter(e, y_ready):
                    PE.wait(y_ready, put_ready[e // 2])
                    for t in range(NT):
                        for hf in range(2):
                            cs = slice(hf * BANK, (hf + 1) * BANK)
                            bank, freed = side.take()
                            m = group(bank[:, :], [(put3[:, e, t * P:(t + 1) * P], z[:, cs]) for z in (yhi, ylo)],
                                      after=freed)
                            xo = x3[:, t, cs]
                            v = V.run(stt, xo, bank[:, :], gate(t, e), xo, ALU.mult, ALU.add, after=[m], own=False)
                            side.give(bank, v)
                        y_read[0] = m
                        yield

                todo = []

                def between():
                    if todo and next(todo[0], 0) is not None:
                        todo.pop(0)
                        between()

                def finish(e):
                    def put_back(ys):
                        slots_read[e // 2] = ys[-1][3]
                        S.wait(y_read[0])
                        V.wait(y_read[0])
                        for _, hf, bank, ym in ys:
                            cs = slice(hf * BANK, (hf + 1) * BANK)
                            v = to_parts(yhi[:, cs], ylo[:, cs], bank[:, :], ym)
                            pool_y.give(bank, v)
                        todo.append(scatter(e, v))
                        if e % 2 == 1 and e // 2 + 2 < NE // 2:
                            todo.append(gather(e // 2 + 2))
                    return put_back

                def tokens(e):
                    z3 = [z.rearrange("p (k n) -> p k n", k=KD) for z in gathered[(e // 2) % 2]]
                    return lambda k, t: tuple(z[:, k, (e % 2) * P:(e % 2 + 1) * P] for z in z3)

                for _ in gather(0):
                    pass
                todo += [make_put(i) for i in range(NE // 2)] + [gather(1)]
                feed_forward(stage, "moe", 1, [(tokens(e), lambda e=e: [slots_ready[e // 2]], finish(e)) for e in range(NE)],
                             pool_a, pool_y, tag="_sparse", between=between)
                while todo:
                    between()

        order = (0, 1, 3, 2)
        branch_items = ["p1", "g0", "d0", "p2", "d1", "g1", "a0", "d2", "p3", "d3", "g2", "d4", "a1", "d5", "g3", "d6",
                        "a2", "d7"]
        fillers = {("branch", 0): 8, ("merged", 0): 1, ("out", 0): 1, ("late", 0): 2,
                   ("head", 1): 2, ("merged", 1): 1, ("out", 1): 1, ("late", 1): 3, ("second", 0): 2, ("mixed", 0): 3}
        filler_of = {}
        chunks_ = iter([(l, c) for l in range(DEPTH) for c in range(MOD // BANK)])
        for place, n in fillers.items():
            filler_of[place] = [next(chunks_) for _ in range(n)]

        def plan_modulation(place):
            for l, c in filler_of.get(place, []):
                plan_half("d", a["ada_w"][l], c * BANK, lo_on="G")

        def fill(place, mod_row):
            for l, c in filler_of.get(place, []):
                modulation(l, c, mod_row)


        def plan_project(l, b):
            w = a["w_in"][l]
            if b == 0:
                plan_full("p0", w, COLS["rq"])
                plan_full("p0", w, COLS["rk"])
                plan_half("p0", w, COLS["rv"], lo_on="G")
            elif b == 1:
                for i in range(3):
                    plan_full("p1", w, COLS["sxbc"] + i * 2 * P, lo_on="G" if i == 1 else "V")
                plan_full("p1", w, COLS["sz"])
            elif b == 2:
                plan_full("p2", w, COLS["mqk"])
                plan_full("p2", w, COLS["mqk"] + 2 * P)
                plan_half("p2", w, COLS["mv"], lo_on="G")
            else:
                plan_full("p3", w, COLS["gq"], lo_on="G")
                plan_half("p3", w, COLS["gv"], lo_on="G")

        for l in range(DEPTH):
            plan_modulation(("head", l))
            plan_strips("z", a["w_in"][l], [(COLS[name], 32) for name in ("sdt", "ga", "mi", "mf")])
            plan_project(l, 0)
            for item in branch_items + ["a3"]:
                b = int(item[1])
                if item[0] == "p":
                    plan_project(l, b)
                elif item[0] == "d":
                    if l == 0:
                        plan_half("d", a["ada_w"][l], b * BANK, lo_on="G")
                elif item[0] == "g":
                    for hf in range(2):
                        plan_half(item, a["w_in"][l], COLS["mgate"] + order[b] * D + hf * BANK, lo_on="G")
                else:
                    plan_rows(item, a["w_branch"][l][order[b]], 0)
            plan_modulation(("merged", l))
            for hf in range(2):
                plan_half("wout", a["w_out"][l], hf * BANK)
            plan_modulation(("out", l))
            plan_modulation(("late", l))
            if l % 2 == 0:
                plan_ff("ffn", (a["ffn_w1"][l // 2], a["ffn_w3"][l // 2], a["ffn_w2"][l // 2]))
            else:
                plan_ff("moe", *[(a["moe_w1"][l // 2, e], a["moe_w3"][l // 2, e], a["moe_w2"][l // 2, e])
                                 for e in range(NE)])
        for l in range(DEPTH):
            plan_modulation(("second", l))
            plan_full("q2", a["w_in2"][l], 0)
            plan_full("q2", a["w_in2"][l], 2 * P)
            plan.append(("kv2", "V", PIECE, [(lambda ap: ap.rearrange("p (k n) -> p k n", k=KD),
                                              chunk_rows(a["w_in2"][l], 0, KD, 512, 2 * P))]))
            plan_half("u2", a["w_in2"][l], 768)
            for hf in range(2):
                plan_half("wout2", a["w_out2"][l], hf * BANK)
            plan_modulation(("mixed", l))
            plan_ff("ffn2", (a["w_gate"][l], a["w_up"][l], a["w_down"][l]))

        def rope_tables(angles):
            ang, turn, rest = (angles[:, i * T:(i + 1) * T] for i in range(3))
            posi = angles[:, 3 * T:4 * T].bitcast(I32)
            rm = S.dma(nc.scalar.dma_start, posi, a["positions"].broadcast_to([P, T]), s_pos)
            V.run(vcopy, ang, posi, after=[rm])
            V.run(ts, ang, ang, const("invf"), None, ALU.mult)
            two_pi = 2 * np.pi
            part1 = 6.28125
            part2 = float(np.round((two_pi - part1) * 2 ** 20) / 2 ** 20)
            part3 = float(two_pi - part1 - part2)
            to_integer = 1.5 * 2 ** 23
            pi32 = float(np.float32(np.pi))

            def sine(dst, shift):
                V.run(ts, turn, ang, 1.0 / two_pi, shift / two_pi, ALU.mult, ALU.add)
                V.run(ts, turn, turn, to_integer, None, ALU.add)
                V.run(ts, turn, turn, to_integer, None, ALU.subtract)
                V.run(stt, rest, turn, -part1, ang, ALU.mult, ALU.add)
                V.run(stt, rest, turn, -part2, rest, ALU.mult, ALU.add)
                V.run(stt, rest, turn, -part3, rest, ALU.mult, ALU.add)
                V.run(ts, rest, rest, shift, pi32, ALU.add, ALU.min)
                v = V.run(ts, rest, rest, -pi32, None, ALU.max)
                yield
                s = S.run(act, dst, rest, ACT.Sin, after=[v], own=False)
                yield
                V.wait(s)

            yield from sine(sn_, 0.0)
            yield from sine(cs_, float(np.pi / 2))
            V.run(ts, sn_, sn_, const("rotrow"), None, ALU.mult)
            V.run(ts, cs_, cs_, const("rotrow"), const("restrow"), ALU.mult, ALU.add)

        def prepare_c():
            cc = tiny(KD)
            s = S.run(act, cc, col("c", 0, 0, KD), ACT.Silu)
            cb = cc.unsqueeze(2).broadcast_to([P, KD, 4])
            s = S.run(act, c4[0], cb, ACT.Copy)
            return V.run(tt, c4[1], cb, c4[0].bitcast(F32), ALU.subtract, after=[s])

        row_out = {}

        def modulation(l, c, mod_row):
            bank, freed = pool.take()
            PE.wait(*freed, c_ready)
            for half in range(2):
                parts = piece("d")
                w = [z.rearrange("p (k n) -> p k n", k=4) for z in parts]
                m = product(bank[0:4, :], [((c4[0][:, 4 * half + k], c4[1][:, 4 * half + k]), (w[0][:, k], w[1][:, k]))
                                           for k in range(4)], start=half == 0, stop=half == 1)
                finished(parts, m)
            s = S.run(act, mod_row, bank[0:1, :], ACT.Copy, after=[m, row_out.get("last")], own=False)
            pool.give(bank, s)
            row_out[l] = row_out["last"] = S.dma(nc.scalar.dma_start, mod_raw[l:l + 1, c * BANK:(c + 1) * BANK], mod_row,
                                                 s_row, after=[s])

        tokcol = tiny(4 * NT * NH)
        tc4 = tokcol.rearrange("p (r t h) -> p r t h", r=4, t=NT)
        ss8, rs8, den8, aneg = tiny(NT * NH), tiny(NT * NH), tiny(NT * NH), tiny(1)
        ones_row = const("ones")

        mod_stored, added = {}, [None, None]

        def collect_modulation(l, rows_out):
            v3 = mrow[0:MOD // P, :].rearrange("p (s n) -> p s n", s=3)
            rows48 = lambda ap: ap.rearrange("(r n) -> r n", n=P)
            after = [rows_out, mod_stored.get(l - 1)]
            m = S.dma(nc.scalar.dma_start, v3[:, 0, :], rows48(mod_raw[l]), s_mrow, after=after)
            m = S.dma(nc.scalar.dma_start, v3[:, 1, :], rows48(a["ada_b"][l]), s_mrow)
            m = S.dma(nc.scalar.dma_start, v3[:, 2, :], rows48(a["mod_gain"][l]), s_mrow)
            gtt = nc.gpsimd.tensor_tensor
            G.run(gtt, v3[:, 0, :], v3[:, 0, :], v3[:, 1, :], ALU.add, after=[m])
            G.run(gtt, v3[:, 0, :], v3[:, 0, :], const("scale_rows")[0:MOD // P, :].broadcast_to([MOD // P, P]), ALU.add)
            mod_stored[l] = G.run(gtt, v3[:, 0, :], v3[:, 0, :], v3[:, 2, :], ALU.mult)

        def store_modulation(l):
            mod_stored[l] = S.dma(nc.scalar.dma_start, mod_ready[l].rearrange("(r n) -> r n", n=P), mrow[0:MOD // P, 0:P],
                                  s_mout, after=[mod_stored[l]])

        for l in range(DEPTH):
            if l > 0:
                store_modulation(l - 1)
            stage = ExitStack()
            one = lambda name, n, dt=F32: sb(stage, f"{name}_{l}", n, dt)
            gate_t = [one(f"gate_tanh{i}", NT * D) for i in range(2)]
            y_parts = [(one(f"yhi{i}", 2 * T, F32R), one(f"ylo{i}", 2 * T, F32R)) for i in range(2)]
            obuf, osq = one("obuf", NT * MIX), one("osq", NT * MIX)
            scA_, scB_ = one("scoresA", NH * SC), one("scoresB", NH * SC)
            scA, scB = (z.rearrange("p (h n) -> p h n", h=NH) for z in (scA_, scB_))
            rowbuf = one("rowbuf", 8 * T)
            arenas = [one("arena0", 3092), one("arena1", 4626)]
            row = lambda i: rowbuf[0:NH, i * T:(i + 1) * T]
            DT, ACS, LF, BC, CJ, NM, TMP, TMP2 = range(8)
            MX = LF
            gate_feat = one("gate_feat", T)
            mod_row = rowbuf[32:33, 0:BANK]
            merged3 = xn3

            def carve(b, *sizes):
                at, out_ = 0, []
                for n in sizes:
                    out_.append(arenas[b % 2][:, at:at + n])
                    at += n
                return out_

            rv, rg, rqk, rot_raw = carve(0, NT * MIX, NT * MIX, 4 * T, 4 * T)
            pad1, conv1, sz, xs, xdt = carve(1, 6 * (T + PAD), 6 * T, NT * MIX, NT * MIX, NT * MIX)
            mva, mo, pad2, conv2 = carve(2, NT * NH * (HD + 1), NT * MIX, 4 * (T + PAD), 4 * T)
            gv, gr, glaq, glak, glaG, glaE, glaX0, glaX1 = carve(3, NT * MIX, NT * MIX, *[T] * 6)
            branch_done = {}

            rm = S.dma(nc.scalar.dma_start, rows_t, a["rows1"][l:l + 1, :].broadcast_to([P, 4 * MIX + NH]), s_rows,
                       after=[V.last, mod_stored.get(l - 1)])
            V.wait(rm)
            grow = lambda i: rep(rows_t[:, i * MIX:(i + 1) * MIX], NT)
            m = rms(x3, xn3, after=added)
            fill(("head", l), mod_row)
            hm = to_features(xn3, m, scale=lambda k: col("mix_g", l, k), reads=[PE.last])
            if l == 0:
                c_ready = prepare_c()

            def twice_silu(dst, tanh, src, after=()):
                s = S.run(act, tanh, src, ACT.Tanh, scale=0.5, after=after, own=False)
                return V.run(stt, dst, tanh, 1.0, src, ALU.add, ALU.mult, after=[s, *after], own=False)

            parts = piece("z")
            w = full(parts, P)
            bank, freed = pool.take()
            PE.wait(*freed)
            m = project_features(w, 0, hm, bank, 0)
            finished(parts, m)
            s = S.run(act, row(DT), bank[0:NH, 0:T], ACT.Copy, after=[m], own=False)
            s = S.run(act, gate_feat[0:16, :], bank[32:48, 0:T], ACT.Copy, own=False)
            s = S.run(act, row(CJ), bank[64:64 + NH, 0:T], ACT.Copy, own=False)
            s = S.run(act, row(LF), bank[96:96 + NH, 0:T], ACT.Copy, own=False)
            pool.give(bank, s)
            V.run(ts, row(DT), row(DT), col("dt_bias", l, rows=NH), None, ALU.add, after=[s])
            V.run(ts, row(CJ), row(CJ), col("b_i", l, rows=NH), None, ALU.add)
            V.run(ts, row(LF), row(LF), col("b_f", l, rows=NH), -1.0, ALU.add, ALU.mult)
            bank, freed = pool.take()
            m = group(bank[:, 0:T], [(cols[0:16, COLUMN[("w_alpha", l)]:COLUMN[("w_alpha", l)] + P], gate_feat[0:16, :])],
                      after=[*freed, s])
            zalpha = osq[:, 0:T]
            v = V.run(ts, zalpha, bank[:, 0:T], col("b_alpha", l), -1.0, ALU.add, ALU.mult, after=[m])
            pool.give(bank, v)

            def gate_side(dst, bank, m, c0, t, after=()):
                d = tok3(dst)[:, t]
                return twice_silu(d, d, bank[:, c0:c0 + MIX], after=[m, *after])

            def project(b):
                before = branch_done.get(b - 2, [])
                S.wait(*before)
                V.wait(*before)
                if b == 0:
                    for i in range(2):
                        parts = piece("p0")
                        w = full(parts)
                        bank, freed = pool.take()
                        PE.wait(*freed)
                        for j in range(2):
                            m = project_features(w, j * P, hm, bank, j * T)
                        finished(parts, m)
                        s = S.run(act, tiles(rot_raw)[:, 2 * i:2 * i + 2, :], tiles(bank[:, :]), ACT.Copy, after=[m],
                                  own=False)
                        pool.give(bank, s)
                        yield
                    for t, (bank, m) in enumerate(project_tokens("p0", hm)):
                        s = S.run(act, tok3(rv)[:, t], bank[:, 0:MIX], ACT.Copy, after=[m], own=False)
                        v = gate_side(rg, bank, m, MIX, t)
                        pool.give(bank, v)
                    yield
                elif b == 1:
                    V.run(nc.vector.memset, pad1.rearrange("p (c t) -> p c t", c=6)[:, :, 0:PAD], 0.0)
                    for i in range(3):
                        parts = piece("p1")
                        yield from conv_in(parts, pad1.rearrange("p (c t) -> p c t", c=6), tiles(conv1), 2 * i,
                                           "ssd_conv", NSX)
                    parts = piece("p1")
                    w = full(parts)
                    for t in range(NT):
                        bank, freed = pool.take()
                        PE.wait(*freed)
                        m = product(bank[:, 0:MIX], [(stat_tokens(k, t), (w[0][:, k, :], w[1][:, k, :]))
                                                     for k in range(KD)])
                        v = gate_side(sz, bank, m, 0, t)
                        pool.give(bank, v)
                    finished(parts, m)
                    yield
                elif b == 2:
                    V.run(nc.vector.memset, pad2.rearrange("p (c t) -> p c t", c=4)[:, :, 0:PAD], 0.0)
                    V.run(nc.vector.memset, heads(mva)[:, :, :, HD:HD + 1], 1.0)
                    for i in range(2):
                        parts = piece("p2")
                        yield from conv_in(parts, pad2.rearrange("p (c t) -> p c t", c=4), tiles(conv2), 2 * i,
                                           "ml_conv", NMQ)
                    for t, (bank, m) in enumerate(project_tokens("p2", hm)):
                        s = S.run(act, heads(mva)[:, t, :, 0:HD], bank[:, 0:MIX].rearrange("p (h n) -> p h n", h=NH),
                                  ACT.Copy, after=[m], own=False)
                        s = S.run(act, tok3(mo)[:, t], bank[:, MIX:2 * MIX], ACT.Tanh, scale=0.5, own=False)
                        pool.give(bank, s)
                    yield
                else:
                    parts = piece("p3")
                    w = full(parts)
                    bank, freed = pool.take()
                    PE.wait(*freed)
                    for j in range(2):
                        m = project_features(w, j * P, hm, bank, j * T)
                    finished(parts, m)
                    s = S.run(act, glaq, bank[:, 0:T], ACT.Copy, scale=GLA_DK ** -0.5, after=[m], own=False)
                    s = S.run(act, glak, bank[:, T:2 * T], ACT.Copy, own=False)
                    pool.give(bank, s)
                    yield
                    for t, (bank, m) in enumerate(project_tokens("p3", hm)):
                        s = S.run(act, tok3(gv)[:, t], bank[:, 0:MIX], ACT.Copy, after=[m], own=False)
                        v = gate_side(gr, bank, m, MIX, t)
                        pool.give(bank, v)
                    yield

            def conv_in(parts, pad3, conv3, first, name, n):
                w = full(parts)
                bank, freed = pool.take()
                PE.wait(*freed)
                for j in range(2):
                    m = project_features(w, j * P, hm, bank, j * T)
                finished(parts, m)
                s = S.run(act, pad3[:, first:first + 2, PAD:], tiles(bank[:, :]), ACT.Copy, after=[m], own=False)
                pool.give(bank, s)
                yield
                for c in (first, first + 1):
                    dst = conv3[:, c, :]
                    s = S.run(act, dst, pad3[:, c, 0:T], ACT.Identity, scale=col(name + "_w", l, c),
                              bias=col(name + "_b", l, c), after=[V.last])
                    for k in range(1, CONV_K):
                        v = V.run(stt, dst, pad3[:, c, k:k + T], col(name + "_w", l, k * n + c), dst, ALU.mult,
                                  ALU.add, after=[s])
                    twice_silu(dst, pad3[:, c, PAD:], dst, after=[v])

            def scores(qt, kt, rows, bank, after=()):
                PE.wait(*after)
                PE.run(mm, bank[:, 0:T], kt[rows, 0:P], qt[rows, 0:T], start=True, stop=True, mark=False)
                return PE.run(mm, bank[:, T:SC], kt[rows, P:T], qt[rows, P:T], start=True, stop=True)

            def apply_scores(sc, v4, after, width=HD):
                outs = []
                PE.wait(*after)
                for t in range(NT):
                    bank, freed = pool.take()
                    PE.wait(*freed)
                    o = bank[:, 0:NH * width].rearrange("p (h n) -> p h n", h=NH)
                    for h in range(NH):
                        if t == 0:
                            m = group(o[:, h, :], [(sc[:, h, 0:P], v4[:, 0, h, :])])
                        else:
                            m = group(o[:, h, :], [(sc[:, h, P:T], v4[:, 0, h, :]), (sc[:, h, T:SC], v4[:, 1, h, :])])
                    outs.append((bank, o, m))
                return outs

            def head_norm(src, side, b, after=(), lone=False, half=0.5):
                n = 1 if lone else NH
                w_ = MIX // n
                V.run(tt, osq, src, src, ALU.mult, after=after)
                V.run(reduce, ss8[:, 0:NT * n], osq.rearrange("p (g n) -> p g n", n=w_), AXX, ALU.add)
                root = inverse_root(rs8[:, 0:NT * n], ss8[:, 0:NT * n], w_, V.last)
                V.run(tt, src, src, side, ALU.mult)
                V.wait(root)
                g_ = src.rearrange("p (g n) -> p g n", n=w_)
                v = V.run(tt, g_, g_, rs8[:, 0:NT * n].unsqueeze(2).broadcast_to([P, NT * n, w_]), ALU.mult)
                yield
                bank, freed = pool.take()
                PE.wait(*freed, v)
                for c in range(2):
                    for t in range(NT):
                        m = PE.run(nc.tensor.transpose, bank[:, (2 * c + t) * P:(2 * c + t + 1) * P],
                                   tok3(src)[:, t, c * P:(c + 1) * P], ident, mark=(c == 1 and t == 1))
                while done["merged"] < b - 2:
                    advance()
                S.wait(y_read.get(b - 2))
                V.wait(y_read.get(b - 2))
                v = to_parts(*y_parts[b % 2], bank[:, :], m, scale=half)
                pool.give(bank, v)
                branch_done[b] = marks()
                y_ready[b] = v

            y_ready, y_read = {}, {}

            def softplus(dst, src, tmp, tmp2):
                v = V.run(stt, tmp, src, -1.0, src, ALU.mult, ALU.min)
                s = S.run(act, tmp2, tmp, ACT.Exp, after=[v])
                s = S.run(act, tmp2, tmp2, ACT.Ln, bias=1.0)
                return V.run(stt, dst, src, 0.0, tmp2, ALU.max, ALU.add, after=[s])

            def decays(dst, r_, colid):
                op = ALU.subtract if colid == 0 else ALU.add
                for h2 in range(2):
                    bank, freed = pool.take()
                    PE.wait(*freed)
                    for j in range(2):
                        m = PE.run(mm, bank[:, j * T:(j + 1) * T],
                                   ident[0:NH, 2 * h2 + j:2 * h2 + j + 1].broadcast_to([NH, P]), r_,
                                   start=True, stop=True, mark=(j == 1))
                    for j in range(2):
                        h = 2 * h2 + j
                        V.run(ts, dst[:, h, 0:T], bank[:, j * T:(j + 1) * T], tc4[:, colid, 0, h:h + 1], 0.0,
                              op, ALU.min, after=[m], own=(h == 0))
                        v = V.run(ts, dst[:, h, T:SC], bank[:, j * T + P:(j + 1) * T], tc4[:, colid, 1, h:h + 1],
                                  0.0, op, ALU.min, own=False)
                    pool.give(bank, v)
                    s = S.run(act, dst[:, 2 * h2:2 * h2 + 2, :], dst[:, 2 * h2:2 * h2 + 2, :], ACT.Exp, after=[v],
                              own=False)
                return s

            def retention():
                for i in range(2):
                    bank, freed = pool.take()
                    PE.wait(*freed)
                    m = PE.run(mm, bank[:, :], const("rot"), rot_raw[:, i * 2 * T:(i + 1) * 2 * T], start=True, stop=True)
                    two, raw3, out3 = slice(2 * i, 2 * i + 2), tiles(rot_raw), tiles(rqk)
                    V.run(tt, out3[:, two, :], tiles(bank[:, :]), rep(const("sin"), 2), ALU.mult, after=[m])
                    pool.give(bank, V.last)
                    V.run(tt, raw3[:, two, :], raw3[:, two, :], rep(const("cos"), 2), ALU.mult)
                    v = V.run(tt, out3[:, two, :], out3[:, two, :], raw3[:, two, :], ALU.add)
                    yield
                dec = const("decay").rearrange("p (h n) -> p h n", h=NH)
                PE.wait(v)
                r3 = tiles(rqk)
                for h in range(NH):
                    bank, freed = pool.take()
                    rows = slice((h % 2) * HD, (h % 2 + 1) * HD)
                    m = scores(r3[:, h // 2, :], r3[:, 2 + h // 2, :], rows, bank, after=freed)
                    v = V.run(tt, scB[:, h, :], bank[:, 0:SC], dec[:, h, :], ALU.mult, after=[m], own=(h == 0))
                    pool.give(bank, v)
                yield
                outs = apply_scores(scB, heads(rv), [v])
                for t, (bank, o, m) in enumerate(outs):
                    s = S.run(act, tok3(obuf)[:, t], bank[:, 0:MIX], ACT.Copy, after=[m], own=False)
                    pool.give(bank, s)
                V.run(tt, tok3(rg), tok3(rg), grow(0), ALU.mult)
                yield
                yield from head_norm(obuf, rg, 0, [s])

            def ssd():
                c3 = tiles(conv1)
                bank, freed = pool.take()
                PE.wait(*freed, V.last)
                for t in range(NT):
                    for c in range(2):
                        m = PE.run(nc.tensor.transpose, bank[:, (2 * t + c) * P:(2 * t + c + 1) * P],
                                   c3[:, c, t * P:(t + 1) * P], ident, mark=(c == 1 and t == 1))
                s = S.run(act, xs, bank[:, :], ACT.Copy, scale=0.5, after=[m], own=False)
                pool.give(bank, s)
                yield
                s_e = decays(scA, row(ACS), 0)
                yield
                for t in range(NT):
                    V.run(tt, heads(xdt)[:, t], heads(xs)[:, t], tc4[:, 1, t].unsqueeze(2).broadcast_to([P, NH, HD]),
                          ALU.mult, after=[s])
                yield
                for g in range(2):
                    bank, freed = pool.take()
                    m = scores(c3[:, 4 + g, :], c3[:, 2 + g, :], slice(0, P), bank, after=freed)
                    v = V.run(stt, scB[:, g, :], bank[:, 0:SC], 0.25, const("tri"), ALU.mult, ALU.mult, after=[m])
                    pool.give(bank, v)
                    V.run(tt, scA[:, 2 * g:2 * g + 2, :], scA[:, 2 * g:2 * g + 2, :], rep(scB[:, g, :], 2), ALU.mult,
                          after=[s_e])
                yield
                outs = apply_scores(scA, heads(xdt), [V.last])
                drow = rows_t[:, 4 * MIX:4 * MIX + NH].unsqueeze(2).broadcast_to([P, NH, HD])
                for t in range(NT):
                    V.run(tt, heads(obuf)[:, t], heads(xs)[:, t], drow, ALU.mult)
                yield
                for t, (bank, o, m) in enumerate(outs):
                    v = V.run(tt, heads(obuf)[:, t], heads(obuf)[:, t], o, ALU.add, after=[m])
                    pool.give(bank, v)
                V.run(stt, obuf, obuf, 0.5, sz, ALU.mult, ALU.mult)
                V.run(vcopy, tok3(sz), grow(1))
                yield
                yield from head_norm(obuf, sz, 1, lone=True, half=1.0)

            def mlstm():
                c3 = tiles(conv2)
                PE.wait(V.last)
                s = decays(scA, row(NM), 2)
                yield
                V.run(stt, scA, scA, 0.25 * HD ** -0.5, rep(const("tri"), NH), ALU.mult, ALU.mult, after=[s])
                for h in range(NH):
                    bank, freed = pool.take()
                    rows = slice((h % 2) * HD, (h % 2 + 1) * HD)
                    m = scores(c3[:, h // 2, :], c3[:, 2 + h // 2, :], rows, bank, after=freed)
                    v = V.run(tt, scA[:, h, :], scA[:, h, :], bank[:, 0:SC], ALU.mult, after=[m], own=(h == 0))
                    pool.give(bank, v)
                yield
                outs = apply_scores(scA, mva.rearrange("p (t h n) -> p t h n", t=NT, h=NH), [v], width=HD + 1)
                V.run(stt, tok3(mo), tok3(mo), 1.0, grow(3), ALU.add, ALU.mult)
                yield
                d3 = den8.rearrange("p (t h) -> p t h", t=NT)
                for t, (bank, o, m) in enumerate(outs):
                    V.run(vcopy, ss8[:, 0:NH], o[:, :, HD], after=[m])
                    V.run(stt, d3[:, t], ss8[:, 0:NH], -1.0, ss8[:, 0:NH], ALU.mult, ALU.max)
                    V.run(tt, d3[:, t], d3[:, t], tc4[:, 3, t], ALU.max)
                    V.run(nc.vector.reciprocal, d3[:, t], d3[:, t])
                    v = V.run(tt, heads(obuf)[:, t], o[:, :, 0:HD], d3[:, t].unsqueeze(2).broadcast_to([P, NH, HD]),
                              ALU.mult)
                    pool.give(bank, v)
                yield
                yield from head_norm(obuf, mo, 2)

            def gla():
                V.run(scan, glaG, ones_row, gate_feat, 0.0, ALU.mult, ALU.add)
                V.run(nc.vector.memset, scB[:, :, 0:P], 0.0)
                V.run(nc.vector.memset, scB[:, :, T:SC], 0.0)
                lm3 = lmask.rearrange("p (l n) -> p l n", n=P)
                reads, X = [None, None], [glaX0, glaX1]

                def level_scores(kt, qt, after):
                    PE.wait(*after)
                    own = [pool.take() for _ in range(NH)]
                    PE.wait(*[f for _, freed in own for f in freed])
                    blocks = [(0, slice(0, P), slice(P, T))] if kt is X[0] and not started else [
                        (t, slice(t * P, (t + 1) * P), slice(t * P, (t + 1) * P)) for t in range(NT)]
                    done = []
                    for b, kc, qc in blocks:
                        for h in range(NH):
                            rows = slice(h * GLA_DK, (h + 1) * GLA_DK)
                            done.append(PE.run(mm, own[h][0][:, b * P:(b + 1) * P], kt[rows, kc], qt[rows, qc],
                                               start=True, stop=True, tile_position=(h * GLA_DK, 0),
                                               mark=(b == len(blocks) - 1)))
                    started.append(True)
                    return [(o_[0], m) for o_, m in zip(own, done[-NH:])]

                def keep_scores(own, li):
                    for h, (bank, m) in enumerate(own):
                        if li is None:
                            v = V.run(vcopy, scB[:, h, P:T], bank[:, 0:P], after=[m], own=False)
                        else:
                            dst = scB[:, h, :].rearrange("p (b n) -> p b n", n=P)[:, ::2, :]
                            v = V.run(nc.vector.copy_predicated, dst, rep(lm3[:, li, :], NT),
                                      bank[:, 0:T].rearrange("p (b n) -> p b n", n=P), after=[m], own=(h == 0))
                        pool.give(bank, v)

                started, before = [], None
                for i, half in enumerate((P,) + GLA_LEVELS):
                    buf = X[i % 2]
                    n = T // (2 * half)
                    view = lambda ap: ap.rearrange("p (n s c) -> p n s c", n=n, s=2)
                    ref = view(glaG)[:, :, 0, half - 1:half].broadcast_to([P, n, half])
                    V.run(tt, view(glaE)[:, :, 1, :], view(glaG)[:, :, 1, :], ref, ALU.subtract)
                    v = V.run(tt, view(glaE)[:, :, 0, :], ref, view(glaG)[:, :, 0, :], ALU.subtract, own=False)
                    s = S.run(act, glaE, glaE, ACT.Exp, after=[v])
                    V.run(tt, view(buf)[:, :, 1, :], view(glaE)[:, :, 1, :], view(glaq)[:, :, 1, :], ALU.mult,
                          after=[s, reads[i % 2]])
                    v = V.run(tt, view(buf)[:, :, 0, :], view(glaE)[:, :, 0, :], view(glak)[:, :, 0, :], ALU.mult,
                              own=False)
                    if before is not None:
                        keep_scores(before, None if i == 1 else i - 2)
                    before = level_scores(buf, buf, [v])
                    reads[i % 2] = before[-1][1]
                    yield
                keep_scores(before, len(GLA_LEVELS) - 1)
                keep_scores(level_scores(glak, glaq, [S.last]), len(GLA_LEVELS))
                yield
                outs = apply_scores(scB, heads(gv), [V.last])
                for t, (bank, o, m) in enumerate(outs):
                    s = S.run(act, tok3(obuf)[:, t], bank[:, 0:MIX], ACT.Copy, after=[m], own=False)
                    pool.give(bank, s)
                V.run(tt, tok3(gr), tok3(gr), grow(2), ALU.mult)
                yield
                yield from head_norm(obuf, gr, 3, [s])

            def modulation_step(c):
                modulation(l, c, mod_row)
                yield

            gate_reads = [[], []]

            def gate(b):
                g3 = tok3(gate_t[b % 2])
                S.wait(*gate_reads[b % 2])
                for hf in range(2):
                    for t, (bank, m) in enumerate(project_tokens(f"g{b}", hm)):
                        s = S.run(act, g3[:, t, hf * BANK:(hf + 1) * BANK], bank[:, :], ACT.Tanh, scale=0.5, after=[m],
                                  own=False)
                        pool.give(bank, s)
                    yield
                gate_ready[b] = s

            gate_ready = {}

            def merge(b):
                parts = piece(f"a{b}")
                w = [z.rearrange("p (c n) -> p c n", c=2) for z in parts]
                yp = [tiles(z) for z in y_parts[b % 2]]
                g3 = tok3(gate_t[b % 2])
                PE.wait(y_ready[b])
                for t in range(NT):
                    for hf in range(2):
                        cs = slice(hf * BANK, (hf + 1) * BANK)
                        bank, freed = pool.take()
                        PE.wait(*freed)
                        m = product(bank[:, :], [((yp[0][:, c, t * P:(t + 1) * P], yp[1][:, c, t * P:(t + 1) * P]),
                                                  (w[0][:, c, cs], w[1][:, c, cs])) for c in range(2)])
                        dst = merged3[:, t, cs] if b == 0 else g3[:, t, cs]
                        v = V.run(stt, dst, g3[:, t, cs], 1.0, bank[:, :], ALU.add, ALU.mult,
                                  after=[m, gate_ready[b]], own=False)
                        pool.give(bank, v)
                finished(parts, m)
                y_read[b] = m
                if b > 0:
                    v = V.run(tt, merged3, merged3, g3, ALU.add)
                gate_reads[b % 2] = [v]
                yield

            branches = [retention, ssd, mlstm, gla]
            done = {"p": -1, "core": -1, "merged": -1}
            items = [(z[0], int(z[1])) for z in branch_items if l == 0 or z[0] != "d"]
            current = []

            def advance():
                if not current:
                    if not items:
                        return False
                    kind, b = items[0]
                    if done["core"] < {"a": b, "p": b - 2}.get(kind, -1):
                        return False
                    items.pop(0)
                    current.append((kind, b, {"p": project, "g": gate, "a": merge, "d": modulation_step}[kind](b)))
                kind, b, steps = current[0]
                if next(steps, 0) is not None:
                    current.clear()
                    if kind in "pa":
                        done["p" if kind == "p" else "merged"] = b
                    return advance()
                return True

            def row_steps():
                softplus(row(DT), row(DT), row(TMP), row(TMP2))
                yield
                softplus(row(LF), row(LF), row(TMP), row(TMP2))
                yield
                softplus(gate_feat, zalpha, scA_[:, 0:T], scA_[:, T:2 * T])
                yield
                V.run(ts, gate_feat, gate_feat, -1.0 / GLA_TAU, None, ALU.mult)
                s = S.run(act, aneg[0:NH, :], col("a_log", l, rows=NH), ACT.Exp)
                V.run(ts, row(TMP), row(DT), aneg[0:NH, :], -1.0, ALU.mult, ALU.mult, after=[s])
                V.run(scan, row(ACS), ones_row[0:NH, :], row(TMP), 0.0, ALU.mult, ALU.add)
                yield
                V.run(ts, row(LF), row(LF), -1.0, None, ALU.mult)
                V.run(scan, row(BC), ones_row[0:NH, :], row(LF), 0.0, ALU.mult, ALU.add)
                V.run(tt, row(CJ), row(CJ), row(BC), ALU.subtract)
                V.run(scan, row(MX), ones_row[0:NH, :], row(CJ), 0.0, ALU.mult, ALU.max)
                yield
                V.run(tt, row(TMP), row(BC), row(MX), ALU.add)
                v = V.run(ts, row(NM), row(MX), -1.0, None, ALU.mult)
                s = S.run(act, row(TMP2), row(TMP), ACT.Exp, scale=-1.0, after=[v])
                yield
                bank, freed = pool.take()
                PE.wait(*freed, v, s)
                for i, r_ in enumerate((ACS, DT, CJ, TMP2)):
                    for t in range(NT):
                        c = (i * NT + t) * NH
                        m = PE.run(nc.tensor.transpose, bank[:, c:c + NH], row(r_)[:, t * P:(t + 1) * P],
                                   ident[0:NH, 0:NH], mark=(i == 3 and t == 1))
                v = V.run(vcopy, tokcol, bank[:, 0:4 * NT * NH], after=[m])
                pool.give(bank, v)
                yield

            steps = row_steps()
            for _ in project(0):
                next(steps, None)
            for _ in steps:
                advance()

            for b, branch in enumerate(branches):
                while done["p"] < b and b > 0:
                    advance()
                for _ in branch():
                    advance()
                done["core"] = b
            while advance():
                pass
            for _ in merge(3):
                pass
            merged = V.last
            fill(("merged", l), mod_row)
            mT = to_features(merged3, [merged] * NT, scale=0.5, reads=[PE.last])
            added = [None, None]
            for hf in range(2):
                for t, (bank, m) in enumerate(project_tokens("wout", mT)):
                    xo = x3[:, t, hf * BANK:(hf + 1) * BANK]
                    added[t] = V.run(tt, xo, xo, bank[:, :], ALU.add, after=[m], own=False)
                    pool.give(bank, added[t])
            wout_read = PE.last
            m = rms(x3, xn3, after=added)
            fill(("out", l), mod_row)

            ffn_gain = lambda k: col("ffn_g", l, k)
            if l % 2 == 0:
                hm = to_features(xn3, m, scale=ffn_gain, reads=[wout_read])
                fill(("late", l), mod_row)
                stage.close()
                stage = ExitStack()
                collect_modulation(l, row_out[l])
                V.wait(row_out[l])
                pool_a, pool_y = split_banks()

                def add_outputs(ys):
                    for t, hf, bank, ym in ys:
                        xo = x3[:, t, hf * BANK:(hf + 1) * BANK]
                        added[t] = V.run(tt, xo, xo, bank[:, :], ALU.add, after=[ym], own=False)
                    rejoin_banks(pool_a, ys, V.last)

                steps = rope_tables(sb(stage, "angles", 4 * T))
                feed_forward(stage, "ffn", NT, [(stat_tokens, lambda: hm, add_outputs)], pool_a, pool_y,
                             between=lambda: next(steps, None))
                for _ in steps:
                    pass
                stage.close()
                for q in (S, V, G):
                    q.wait(PE.last)
            else:
                stage.close()
                closing = ExitStack()
                mod_row = sb(closing, "modulation_row_spare", BANK)[0:1, :]
                fg = sb(closing, "final_gain", D)
                for q in (PE, V, G, S):
                    q.wait(PE.last, V.last)
                late = (modulation(l_, c, mod_row) for l_, c in filler_of[("late", l)])
                fg_in = S.dma(nc.scalar.dma_start, fg, a["final_g"].broadcast_to([P, D]), s_gain)
                experts(l, m, ffn_gain, lambda: next(late, None))
                pool.free = [(b, ()) for b in banks]
                added = [V.last] * NT

        stage2 = ExitStack()
        mod = sb(stage2, "mod", MOD)
        m3 = mod.rearrange("p (s d) -> p s d", s=6)
        sink8, max8, sum8, neg8 = tiny(QH), tiny(NT * QH), tiny(NT * QH), tiny(NT * QH)
        mod_in = [None, None]

        def load_modulation(l, half, after):
            cs = slice(half * 3 * D, (half + 1) * 3 * D)
            mod_in[half] = S.dma(nc.scalar.dma_start, mod[:, cs], mod_ready[l:l + 1, cs].broadcast_to([P, 3 * D]),
                                 s_mod[half], after=[mod_stored[l], *after])

        load_modulation(0, 0, [])
        load_modulation(0, 1, [])
        rms(x3, xn3, after=added)
        fill(("second", 0), mod_row)
        V.wait(fg_in)
        first_x = [V.run(tt, x3[:, t], xn3[:, t], fg, ALU.mult) for t in range(NT)]
        S.wait(V.last)

        def norm_and_add(banks_in, gate_part):
            roots = []
            for t in range(NT):
                for t_, hf, bank, ym in banks_in:
                    if t_ == t:
                        m = S.run(act, xn3[:, t, hf * BANK:(hf + 1) * BANK], bank[:, :], ACT.Square,
                                  accum_out=stat[:, 2 * t + hf:2 * t + hf + 1], after=[ym], own=False)
                total = stat[:, 6 + t:7 + t]
                m = G.run(nc.gpsimd.tensor_tensor, total, stat[:, 2 * t:2 * t + 1], stat[:, 2 * t + 1:2 * t + 2], ALU.add,
                          after=[m])
                roots.append(inverse_root(stat[:, 4 + t:5 + t], total, D, m))
            done_ = []
            for t in range(NT):
                for t_, hf, bank, _ in banks_in:
                    if t_ == t:
                        cs = slice(hf * BANK, (hf + 1) * BANK)
                        v = V.run(stt, xn3[:, t, cs], bank[:, :], stat[:, 4 + t:5 + t], m3[:, gate_part, cs], ALU.mult,
                                  ALU.mult, after=[roots[t]], own=False)
                done_.append(V.run(tt, x3[:, t], x3[:, t], xn3[:, t], ALU.add))
            return done_

        def modulated(half, after):
            shift, scale = m3[:, 3 * half, :], m3[:, 3 * half + 1, :]
            roots, ms = [], []
            for t in range(NT):
                m = S.run(act, xn3[:, t, :], x3[:, t, :], ACT.Square, accum_out=stat[:, 8 + t:9 + t], after=[after[t]])
                roots.append(inverse_root(stat[:, 10 + t:11 + t], stat[:, 8 + t:9 + t], D, m))
            V.wait(mod_in[half])
            for t in range(NT):
                V.run(stt, xn3[:, t, :], x3[:, t, :], stat[:, 10 + t:11 + t], scale, ALU.mult, ALU.mult, after=[roots[t]])
                ms.append(V.run(tt, xn3[:, t, :], xn3[:, t, :], shift, ALU.add))
            return to_features(xn3, ms, reads=[PE.last])

        added = first_x
        for l in range(DEPTH):
            if l > 0:
                load_modulation(l, 1, [V.last])
            stage = ExitStack()
            hm = modulated(0, added)
            tables_in = one("attention_tables", a["poolm"].shape[1])
            poolm, rot2 = tables_in[:, 0:4 * SC], tables_in[:, 4 * SC:4 * SC + P]
            causal, banded = tables_in[:, 4 * SC + P:4 * SC + 2 * P], tables_in[:, 4 * SC + 2 * P:]
            pw_ = one("pool_weights", 4 * P)
            brow = one("bias_rows", P + BANK)
            qraw, qrot = one("qraw", 6 * T), one("qrot", 6 * T)
            vtok, utok = one("vtok", NT * P), one("utok", NT * BANK)
            prob, probT = xn, one("probT", QH * T)
            pooled, obuf, obuf1 = one("pooled", 4 * T), one("attended", BANK), one("attended1", BANK)
            prob0 = fg
            pw = pw_.rearrange("p (g n) -> p g n", g=4)
            rm = S.dma(nc.scalar.dma_start, tables_in, a["poolm"], s_att)
            rm = S.dma(nc.scalar.dma_start, pw, a["pool_w"][l].rearrange("g p n -> p g n"), s_att)
            rm = S.dma(nc.scalar.dma_start, brow, a["b_in2"][l:l + 1, 640:1280].broadcast_to([P, P + BANK]), s_att)
            rm = S.dma(nc.scalar.dma_start, sink8, a["sinks"][l:l + 1, :].broadcast_to([P, QH]), s_att)
            V.wait(rm)
            PE.wait(rm)
            qraw3, qrot3 = tiles(qraw), tiles(qrot)

            def rotate(i):
                bank, freed = pool.take()
                two = slice(2 * i, 2 * i + 2)
                m = group(bank[:, :], [(rot2, qraw[:, 2 * i * T:2 * (i + 1) * T])], after=[*freed, raw_ready[i]])
                v = V.run(tt, qrot3[:, two, :], tiles(bank[:, :]), rep(sn_, 2), ALU.mult, after=[m])
                pool.give(bank, v)
                V.run(tt, qraw3[:, two, :], qraw3[:, two, :], rep(cs_, 2), ALU.mult)
                return V.run(tt, qrot3[:, two, :], qrot3[:, two, :], qraw3[:, two, :], ALU.add)

            raw_ready = {}
            for i in range(2):
                parts = piece("q2")
                w = full(parts)
                bank, freed = pool.take()
                PE.wait(*freed)
                for j in range(2):
                    m = project_features(w, j * P, hm, bank, j * T)
                finished(parts, m)
                for j in range(2):
                    v = V.run(ts, qraw3[:, 2 * i + j, :], bank[:, j * T:(j + 1) * T], col("b_q", l, 2 * i + j), None,
                              ALU.add, after=[m], own=False)
                pool.give(bank, v)
                raw_ready[i] = v
                if i == 1:
                    rotate(0)
            parts = piece("kv2")
            w = full(parts)
            bank, freed = pool.take()
            PE.wait(*freed)
            m = project_features(w, 0, hm, bank, 0)
            v = V.run(ts, qraw3[:, 4, :], bank[:, 0:T], col("b_k", l), None, ALU.add, after=[m], own=False)
            pool.give(bank, v)
            kmark = v
            vt3, ut3 = tok3(vtok), tok3(utok)
            bank, freed = pool.take()
            PE.wait(*freed)
            for t in range(NT):
                m = product(bank[:, t * P:(t + 1) * P], [(stat_tokens(k, t), (w[0][:, k, P:2 * P], w[1][:, k, P:2 * P]))
                                                         for k in range(KD)])
            finished(parts, m)
            v = V.run(tt, vt3, bank[:, 0:T].rearrange("p (t n) -> p t n", t=NT), rep(brow[:, 0:P], NT), ALU.add,
                      after=[m], own=False)
            pool.give(bank, v)
            rotate(1)
            bank, freed = pool.take()
            m = group(bank[:, 0:T], [(const("swap"), qraw3[:, 4, :])], after=[*freed, kmark])
            raw_ready[2] = V.run(vcopy, qraw3[:, 5, :], bank[:, 0:T], after=[m])
            pool.give(bank, raw_ready[2])
            for t, (bank, m) in enumerate(project_tokens("u2", hm)):
                v = V.run(tt, ut3[:, t, :], bank[:, :], brow[:, P:P + BANK], ALU.add, after=[m], own=False)
                pool.give(bank, v)
            u_ready = v
            rotated = rotate(2)
            h_read = PE.last

            def pooling():
                pm3 = poolm.rearrange("p (g n) -> p g n", g=4)
                PE.wait(u_ready)
                S.wait(h_read)
                V.wait(h_read)
                for g in range(4):
                    bank, freed = pool.take()
                    PE.wait(*freed)
                    group(bank[:, 0:P], [(ut3[:, 0, g * P:(g + 1) * P], pm3[:, g, 0:P])])
                    m = group(bank[:, P:T], [(ut3[:, 0, g * P:(g + 1) * P], pm3[:, g, P:T]),
                                             (ut3[:, 1, g * P:(g + 1) * P], pm3[:, g, T:SC])])
                    s = S.run(act, pooled[:, g * T:(g + 1) * T], bank[:, 0:T], ACT.Copy, after=[m], own=False)
                    pool.give(bank, s)
                    yield
                    bank, freed = pool.take()
                    m = group(bank[:, 0:T], [(pw[:, g, :], pooled[:, g * T:(g + 1) * T])], after=[*freed, s])
                    v = to_parts(hi3[:, 4 + g, :], lo3[:, 4 + g, :], bank[:, 0:T], m, scale=col("pool_scale", l, g))
                    pool.give(bank, v)
                    yield

            pool_steps = pooling()
            PE.wait(rotated)

            def attend(t, pr3, pT3, out_t):
                mx8, sm8, nb8 = (z[:, t * QH:(t + 1) * QH] for z in (max8, sum8, neg8))
                nk = (t + 1) * P
                for h4 in range(QH // 4):
                    for odd in range(2):
                        bank, freed = pool.take()
                        PE.wait(*freed)
                        rows = slice(odd * HD, (odd + 1) * HD)
                        for j in range(2):
                            m = PE.run(mm, bank[:, j * T:j * T + nk], qrot3[rows, 2 * h4 + j, t * P:(t + 1) * P],
                                       qrot3[rows, 4 + (h4 ^ odd), 0:nk], start=True, stop=True, mark=(j == 1))
                        b3 = bank[:, :].rearrange("p (j n) -> p j n", j=2)[:, :, 0:nk]
                        v = V.run(stt, pr3[:, 4 * h4 + odd:4 * h4 + odd + 3:2, 0:nk], b3, HD ** -0.5,
                                  rep(banded[:, 0:nk] if t else causal, 2), ALU.mult, ALU.add, after=[m], own=False)
                        pool.give(bank, v)
                yield
                V.run(reduce, mx8, pr3[:, :, 0:nk], AXX, ALU.max)
                V.run(tt, mx8, mx8, sink8, ALU.max)
                v = V.run(ts, nb8, mx8, -1.0, None, ALU.mult)
                for h in range(QH):
                    s = S.run(act, pr3[:, h, 0:nk], pr3[:, h, 0:nk], ACT.Exp, bias=nb8[:, h:h + 1],
                              accum_out=sm8[:, h:h + 1], after=[v], own=False)
                yield
                v = V.run(tt, mx8, sink8, mx8, ALU.subtract)
                s = S.run(act, mx8, mx8, ACT.Exp, after=[v])
                V.run(tt, sm8, sm8, mx8, ALU.add, after=[s])
                rden = V.run(nc.vector.reciprocal, sm8, sm8)
                yield
                for h2 in range(QH // 2):
                    bank, freed = pool.take()
                    PE.wait(*freed, s)
                    for j in range(2):
                        for kt in range(t + 1):
                            m = PE.run(nc.tensor.transpose, bank[:, j * T + kt * P:j * T + (kt + 1) * P],
                                       pr3[:, 2 * h2 + j, kt * P:(kt + 1) * P], ident, mark=(j == 1 and kt == t))
                    b3 = bank[:, :].rearrange("p (j n) -> p j n", j=2)[:, :, 0:nk]
                    v = V.run(vcopy, pT3[:, 2 * h2:2 * h2 + 2, 0:nk], b3, after=[m], own=False)
                    pool.give(bank, v)
                yield
                bank, freed = pool.take()
                PE.wait(*freed, v)
                for h in range(QH):
                    kv = slice((h // 4) * HD, (h // 4 + 1) * HD)
                    m = group(bank[:, h * HD:(h + 1) * HD],
                              [(pT3[:, h, kt * P:(kt + 1) * P], vt3[:, kt, kv]) for kt in range(t + 1)])
                yield
                v = V.run(tt, out_t.rearrange("p (h n) -> p h n", h=QH), bank[:, :].rearrange("p (h n) -> p h n", h=QH),
                          sm8.unsqueeze(2).broadcast_to([P, QH, HD]), ALU.mult, after=[m, rden])
                pool.give(bank, v)
                bank, freed = pool.take()
                PE.wait(*freed, v)
                for c in range(4):
                    m = PE.run(nc.tensor.transpose, bank[:, c * P:(c + 1) * P], out_t[:, c * P:(c + 1) * P], ident,
                               mark=(c == 3))
                v = to_parts(hi3[:, 0:4, t * P:(t + 1) * P], lo3[:, 0:4, t * P:(t + 1) * P],
                             bank[:, :].rearrange("p (c n) -> p c n", c=4), m)
                pool.give(bank, v)
                yield

            by_head = lambda ap: ap.rearrange("p (h n) -> p h n", h=QH)
            tiles_of_queries = [attend(0, by_head(prob0), by_head(qraw[:, 0:QH * P]), obuf),
                                attend(1, by_head(prob), by_head(probT), obuf1)]
            going = True
            while going:
                going = [next(z, 0) is None for z in tiles_of_queries][1]
                next(pool_steps, 0)
            for _ in pool_steps:
                pass
            mixed = V.last
            banks_in = []
            for hf in range(2):
                for t, (bank, m) in enumerate(project_tokens("wout2", [mixed] * NT)):
                    banks_in.append((t, hf, bank, m))
            S.wait(V.last)
            added = norm_and_add(banks_in, 2)
            for _, _, bank, _ in banks_in:
                pool.give(bank, V.last)
            fill(("mixed", l), obuf[0:1, :])
            hm = modulated(1, added)
            stage.close()
            if l + 1 < DEPTH:
                collect_modulation(l + 1, row_out[l + 1])
                free_after = [V.last]
            stage = ExitStack()

            pool_a, pool_y = split_banks()

            def finish(ys):
                added[:] = norm_and_add(ys, 5)
                rejoin_banks(pool_a, ys, V.last)

            def next_modulation():
                for i in range(FF // (2 * P) + 2):
                    if i == 2 and l + 1 < DEPTH:
                        store_modulation(l + 1)
                    if i == 4 and l + 1 < DEPTH:
                        load_modulation(l + 1, 0, free_after)
                    yield

            steps = next_modulation()
            feed_forward(stage, "ffn2", NT, [(stat_tokens, lambda: hm, finish)], pool_a, pool_y,
                         tag=l, between=lambda: next(steps, None))
            stage.close()
            for q in (S, V, G):
                q.wait(PE.last)

        om = SP.dma(nc.sync.dma_start, out.rearrange("o (t p) d -> p (o t) d", p=P), x3, s_out, after=[V.last])
        SP.wait(om)
        stage2.close()
        closing.close()
        assert counts["used"] == len(plan) and not ready

        with nc.Block() as block:
            @block.sync
            def _(_e):
                SP.play()

            @block.scalar
            def _(_e):
                S.play()

            @block.vector
            def _(_e):
                V.play()

            @block.tensor
            def _(_e):
                PE.play()

            @block.gpsimd
            def _(_e):
                G.play()


CONST, COLUMN = {}, {}


def constant_tables():
    parts, at = [], 0
    p = np.arange(P)

    def add(name, table):
        nonlocal at
        table = np.broadcast_to(np.asarray(table, np.float32), (P, np.shape(table)[-1]))
        CONST[name] = (at, table.shape[1])
        at += table.shape[1]
        parts.append(table)

    add("ident", np.eye(P))
    half = HD // 2
    rot = np.zeros((P, P))
    for m in range(P):
        if m % HD < half:
            rot[m + half, m] = -1.0
        else:
            rot[m - half, m] = 1.0
    add("rot", rot)
    inv = (np.float32(10000.0) ** (-np.arange(half, dtype=np.float32) / np.float32(half))).astype(np.float32)
    ang = np.arange(T, dtype=np.float32)[None, :] * inv[p % half][:, None]
    add("cos", np.cos(ang.astype(np.float64)))
    add("sin", np.sin(ang.astype(np.float64)))
    i = np.concatenate([np.arange(T), np.arange(P, T)])
    j = np.concatenate([np.zeros(T), np.full(P, P)])[None, :] + p[:, None]
    lag = i[None, :] - j
    tri = lag >= 0
    log_gamma = np.log1p(-np.exp2(-5.0 - np.arange(NH)))
    add("decay", np.concatenate([np.where(tri, np.exp(np.maximum(lag, 0) * g), 0) * HD ** -0.5 for g in log_gamma], 1))
    add("tri", tri)
    add("ones", np.ones((P, T)))
    add("power", np.full((P, 1), -0.5))
    add("iota8", np.arange(NE)[None, :])
    add("scale_rows", np.isin(p // (D // P), (1, 4)).astype(np.float32)[:, None])
    add("slots", np.arange(1, P + 1)[None, :])
    swap = np.zeros((P, P))
    swap[(p + HD) % P, p] = 1.0
    add("swap", swap)
    hr = ROT // 2
    rot2 = np.zeros((P, P))
    for m in range(P):
        r = m % HD
        if r < hr:
            rot2[m + hr, m] = -1.0
        elif r < ROT:
            rot2[m - hr, m] = 1.0
    inv2 = (np.float32(500000.0) ** (-np.arange(0, ROT, 2, dtype=np.float32) / np.float32(ROT))).astype(np.float32)
    add("invf", np.where(p % HD < ROT, inv2[(p % HD) % hr], 0.0)[:, None])
    add("rotrow", (p % HD < ROT).astype(np.float32)[:, None])
    add("restrow", (p % HD >= ROT).astype(np.float32)[:, None])
    q = p[:, None]
    d = q + P - np.arange(T)[None, :]
    k_, q_ = p[:, None], p[None, :]
    masks = [(k_ // (2 * b) == q_ // (2 * b)) & (k_ % (2 * b) < b) & (q_ % (2 * b) >= b) for b in GLA_LEVELS]
    masks.append(k_ == q_)
    causal = np.where(np.arange(P)[None, :] <= q, 0.0, -1e30)
    band = np.where((d >= 0) & (d < P), 0.0, -1e30)
    pm = []
    for w in WINDOWS:
        avg = np.where((lag >= 0) & (lag < w), 1.0 / np.minimum(i + 1, w)[None, :], 0.0) - (lag == 0)
        pm.append(avg)
    return (np.concatenate(parts, 1).astype(np.float32), np.concatenate(masks, 1).astype(np.int32),
            np.concatenate(pm + [rot2, causal, band], 1).astype(np.float32))


def column_parameters(v):
    parts, at = [], 0

    def add(name, l, table):
        nonlocal at
        if table.shape[0] < P:
            table = np.concatenate([table, np.zeros((P - table.shape[0], table.shape[1]), table.dtype)], 0)
        COLUMN[(name, l)] = at
        at += table.shape[1]
        parts.append(table)

    chunks = lambda r: r.reshape(-1, P).T
    for l in range(DEPTH):
        add("mix_g", l, chunks(v["mix_norm_g"][l]))
        add("ffn_g", l, chunks(v["ffn_norm_g"][l]))
        add("ssd_conv_w", l, chunks(v["ssd_conv_w"][l].reshape(-1)))
        add("ssd_conv_b", l, chunks(v["ssd_conv_b"][l]))
        add("ml_conv_w", l, chunks(v["ml_conv_w"][l].reshape(-1)))
        add("ml_conv_b", l, chunks(v["ml_conv_b"][l]))
        add("b_alpha", l, chunks(v["gla_b_alpha"][l]))
        add("w_alpha", l, v["gla_w_alpha"][l])
        for name, key in (("dt_bias", "ssd_dt_bias"), ("a_log", "ssd_a_log"), ("b_i", "ml_b_i"), ("b_f", "ml_b_f")):
            add(name, l, v[key][l].reshape(NH, 1))
        add("b_q", l, chunks(v["b_in_2"][l, 0:512]))
        k = chunks(v["b_in_2"][l, 512:640])
        add("b_k", l, k)
        add("pool_scale", l, chunks(v["pool_scale_2"][l]))
    add("router", 0, v["router_w"][0].reshape(KD, P, NE).transpose(1, 0, 2).reshape(P, KD * NE))
    add("c", 0, chunks(v["c_2"][0]))
    return np.concatenate(parts, 1)


def arrange(v):
    const, lmask, poolm = constant_tables()
    rows1 = np.concatenate([v["ret_norm_g"], v["ssd_norm_g"], v["gla_norm_g"], v["ml_norm_g"], v["ssd_d"]], 1)
    same = np.ones((DEPTH, D), np.float32)
    mod_gain = np.concatenate([same, v["g_pre_mix_2"], v["g_post_mix_2"], same, v["g_pre_ffn_2"], v["g_post_ffn_2"]], 1)
    arrays = {
        "const": const, "lmask": lmask, "poolm": poolm, "cols": column_parameters(v), "rows1": rows1,
        "mod_gain": mod_gain, "final_g": v["final_norm_g"][None, :], "x": v["x"], "positions": v["positions_2"], "ada_w": v["ada_w_2"],
        "ada_b": v["ada_b_2"], "w_in2": v["w_in_2"], "b_in2": v["b_in_2"], "sinks": v["sinks_2"],
        "pool_w": v["pool_w_2"], "w_out2": v["w_out_2"], "w_gate": v["w_gate_2"], "w_up": v["w_up_2"],
        "w_down": v["w_down_2"],
    }
    for n in ("w_in", "w_branch", "w_out", "ffn_w1", "ffn_w3", "ffn_w2", "moe_w1", "moe_w3", "moe_w2"):
        arrays[n] = v[n]
    return {n: np.ascontiguousarray(z) for n, z in arrays.items()}


def kernel(**inputs):
    import concourse.bacc as bacc
    from concourse.bass_utils import run_bass_kernel_spmd

    arrays = arrange({n: np.asarray(z) for n, z in inputs.items()})
    nc = bacc.Bacc("TRN2", target_bir_lowering=False, num_devices=1,
                    dynamic_dma_scratch_size=1024)
    aps = {n: nc.dram_tensor("in_" + n, z.shape, mybir.dt.from_np(z.dtype), kind="ExternalInput").ap()
           for n, z in arrays.items()}
    out = nc.dram_tensor("out_y", (1, T, D), F32, kind="ExternalOutput").ap()
    program(nc, aps, out)
    r = run_bass_kernel_spmd(nc, [{"in_" + n: z for n, z in arrays.items()}], core_ids=[0])
    return r.results[0]["out_y"]
```
